# Optimizing a Trainium2 kernel written in Bass

```python
import math
import jax
import jax.numpy as jnp
from jax import lax
import numpy as np
import jax, jax.numpy as jnp

D_MODEL = 1024
BATCH = 1
SEQ = 256
DEPTH = 2

CHUNK = 64
GDN_HEADS = 8
GDN_DK = 128
GDN_DV = 128
GDN_CONV = 4
GDN_QK = GDN_HEADS * GDN_DK
GDN_V = GDN_HEADS * GDN_DV
GDN_IN = 2 * GDN_QK + 2 * GDN_V + 2 * GDN_HEADS
GDN_DT_MIN = 1e-3
GDN_DT_MAX = 1e-1
S5_GROUP = 16
S5_GROUPS = D_MODEL // S5_GROUP
S5_STATE = 64
S5_DT_MIN = 1e-3
S5_DT_MAX = 1e-1
D_FF = 11 * D_MODEL // 4
N_EXPERTS = 8
TOP_K = 2
D_FF_EXPERT = D_FF // 2
N_EVEN = (DEPTH + 1) // 2
N_ODD = DEPTH // 2
ALPHA = (2 * DEPTH) ** 0.25
BETA_INIT = (8 * DEPTH) ** -0.25
LN_EPS = 1e-5
NORM_EPS = 1e-6


def layer_norm(x, g, b):
    xf = x.astype(jnp.float32)
    mu = jnp.mean(xf, -1, keepdims=True)
    var = jnp.mean(jnp.square(xf - mu), -1, keepdims=True)
    y = (xf - mu) * lax.rsqrt(var + LN_EPS) * g.astype(jnp.float32) + b.astype(jnp.float32)
    return y.astype(x.dtype)

def l2norm(t):
    return t * lax.rsqrt(jnp.sum(t * t, -1, keepdims=True) + NORM_EPS)

def causal_dwconv(x, w):
    k = w.shape[0]
    return lax.conv_general_dilated(x, w[:, None, :].astype(x.dtype), window_strides=(1,),
                                    padding=[(k - 1, 0)], dimension_numbers=('NWC', 'WIO', 'NWC'),
                                    feature_group_count=x.shape[-1])

def gated_delta_rule_chunked(q, k, v, g, beta):
    bsz, seq, nh, dk = q.shape
    dv = v.shape[-1]
    n = seq // CHUNK

    def to_chunks(t):
        t = t.reshape((bsz, n, CHUNK) + t.shape[2:])
        return jnp.moveaxis(t, 3, 1)

    q, k, v, g, beta = (to_chunks(t) for t in (q, k, v, g, beta))
    g = jnp.cumsum(g, axis=-1)
    idx = jnp.arange(CHUNK)
    causal = idx[:, None] >= idx[None, :]
    strict = idx[:, None] > idx[None, :]
    decay = jnp.exp(jnp.where(causal, g[..., :, None] - g[..., None, :], -jnp.inf))
    k_beta = k * beta[..., None]
    v_beta = v * beta[..., None]
    lmat = jnp.where(strict, jnp.einsum('bhncd,bhnsd->bhncs', k_beta, k) * decay, 0.0)
    eye = jnp.eye(CHUNK, dtype=jnp.float32)
    t_inv = lax.linalg.triangular_solve(eye + lmat, jnp.broadcast_to(eye, lmat.shape),
                                        left_side=True, lower=True, unit_diagonal=True)
    u = jnp.einsum('bhncs,bhnsd->bhncd', t_inv, v_beta)
    w = jnp.einsum('bhncs,bhnsd->bhncd', t_inv, k_beta * jnp.exp(g)[..., None])
    a_intra = jnp.einsum('bhncd,bhnsd->bhncs', q, k) * decay

    def step(state, inp):
        q_c, k_c, u_c, w_c, g_c, a_c = inp
        v_new = u_c - jnp.einsum('bhcd,bhde->bhce', w_c, state)
        o = (jnp.einsum('bhcd,bhde->bhce', q_c * jnp.exp(g_c)[..., None], state)
             + jnp.einsum('bhcs,bhse->bhce', a_c, v_new))
        g_last = g_c[..., -1]
        state = (state * jnp.exp(g_last)[..., None, None]
                 + jnp.einsum('bhcd,bhce->bhde', k_c * jnp.exp(g_last[..., None] - g_c)[..., None], v_new))
        return state, o

    xs = tuple(jnp.moveaxis(t, 2, 0) for t in (q, k, u, w, g, a_intra))
    s0 = jnp.zeros((bsz, nh, dk, dv), jnp.float32)
    _, o = lax.scan(step, s0, xs)
    o = jnp.moveaxis(jnp.moveaxis(o, 0, 2), 1, 3)
    return o.reshape(bsz, seq, nh, dv)

def gdn_mixer(x, w_in, conv_w, a_log, dt_bias, norm_g, w_out):
    bsz, seq, _ = x.shape
    f32 = jnp.float32
    proj = x @ w_in
    qkv, z, b, a = jnp.split(proj, [2 * GDN_QK + GDN_V, 2 * GDN_QK + 2 * GDN_V,
                                    2 * GDN_QK + 2 * GDN_V + GDN_HEADS], axis=-1)
    qkv = jax.nn.silu(causal_dwconv(qkv, conv_w)).astype(f32)
    q, k, v = jnp.split(qkv, [GDN_QK, 2 * GDN_QK], axis=-1)
    q = l2norm(q.reshape(bsz, seq, GDN_HEADS, GDN_DK)) * (GDN_DK ** -0.5)
    k = l2norm(k.reshape(bsz, seq, GDN_HEADS, GDN_DK))
    v = v.reshape(bsz, seq, GDN_HEADS, GDN_DV)
    beta = jax.nn.sigmoid(b.astype(f32))
    g = -jnp.exp(a_log.astype(f32)) * jax.nn.softplus(a.astype(f32) + dt_bias.astype(f32))
    o = gated_delta_rule_chunked(q, k, v, g, beta)
    o = o * lax.rsqrt(jnp.mean(o * o, -1, keepdims=True) + NORM_EPS) * norm_g.astype(f32)
    o = o * jax.nn.silu(z.reshape(bsz, seq, GDN_HEADS, GDN_DV).astype(f32))
    return o.reshape(bsz, seq, GDN_V).astype(x.dtype) @ w_out

def s5_mixer(x, w_in, lam_re, lam_im, log_dt, b_re, b_im, c_re, c_im, d_skip, w_glu):
    bsz, seq, _ = x.shape
    f32 = jnp.float32
    n = seq // CHUNK
    u = (x @ w_in).astype(f32)
    lam = lax.complex(lam_re.astype(f32), lam_im.astype(f32))
    dt = jnp.exp(log_dt.astype(f32))[:, None]
    a_bar = jnp.exp(lam * dt)
    b_bar = ((a_bar - 1.0) / lam)[..., None] * lax.complex(b_re.astype(f32), b_im.astype(f32))
    c = lax.complex(c_re.astype(f32), c_im.astype(f32))
    steps = jnp.arange(1, CHUNK + 1, dtype=f32)[:, None, None]
    a_pow = jnp.exp((lam * dt)[None] * steps)

    def binop(e1, e2):
        a1, b1 = e1
        a2, b2 = e2
        return a2 * a1, a2 * b1 + b2

    def step(h, u_c):
        bu = jnp.einsum('gpc,btgc->btgp', b_bar, u_c.astype(jnp.complex64))
        _, hs = lax.associative_scan(binop, (jnp.broadcast_to(a_bar, bu.shape), bu), axis=1)
        hs = hs + a_pow[None] * h[:, None]
        y = jnp.einsum('gcp,btgp->btgc', c, hs).real
        return hs[:, -1], y

    uc = jnp.moveaxis(u.reshape(bsz, n, CHUNK, S5_GROUPS, S5_GROUP), 1, 0)
    h0 = jnp.zeros((bsz, S5_GROUPS, S5_STATE), jnp.complex64)
    _, ys = lax.scan(step, h0, uc)
    y = jnp.moveaxis(ys, 0, 1).reshape(bsz, seq, D_MODEL) + d_skip.astype(f32) * u
    hid = jax.nn.gelu(y.astype(x.dtype), approximate=False)
    val, gate = jnp.split(hid @ w_glu, 2, axis=-1)
    return val * jax.nn.sigmoid(gate)

def swiglu(x, w1, w3, w2):
    return (jax.nn.silu(x @ w1) * (x @ w3)) @ w2

def moe_swiglu(x, w_router, b_router, w1, w3, w2):
    bsz, seq, d = x.shape
    xt = x.reshape(-1, d)
    logits = (xt @ w_router).astype(jnp.float32) + b_router.astype(jnp.float32)
    top_v, top_i = lax.top_k(logits, TOP_K)
    gates = jax.nn.softmax(top_v, axis=-1)
    dense_gate = jnp.sum(jax.nn.one_hot(top_i, N_EXPERTS, dtype=jnp.float32) * gates[..., None], axis=1)
    y = jnp.zeros_like(xt)
    for e in range(N_EXPERTS):
        y = y + dense_gate[:, e:e + 1].astype(x.dtype) * swiglu(xt, w1[e], w3[e], w2[e])
    return y.reshape(bsz, seq, d)

def first_inputs(seed: int = 0) -> dict:
    key = jax.random.key(seed)
    ks = jax.random.split(key, 27)
    f32 = jnp.float32

    def nrm(i, shape, scale):
        return jax.random.normal(ks[i], shape, f32) * scale

    x = nrm(0, (BATCH, SEQ, D_MODEL), 1.0)
    gdn_w_in = nrm(1, (N_EVEN, D_MODEL, GDN_IN), D_MODEL ** -0.5)
    gdn_conv_w = nrm(2, (N_EVEN, GDN_CONV, 2 * GDN_QK + GDN_V), GDN_CONV ** -0.5)
    gdn_a_log = jnp.log(jax.random.uniform(ks[3], (N_EVEN, GDN_HEADS), f32, 1.0, 16.0))
    dt = jnp.exp(jax.random.uniform(ks[4], (N_EVEN, GDN_HEADS), f32, math.log(GDN_DT_MIN), math.log(GDN_DT_MAX)))
    gdn_dt_bias = dt + jnp.log(-jnp.expm1(-dt))
    gdn_norm_g = 1.0 + nrm(5, (N_EVEN, GDN_DV), 0.02)
    gdn_w_out = nrm(6, (N_EVEN, GDN_V, D_MODEL), GDN_V ** -0.5 * BETA_INIT)
    ffn_w1 = nrm(7, (N_EVEN, D_MODEL, D_FF), D_MODEL ** -0.5)
    ffn_w3 = nrm(8, (N_EVEN, D_MODEL, D_FF), D_MODEL ** -0.5)
    ffn_w2 = nrm(9, (N_EVEN, D_FF, D_MODEL), D_FF ** -0.5 * BETA_INIT)
    s5_w_in = nrm(10, (N_ODD, D_MODEL, D_MODEL), D_MODEL ** -0.5)
    s5_lam_re = -0.5 + nrm(11, (N_ODD, S5_GROUPS, S5_STATE), 0.01)
    s5_lam_im = math.pi * jnp.arange(S5_STATE, dtype=f32) + nrm(12, (N_ODD, S5_GROUPS, S5_STATE), 0.01)
    s5_log_dt = jax.random.uniform(ks[13], (N_ODD, S5_GROUPS), f32, math.log(S5_DT_MIN), math.log(S5_DT_MAX))
    s5_b_re = nrm(14, (N_ODD, S5_GROUPS, S5_STATE, S5_GROUP), (2 * S5_GROUP) ** -0.5)
    s5_b_im = nrm(15, (N_ODD, S5_GROUPS, S5_STATE, S5_GROUP), (2 * S5_GROUP) ** -0.5)
    s5_c_re = nrm(16, (N_ODD, S5_GROUPS, S5_GROUP, S5_STATE), S5_STATE ** -0.5)
    s5_c_im = nrm(17, (N_ODD, S5_GROUPS, S5_GROUP, S5_STATE), S5_STATE ** -0.5)
    s5_d = nrm(18, (N_ODD, D_MODEL), 1.0)
    s5_w_glu = nrm(19, (N_ODD, D_MODEL, 2 * D_MODEL), D_MODEL ** -0.5 * BETA_INIT)
    moe_w_router = nrm(20, (N_ODD, D_MODEL, N_EXPERTS), D_MODEL ** -0.5)
    moe_b_router = nrm(21, (N_ODD, N_EXPERTS), 0.01)
    moe_w1 = nrm(22, (N_ODD, N_EXPERTS, D_MODEL, D_FF_EXPERT), D_MODEL ** -0.5)
    moe_w3 = nrm(23, (N_ODD, N_EXPERTS, D_MODEL, D_FF_EXPERT), D_MODEL ** -0.5)
    moe_w2 = nrm(24, (N_ODD, N_EXPERTS, D_FF_EXPERT, D_MODEL), D_FF_EXPERT ** -0.5 * BETA_INIT)
    ln_g = 1.0 + nrm(25, (DEPTH, 2, D_MODEL), 0.02)
    ln_b = nrm(26, (DEPTH, 2, D_MODEL), 0.02)
    return {'x': x, 'gdn_w_in': gdn_w_in, 'gdn_conv_w': gdn_conv_w, 'gdn_a_log': gdn_a_log,
            'gdn_dt_bias': gdn_dt_bias, 'gdn_norm_g': gdn_norm_g, 'gdn_w_out': gdn_w_out,
            'ffn_w1': ffn_w1, 'ffn_w3': ffn_w3, 'ffn_w2': ffn_w2,
            's5_w_in': s5_w_in, 's5_lam_re': s5_lam_re, 's5_lam_im': s5_lam_im, 's5_log_dt': s5_log_dt,
            's5_b_re': s5_b_re, 's5_b_im': s5_b_im, 's5_c_re': s5_c_re, 's5_c_im': s5_c_im,
            's5_d': s5_d, 's5_w_glu': s5_w_glu,
            'moe_w_router': moe_w_router, 'moe_b_router': moe_b_router,
            'moe_w1': moe_w1, 'moe_w3': moe_w3, 'moe_w2': moe_w2,
            'ln_g': ln_g, 'ln_b': ln_b}

def first_block(x, gdn_w_in, gdn_conv_w, gdn_a_log, gdn_dt_bias, gdn_norm_g, gdn_w_out,
              ffn_w1, ffn_w3, ffn_w2,
              s5_w_in, s5_lam_re, s5_lam_im, s5_log_dt, s5_b_re, s5_b_im, s5_c_re, s5_c_im,
              s5_d, s5_w_glu,
              moe_w_router, moe_b_router, moe_w1, moe_w3, moe_w2,
              ln_g, ln_b):
    for i in range(DEPTH):
        j = i // 2
        if i % 2 == 0:
            h = gdn_mixer(x, gdn_w_in[j], gdn_conv_w[j], gdn_a_log[j], gdn_dt_bias[j],
                          gdn_norm_g[j], gdn_w_out[j])
        else:
            h = s5_mixer(x, s5_w_in[j], s5_lam_re[j], s5_lam_im[j], s5_log_dt[j], s5_b_re[j],
                         s5_b_im[j], s5_c_re[j], s5_c_im[j], s5_d[j], s5_w_glu[j])
        x = layer_norm(ALPHA * x + h, ln_g[i, 0], ln_b[i, 0])
        if i % 2 == 0:
            f = swiglu(x, ffn_w1[j], ffn_w3[j], ffn_w2[j])
        else:
            f = moe_swiglu(x, moe_w_router[j], moe_b_router[j], moe_w1[j], moe_w3[j], moe_w2[j])
        x = layer_norm(ALPHA * x + f, ln_g[i, 1], ln_b[i, 1])
    return x


DEPTH_2 = 1

MIX_WIDTH = D_MODEL
POOL_WIDTH = MIX_WIDTH // 2
POOL_WINDOWS = (2, 4, 8, 16)
N_POOL_GROUPS = len(POOL_WINDOWS)
POOL_GROUP = POOL_WIDTH // N_POOL_GROUPS
NA_WIDTH = MIX_WIDTH - POOL_WIDTH
NA_HEAD_DIM = 64
NA_HEADS = NA_WIDTH // NA_HEAD_DIM
GRID_W = 64
WIN_ROWS = 8
WIN_COLS = 16
COL_BLOCK = 16
COL_BAND = 2 * WIN_COLS
N_COL_BLOCKS = GRID_W // COL_BLOCK
D_FF_2 = 4 * D_MODEL
IN_WIDTH = POOL_WIDTH + 3 * NA_WIDTH
EPS = 1e-6


def rmsnorm(x, g):
    x32 = x.astype(jnp.float32)
    y = x32 * lax.rsqrt(jnp.mean(jnp.square(x32), axis=-1, keepdims=True) + EPS)
    return y.astype(x.dtype) * g

def pool_mixer(u, w_pool, pool_scale):
    B, T, _ = u.shape
    u32 = u.astype(jnp.float32)
    cs = jnp.concatenate([jnp.zeros((B, 1, POOL_WIDTH), jnp.float32),
                          jnp.cumsum(u32, axis=1)], axis=1)
    t = jnp.arange(T)
    outs = []
    for gi, w in enumerate(POOL_WINDOWS):
        sl = slice(gi * POOL_GROUP, (gi + 1) * POOL_GROUP)
        lo = jnp.clip(t - w // 2, 0, T)
        hi = jnp.clip(t - w // 2 + w, 0, T)
        cs_g = cs[:, :, sl]
        win_sum = jnp.take(cs_g, hi, axis=1) - jnp.take(cs_g, lo, axis=1)
        mean = win_sum / (hi - lo).astype(jnp.float32)[None, :, None]
        outs.append(mean - u32[:, :, sl])
    pooled = jnp.stack(outs, axis=2).astype(u.dtype)
    mixed = jnp.einsum('btgc,gcd->btgd', pooled, w_pool)
    return mixed.reshape(B, T, POOL_WIDTH) * pool_scale

def neighbourhood_attention(q, k, v, rpb):
    B, T, H, dh = q.shape
    rows = T // GRID_W
    kr = min(WIN_ROWS, rows)
    scale = dh ** -0.5

    def to_grid(a):
        return a.reshape(B, rows, GRID_W, H, dh).transpose(0, 3, 1, 2, 4)

    q_g, k_g, v_g = to_grid(q), to_grid(k), to_grid(v)

    cols = np.arange(GRID_W)
    c0 = np.clip(cols - WIN_COLS // 2, 0, GRID_W - WIN_COLS)
    band_start = np.clip(np.arange(N_COL_BLOCKS) * COL_BLOCK - WIN_COLS // 2, 0, GRID_W - COL_BAND)
    key_cols = band_start[:, None] + np.arange(COL_BAND)
    q_cols = (np.arange(N_COL_BLOCKS) * COL_BLOCK)[:, None] + np.arange(COL_BLOCK)
    qc0 = c0[q_cols][:, :, None]
    kc = key_cols[:, None, :]
    col_ok = (kc >= qc0) & (kc < qc0 + WIN_COLS)
    dc_idx = np.clip(kc - q_cols[:, :, None] + WIN_COLS - 1, 0, 2 * WIN_COLS - 2)
    bias_c = rpb[:, :, dc_idx]
    col_ok_b = jnp.asarray(col_ok)[:, :, None, :]

    def row_block(r):
        r0 = jnp.clip(r - kr // 2, 0, rows - kr)
        k_rows = lax.dynamic_slice_in_dim(k_g, r0, kr, axis=2)
        v_rows = lax.dynamic_slice_in_dim(v_g, r0, kr, axis=2)
        k_band = jnp.take(k_rows, key_cols, axis=3)
        v_band = jnp.take(v_rows, key_cols, axis=3)
        q_row = lax.dynamic_index_in_dim(q_g, r, axis=2, keepdims=False)
        q_row = q_row.reshape(B, H, N_COL_BLOCKS, COL_BLOCK, dh)
        s = jnp.einsum('bhjqd,bhijkd->bhjqik', q_row, k_band).astype(jnp.float32) * scale
        dr_idx = r0 + jnp.arange(kr) - r + (WIN_ROWS - 1)
        bias = jnp.take(bias_c, dr_idx, axis=1).transpose(0, 2, 3, 1, 4)
        s = s + bias[None].astype(jnp.float32)
        s = jnp.where(col_ok_b, s, -jnp.inf)
        p = jax.nn.softmax(s.reshape(B, H, N_COL_BLOCKS, COL_BLOCK, kr * COL_BAND), axis=-1)
        p = p.reshape(B, H, N_COL_BLOCKS, COL_BLOCK, kr, COL_BAND).astype(v.dtype)
        o = jnp.einsum('bhjqik,bhijkd->bhjqd', p, v_band)
        return o.reshape(B, H, GRID_W, dh)

    out = lax.map(row_block, jnp.arange(rows))
    return out.transpose(1, 0, 3, 2, 4).reshape(B, T, H * dh)

def second_inputs(seed: int = 0) -> dict:
    key = jax.random.key(seed)
    ks = jax.random.split(key, 12)
    f32 = jnp.float32
    x = jax.random.normal(ks[0], (BATCH, SEQ, D_MODEL), f32)
    norm_mix_g = 1.0 + 0.02 * jax.random.normal(ks[1], (DEPTH_2, D_MODEL), f32)
    w_in = jax.random.normal(ks[2], (DEPTH_2, D_MODEL, IN_WIDTH), f32) * D_MODEL ** -0.5
    w_pool = jax.random.normal(ks[3], (DEPTH_2, N_POOL_GROUPS, POOL_GROUP, POOL_GROUP), f32) * POOL_GROUP ** -0.5
    pool_scale = 1.0 + 0.1 * jax.random.normal(ks[4], (DEPTH_2, POOL_WIDTH), f32)
    rpb = 0.5 * jax.random.normal(ks[5], (DEPTH_2, NA_HEADS, 2 * WIN_ROWS - 1, 2 * WIN_COLS - 1), f32)
    w_out = jax.random.normal(ks[6], (DEPTH_2, MIX_WIDTH, D_MODEL), f32) * MIX_WIDTH ** -0.5
    norm_mlp_g = 1.0 + 0.02 * jax.random.normal(ks[7], (DEPTH_2, D_MODEL), f32)
    w_up = jax.random.normal(ks[8], (DEPTH_2, D_MODEL, D_FF_2), f32) * D_MODEL ** -0.5
    w_down = jax.random.normal(ks[9], (DEPTH_2, D_FF_2, D_MODEL), f32) * D_FF_2 ** -0.5
    final_g = 1.0 + 0.02 * jax.random.normal(ks[10], (D_MODEL,), f32)
    return {"x": x, "norm_mix_g": norm_mix_g, "w_in": w_in, "w_pool": w_pool,
            "pool_scale": pool_scale, "rpb": rpb, "w_out": w_out,
            "norm_mlp_g": norm_mlp_g, "w_up": w_up, "w_down": w_down,
            "final_g": final_g}

def second_block(x, norm_mix_g, w_in, w_pool, pool_scale, rpb, w_out,
              norm_mlp_g, w_up, w_down, final_g):
    B, T, _ = x.shape
    for l in range(DEPTH_2):
        h = rmsnorm(x, norm_mix_g[l])
        proj = h @ w_in[l]
        u = proj[..., :POOL_WIDTH]
        q, k, v = jnp.split(proj[..., POOL_WIDTH:], 3, axis=-1)
        q = q.reshape(B, T, NA_HEADS, NA_HEAD_DIM)
        k = k.reshape(B, T, NA_HEADS, NA_HEAD_DIM)
        v = v.reshape(B, T, NA_HEADS, NA_HEAD_DIM)
        a = pool_mixer(u, w_pool[l], pool_scale[l])
        b = neighbourhood_attention(q, k, v, rpb[l])
        x = x + jnp.concatenate([a, b], axis=-1) @ w_out[l]
        h = rmsnorm(x, norm_mlp_g[l])
        x = x + jnp.square(jax.nn.relu(h @ w_up[l])) @ w_down[l]
    return rmsnorm(x, final_g)


def setup_inputs(seed=0):
    out = dict(first_inputs(seed))
    for name, value in second_inputs(seed + 1).items():
        if name != "x":
            out[name + "_2"] = value
    return out


def reference(
    x, gdn_w_in, gdn_conv_w, gdn_a_log, gdn_dt_bias, gdn_norm_g, gdn_w_out, ffn_w1, ffn_w3,
    ffn_w2, s5_w_in, s5_lam_re, s5_lam_im, s5_log_dt, s5_b_re, s5_b_im, s5_c_re, s5_c_im, s5_d,
    s5_w_glu, moe_w_router, moe_b_router, moe_w1, moe_w3, moe_w2, ln_g, ln_b, norm_mix_g_2,
    w_in_2, w_pool_2, pool_scale_2, rpb_2, w_out_2, norm_mlp_g_2, w_up_2, w_down_2, final_g_2,
):
    x = first_block(
        x, gdn_w_in, gdn_conv_w, gdn_a_log, gdn_dt_bias, gdn_norm_g, gdn_w_out, ffn_w1, ffn_w3,
        ffn_w2, s5_w_in, s5_lam_re, s5_lam_im, s5_log_dt, s5_b_re, s5_b_im, s5_c_re, s5_c_im,
        s5_d, s5_w_glu, moe_w_router, moe_b_router, moe_w1, moe_w3, moe_w2, ln_g, ln_b,
    )
    return second_block(
        x, norm_mix_g_2, w_in_2, w_pool_2, pool_scale_2, rpb_2, w_out_2, norm_mlp_g_2, w_up_2,
        w_down_2, final_g_2,
    )


_drawn_inputs = setup_inputs


def setup_inputs(seed=0):
    import zlib

    import numpy as np

    out = dict(_drawn_inputs(seed))
    spreads = {}
    factors = {'gdn_norm_g': 8.0,
     's5_lam_re': 64.0,
     's5_lam_im': 21.404,
     's5_log_dt': 23.218,
     's5_b_re': 34.46,
     's5_b_im': 4.076,
     's5_c_re': 46.272,
     's5_c_im': 38.592,
     'moe_b_router': 8.0,
     'norm_mix_g_2': 4.599,
     'norm_mlp_g_2': 3.384,
     'final_g_2': 8.265}
    for name, (base, spread) in spreads.items():
        noise = np.random.default_rng([zlib.crc32(name.encode()), seed]).standard_normal(out[name].shape)
        drawn = base * np.exp(spread * noise) if base else spread * noise
        out[name] = jnp.asarray(drawn.astype(out[name].dtype))
    for name, factor in factors.items():
        out[name] = (out[name] * factor).astype(out[name].dtype)
    return out
```

```python
from contextlib import ExitStack

import numpy as np

import concourse.bass as bass
from concourse import mybir

P = 128
F32 = mybir.dt.float32
ALU = mybir.AluOpType
ACT = mybir.ActivationFunctionType
AX = mybir.AxisListType.X

SEQ, DM = 256, 1024
NT = SEQ // P
KT = DM // P
HEADS, DK = 8, 128
CONV = 4
QKV_T = 3 * HEADS
FE = 1408
FE_T = FE // P
EC = 4
EW1, EW2 = FE // EC, DM // EC
ESLAB = KT * EW1
EXPERTS = 8
GROUPS, STATE, GC = 64, 64, 16
PAIRS = GROUPS // 2
SUB = 8
NSUB = SEQ // SUB
PIECE = 8
NPIECE = PAIRS // PIECE
POOLS = (2, 4, 8, 16)
AH, AD = 8, 64
GRID, WCOL = 64, 16
FF2 = 4096
ALPHA = 4.0 ** 0.25
LN_EPS, EPS = 1e-5, 1e-6
MASKED = -1e30

C_ID, C_TRI, C_LOW, C_ONE, C_REV, C_LV = 0, 1, 2, 3, 4, 5
LEVELS = 7
C_M0 = C_LV
C_EYE = C_LV + LEVELS
C_IOTA = C_EYE + 1
N_CONST = C_IOTA + 1


def shape_constants():
    i = np.arange(P)
    row, col = i[:, None], i[None, :]
    mats = [row == col, row <= col, row > col, np.ones((P, P)),
            (row // GRID == col // GRID) & (row % GRID == GRID - 1 - col % GRID)]
    for lv in range(LEVELS):
        low = (row >> (lv + 1) == col >> (lv + 1)) & (row >> lv & 1 == 1) & (col >> lv & 1 == 0)
        mats.append(low.T if lv else low)
    eye = np.zeros((P, P))
    eye[:2 * GC, :GC] = row[:2 * GC] % GC == col[:, :GC]
    eye[:, 16] = row[:, 0] % 8
    eye[:, 32:96] = (np.arange(8)[None, :] < np.arange(8)[:, None]).reshape(1, 64)
    mats.append(eye)
    mats.append(np.broadcast_to(col, (P, P)))
    const = np.concatenate([np.asarray(m, np.float32) for m in mats], axis=1)
    t = np.arange(SEQ)
    pool = np.zeros((SEQ, len(POOLS), SEQ), np.float32)
    for g, w in enumerate(POOLS):
        lo, hi = np.clip(t - w // 2, 0, SEQ), np.clip(t - w // 2 + w, 0, SEQ)
        inside = (t[:, None] >= lo[None]) & (t[:, None] < hi[None])
        pool[:, g] = inside / (hi - lo).astype(np.float32)[None] - (t[:, None] == t[None])
    c = GRID - 1 - np.arange(P) % GRID
    c0 = np.clip(c - WCOL // 2, 0, GRID - WCOL)[:, None]
    kc = np.arange(GRID)[None]
    mask = np.where((kc >= c0) & (kc < c0 + WCOL), 0.0, MASKED).astype(np.float32)
    return const, pool, mask


def build(nc, A, out):
    with ExitStack() as ctx:
        def sb(name, shape):
            return ctx.enter_context(nc.sbuf_tensor(name, shape, F32))

        def sem(name):
            return ctx.enter_context(nc.semaphore(name))

        xres = sb("xres", [P, NT, DM])
        xT = sb("xT", [P, KT, SEQ])
        const = sb("const", [P, N_CONST, P])
        norm_w = sb("norm_w", [P, 2, DM])
        small = sb("small", [P, 900])
        arena = sb("arena", [P, 44288])
        banks = [ctx.enter_context(nc.psum_tensor(f"bank{i}", [P, 512], F32)) for i in range(8)]

        def region(off, *dims, parts=P):
            n = int(np.prod(dims))
            ap = arena[0:parts, off:off + n]
            if len(dims) == 1:
                return ap
            names = "abcde"[:len(dims)]
            return ap.rearrange(f"p ({' '.join(names)}) -> p {' '.join(names)}",
                                **{n: d for n, d in zip(names[1:], dims[1:])})

        used = [0]

        def vec(*dims):
            n = int(np.prod(dims))
            ap = small[:, used[0]:used[0] + n]
            used[0] += n
            assert used[0] <= 900
            if len(dims) == 1:
                return ap
            names = "abcd"[:len(dims)]
            return ap.rearrange(f"p ({' '.join(names)}) -> p {' '.join(names)}",
                                **{n: d for n, d in zip(names[1:], dims[1:])})

        def mat(i):
            return const[:, i, :]

        def over(ap, n):
            return ap[:, None, :].broadcast_to((ap.shape[0], n, ap.shape[1]))

        def four(bank):
            return bank[:, :].rearrange("p (a b) -> p a b", a=4)

        ident = mat(C_ID)
        stats, mv, rstd = vec(NT, 2, 6), vec(NT, 2), vec(NT)
        eps_ln, eps_rms, one_c, zero_c = vec(1), vec(1), vec(1), vec(1)
        vecT = vec(101)
        ba, a_log, dt_b = vec(NT, 16), vec(8), vec(8)
        beta, g, gc, tmp_a, tmp_b = vec(NT, 8), vec(NT, 8), vec(NT, 8), vec(NT, 8), vec(NT, 8)
        glast, kdf, neg_eg = vec(8), vec(8), vec(8)
        o_ss = vec(NT * HEADS)
        router_b, logits, top, gate = vec(8), vec(NT, 8), vec(NT, 8), vec(NT, 8)
        cmp_a, cmp_b, rank, etop = vec(64), vec(64), vec(8), vec(NT, 2)
        a8 = vec(2, PAIRS)
        w_router = vec(KT, 8)
        chosen = vec(NT, 8)
        place = vec(NT, 2 * EXPERTS + 1)
        gates = vec(NT, 2 * EXPERTS + 1)
        passes_f, scratch1 = vec(1), vec(1)
        passes = ctx.enter_context(nc.sbuf_tensor("passes", [P, 1], mybir.dt.int32))
        nmax, psum_p = vec(2), vec(2)
        vrows = xT[0:101, 0, 0:128]

        pre = region(16384, QKV_T, SEQ + CONV - 1)
        qkvT = region(22600, QKV_T, SEQ)
        zT = region(28744, HEADS, SEQ)
        decT = region(30792, 16, P)
        decL = region(32840, 16, P)
        e_row = region(34888, HEADS, P)
        vn = region(35912, NT, HEADS, P)
        s1 = region(37960, HEADS, P)
        o = region(38984, NT * HEADS, P)
        sq = region(38984, 2, 512)
        rs = region(40008, 2, 512)
        r1 = region(41032, HEADS, P)
        kd = region(42056, HEADS, P)
        D, DT, QT = region(16384, 16, P), region(18432, 16, P), region(20480, 16, P)
        vtok = region(22600 + 16 * SEQ, 16, P)
        oT = region(32840, HEADS, SEQ)
        GR = [(0, 4), (4, 4), (8, 3)]
        w1s = [region(4096 * i, KT, P * n) for i, (_, n) in enumerate(GR)]
        w3s = [region(11264 + 4096 * i, KT, P * n) for i, (_, n) in enumerate(GR)]
        w2s = [region(22528 + 4096 * i, n, DM) for i, (_, n) in enumerate(GR)]
        hT = region(33792, FE_T, SEQ)
        acc = region(36608, NT, DM)
        hsil = region(38656, 2, SEQ)
        m1 = [region(ESLAB * c, KT, EW1) for c in range(EC)]
        m3 = [region(ESLAB * (EC + c), KT, EW1) for c in range(EC)]
        m2 = [region(ESLAB * (2 * EC + c), FE_T, EW2) for c in range(EC)]
        xg = region(33792, KT, P)
        msil = region(34816, 2, EW1)
        mh = region(35520, FE)
        macc = region(36928, NT, DM)
        mhT = region(38976, FE_T, P)
        ysb = region(40384, DM)
        pick = region(41408, NT, P)
        pick_g = region(41664, NT, P)
        spread = region(41920, NT, P)
        u_n = region(0, SUB, PAIRS * GC, parts=64)
        u_r = region(4096, PAIRS, P, parts=64)
        y_sb = region(0, 2, SUB, P, parts=64)
        hidT = region(2048, KT, SEQ)
        V = region(8192, 2, PAIRS, 9, GC)
        T = region(17408, 2, PAIRS, P)
        W1T = region(25600, 2, PAIRS, P)
        Bb = region(33792, 2, PAIRS, GC)
        Ct = region(34816, 2, PAIRS, GC)
        U = region(35840, PAIRS, 2, NSUB)
        Bbd = region(35840, 2, PAIRS, 2 * GC)
        E = region(37888, 2, PAIRS, NSUB)
        KD = region(37888, PIECE, P, parts=2 * GC)
        kzero = region(38912, 1024, parts=2 * GC)
        Wp = region(39936, 2, PIECE, SUB, GC)
        t_v = region(41984, PIECE * 9 * GC)
        t_p = region(43136, PIECE * 9 * GC)
        B_raw = region(17408, 2, PAIRS, GC)
        C_raw = region(18432, 2, 8, STATE)
        lam_raw = region(19456, 2, STATE, parts=32)
        lam_raw2 = region(19584, 2, STATE, parts=32)
        lam = region(19712, 2, PAIRS)
        dts = region(19776, PAIRS)
        z = region(19808, 2, PAIRS)
        pw_mag = region(19872, 9, PAIRS)
        pw_ang = region(20160, 2, 9, PAIRS)
        pw_n = region(20736, 2, 9, PAIRS)
        pw = region(21312, 2, 9, PAIRS)
        sc = [region(21888 + 32 * i, PAIRS) for i in range(12)]
        d_col = region(22272, PAIRS, parts=32)
        sin_b = region(22304, PAIRS)
        pw_back = region(22400, 2, SUB, PAIRS)
        H = region(25600, NSUB, 2, PAIRS)
        Hbd = region(27648, 2, PAIRS, 2, NSUB)
        ht = [region(31744 + 64 * i, 2, PAIRS) for i in range(2)]
        glu = [region(8192 + 4096 * i, KT, 512) for i in range(4)]
        gsig = region(35840, NT, DM)
        slot8 = [4096 * i for i in range(8)]
        q2 = region(32768 + 0, 4, SEQ)
        k2 = region(33792, 4, SEQ)
        v2 = region(34816, NT, 512)
        u2 = region(35840, NT, 512)
        poolT = region(36864, 4, SEQ)
        catT = region(37888, 8, SEQ)
        prob = region(39936, 2, 2, SEQ)
        probT = region(40960, 2, 2, SEQ)
        bias = region(16384, NT, AH, SEQ)
        poolw = region(20480, NT, 4, SEQ)
        wpool = region(22528, 4, P)
        amask = region(23040, GRID)
        h2n = region(41984, NT, DM)
        mT = region(32768, 2, 4, SEQ)
        u_dram = nc.dram_tensor("u_scratch", (SEQ, DM), F32, kind="Internal").ap()
        k_dram = nc.dram_tensor("k_scratch", (2 * GC, PAIRS, 2 * P), F32, kind="Internal").ap()

        x_loaded, const_loaded, vecs_loaded = sem("x_loaded"), sem("const_loaded"), sem("vecs_loaded")
        normw_loaded, small_loaded = sem("normw_loaded"), sem("small_loaded")
        ba_w_loaded = sem("ba_w_loaded")
        ready = sem("consts_ready")
        vec_tr, vec_ok = sem("vec_transposed"), sem("vec_ok")
        slab = [sem(f"slab{i}_loaded") for i in range(9)]
        xt_tr, xt_v, xt_a = sem("x_transposed"), sem("xT_by_vector"), sem("xT_by_scalar")
        norm_done = sem("norm_done")
        var_ready, std_ready = sem("var_ready"), sem("std_ready")
        ba_done = sem("ba_done")
        ba_v, ba_a, g_ready = sem("ba_by_vector"), sem("ba_by_scalar"), sem("g_ready")
        in_tile, pre_ready, conv_done, silu_done = sem("in_tile"), sem("pre_ready"), sem("conv_done"), sem("silu_done")
        pad_ready = sem("pad_ready")
        sq_ready, ss_ready, nrm_ready, unit_ready = sem("sq_ready"), sem("ss_ready"), sem("nrm_ready"), sem("unit_ready")
        grow_done, gc_ready, dec_v, dec_a, dec_ready = sem("grow_done"), sem("gc_ready"), sem("dec_v"), sem("dec_a"), sem("dec_ready")
        kq_done, kq_read = sem("kq_done"), sem("kq_read")
        d_tr, d_evac = sem("d_transposed"), sem("dT_ready")
        lv_q, lv_qe, lv_p, lv_pe = sem("level_q"), sem("level_q_read"), sem("level_p"), sem("level_p_read")
        vk_tr, vk_ready = sem("vk_transposed"), sem("vk_ready")
        rec, rec_ev = sem("recurrence_step"), sem("recurrence_read")
        o_std, o_norm, o_tr, o_ready = sem("o_std"), sem("o_norm"), sem("o_tr"), sem("o_ready")
        y_done = sem("y_done")
        up_done, sil_done, h_done = sem("up_done"), sem("sil_done"), sem("h_done")
        down_done, acc_done = sem("down_done"), sem("acc_done")
        s5_loaded, s5_tr, s5_in = sem("s5_loaded"), sem("s5_param_tr"), sem("s5_param_in")
        s5_v, s5_a = sem("s5_by_vector"), sem("s5_by_scalar")
        bb_ready, w_ready, w_tr, w_in, v_ready = sem("bb_ready"), sem("w_ready"), sem("w_tr"), sem("w1t_ready"), sem("v_ready")
        im_ready = sem("im_ready")
        kd_done, kd_ready, kd_stored, t_loaded = sem("kd_done"), sem("kd_ready"), sem("kd_stored"), sem("t_loaded")
        kz_stored = sem("kz_stored")
        u_sb, u_stored, un_loaded, ur_ready, u_tr, u_ready = sem("u_sb"), sem("u_stored"), sem("un_loaded"), sem("ur_ready"), sem("u_tr"), sem("u_ready")
        e_done, e_read, h_bd, hbd_zero = sem("e_done"), sem("e_read"), sem("h_bd"), sem("hbd_zero")
        ys_done, ys_read, yt_done, hid_ready = sem("ys_done"), sem("ys_read"), sem("yt_done"), sem("hid_ready")
        glu_done, sig_done, glu_read = sem("glu_done"), sem("sig_done"), sem("glu_read")
        route_done, route_read, route_a = sem("route_done"), sem("route_read"), sem("route_a")
        chosen_ready, place_done, passes_ready = sem("chosen_ready"), sem("place_done"), sem("passes_ready")
        m_loaded = [sem(f"expert_slabs{i}_loaded") for i in range(2 * EC)]
        pick_ready, pickg_ready, gath_done, xg_ready = sem("pick_ready"), sem("pick_gate_ready"), sem("gather_done"), sem("xg_ready")
        m_up, m_sil, m_h, m_tr, m_hT = sem("expert_up"), sem("expert_silu"), sem("expert_h"), sem("expert_hT_transposed"), sem("expert_hT_ready")
        m_y, m_yread, m_sc, m_acc = sem("expert_y"), sem("expert_y_read"), sem("expert_scattered"), sem("expert_added")
        b2_loaded, bias_ready = sem("b2_loaded"), sem("bias_ready")
        p_done, p_read_a, p_read_v = sem("proj2_done"), sem("proj2_by_scalar"), sem("proj2_by_vector")
        pool_done, pool_read, mix_done, mix_read = sem("pool_done"), sem("pool_read"), sem("mix_done"), sem("mix_read")
        sc_done, max_ready, exp_done, pn_ready = sem("score_done"), sem("max_ready"), sem("exp_done"), sem("prob_ready")
        pt_done, pt_read, pv_done, pv_read = sem("pt_done"), sem("pt_read"), sem("pv_done"), sem("pv_read")
        y2_done, up2_done, relu_done, sqr_done = sem("y2_done"), sem("up2_done"), sem("relu_done"), sem("sqr_done")
        down2_done, out_stored = sem("down2_done"), sem("out_stored")
        chain_v, chain_a, chain_p = sem("vector_chain"), sem("scalar_chain"), sem("pool_chain")

        block = ctx.enter_context(nc.Block())

        def rows(w, k0, n):
            return w[k0 * P:(k0 + n) * P, :].rearrange("(k p) f -> p k f", p=P)

        def after(eng, sem_, value):
            if not isinstance(value, int) or value > 0:
                eng.wait_ge(sem_, value)

        def every(ap, n, off=0):
            return bass.AP(ap.tensor, ap.offset + off, [[0, P], [1, n]])

        def table_product(eng_ns, link, dst, pa, pb, qa, qb, t, sub):
            link(eng_ns.tensor_tensor(dst, pa, qa, ALU.mult))
            link(eng_ns.tensor_tensor(t, pb, qb, ALU.mult))
            return eng_ns.tensor_tensor(dst, dst, t, ALU.subtract if sub else ALU.add)

        def s5_factors(j, powers, n, tab):
            pr = slice(PIECE * j, PIECE * (j + 1))
            shape = (P, PIECE, n, GC)

            def power(c):
                v = powers[:, c, :, pr]
                return v.rearrange("p k a -> p a k")[:, :, :, None].broadcast_to(shape)

            def table(c):
                return tab[:, c, pr, None, :].broadcast_to(shape)
            return power, table

        def s5_v_table(eng_ns, link, j, part, t):
            power, table = s5_factors(j, pw, 9, Ct)
            dst = V[:, part, PIECE * j:PIECE * (j + 1)]
            tt = t.rearrange("p (a b c) -> p a b c", a=PIECE, b=9)
            if part == 0:
                return table_product(eng_ns, link, dst, power(0), power(1), table(0), table(1), tt, True)
            link(table_product(eng_ns, link, dst, power(0), power(1), table(1), table(0), tt, False))
            return eng_ns.tensor_scalar(dst, dst, -1.0, None, ALU.mult)

        def s5_w_table(eng_ns, link, j, part, t):
            power, table = s5_factors(j, pw_back, SUB, Bb)
            tt = t[:, 0:PIECE * SUB * GC].rearrange("p (a b c) -> p a b c", a=PIECE, b=SUB)
            if part == 0:
                return table_product(eng_ns, link, Wp[:, 0], power(0), power(1), table(0), table(1), tt, True)
            return table_product(eng_ns, link, Wp[:, 1], power(0), power(1), table(1), table(0), tt, False)

        def s5_pool(pool, link):
            pool.wait_ge(acc_done, 8)
            for i, name in enumerate(("s5_lam_re", "s5_lam_im")):
                pool.dma_start(lam_raw[:, i], A[name][0, 0:32]).then_inc(s5_loaded, 16)
                pool.dma_start(lam_raw2[:, i], A[name][0, 32:64]).then_inc(s5_loaded, 16)
            for gh in range(2):
                half = slice(64 * gh, 64 * gh + 64)
                pool.dma_start(dts[half], bass.AP(A["s5_log_dt"].tensor, 32 * gh, [[0, 64], [1, 32]])).then_inc(s5_loaded, 16)
                for i, name in enumerate(("s5_b_re", "s5_b_im")):
                    pool.dma_start(B_raw[half, i], A[name][0, 32 * gh:32 * gh + 32].rearrange("g p c -> p g c")).then_inc(s5_loaded, 16)
            for i, name in enumerate(("s5_c_re", "s5_c_im")):
                pool.dma_start(C_raw[:, i], A[name][0].rearrange("(j g) c p -> (g c) j p", j=8)).then_inc(s5_loaded, 16)
            with nc.allow_non_contiguous_dma("1024 values"):
                for gh in range(2):
                    pool.dma_start(d_col[GC * gh:GC * gh + GC], A["s5_d"][0, 512 * gh:512 * gh + 512].rearrange("(a c) -> c a", c=GC)).then_inc(s5_loaded, 16)
            link(nc.gpsimd.memset(kzero, 0.0))
            for q in range(4):
                pool.dma_start(k_dram[:, 8 * q:8 * q + 8, 0:P], kzero.rearrange("p (a b) -> p a b", a=8)).then_inc(kz_stored, 16)
            link(nc.gpsimd.memset(Bbd, 0.0))
            pool.wait_ge(bb_ready, 1)
            for gh in range(2):
                half = slice(64 * gh, 64 * gh + 64)
                link(nc.gpsimd.tensor_copy(Bbd[half, :, :, GC * gh:GC * gh + GC], Bb[half]))
            for j in range(NPIECE):
                if j:
                    pool.wait_ge(w_tr, 4 * j)
                s5_w_table(nc.gpsimd, link, j, 1, t_p).then_inc(im_ready, 1)
                s5_v_table(nc.gpsimd, link, j, 1, t_p).then_inc(im_ready, 1)
                pool.wait_ge(im_ready, 2 * j + 2)
            pool.wait_ge(e_read, 8)
            nc.gpsimd.memset(Hbd, 0.0).then_inc(hbd_zero, 1)

        def inverse_update(dve, V_, lv, j):
            s = slice(4 * j, 4 * j + 4)
            i = 4 * (lv - 1) + j
            dve.wait_ge(lv_p, i + 1)
            V_.tensor_tensor(DT[:, s], DT[:, s], four(banks[2 + j % 2]), ALU.subtract).then_inc(lv_pe, 1)
            if lv < LEVELS - 1:
                V_.tensor_tensor(D[:, s], D[:, s], four(banks[4 + j % 2]), ALU.subtract).then_inc(lv_pe, 1)

        @block.sync
        def _(sp):
            sp.dma_start(xres[:], A["x"][0].rearrange("(n p) d -> p n d", p=P)).then_inc(x_loaded, 16)
            w_in = A["gdn_w_in"][0].rearrange("(k p) f -> p k f", p=P)
            for b in range(8):
                if b >= 4:
                    sp.wait_ge(in_tile, 4 * (b - 3))
                sp.dma_start(region(4096 * (b % 4), KT, 512), w_in[:, :, 512 * b:512 * b + 512]).then_inc(slab[b % 4], 16)
            for c in range(2):
                sp.wait_ge(in_tile, 4 * (c + 5))
                sp.dma_start(region(4096 * c, 4, DM), rows(A["gdn_w_out"][0], 4 * c, 4)).then_inc(slab[c], 16)
            w1, w3, w2 = (A[f"ffn_w{i}"][0] for i in (1, 3, 2))
            sp.wait_ge(y_done, 4)
            for i in range(2):
                for gr, (t0, n) in enumerate(GR):
                    if i:
                        sp.wait_ge(up_done, 2 * (t0 + n))
                    c0 = i * FE + t0 * P
                    sp.dma_start(w1s[gr], w1[:, c0:c0 + n * P].rearrange("(k p) f -> p k f", p=P)).then_inc(slab[gr], 16)
                    sp.dma_start(w3s[gr], w3[:, c0:c0 + n * P].rearrange("(k p) f -> p k f", p=P)).then_inc(slab[3 + gr], 16)
                for gr, (t0, n) in enumerate(GR):
                    if i:
                        sp.wait_ge(down_done, gr + 1)
                    sp.dma_start(w2s[gr], rows(w2, i * FE_T + t0, n)).then_inc(slab[6 + gr], 16)
            sp.wait_ge(up_done, 2 * 2 * FE_T)
            for c in range(2):
                sp.dma_start(region(4096 * c, 4, DM), rows(A["s5_w_in"][0], 4 * c, 4)).then_inc(slab[c], 16)
            for j in range(NPIECE):
                sp.wait_ge(kd_ready, 2 * (j + 1))
                sp.dma_start(k_dram[:, PIECE * j:PIECE * (j + 1), P:2 * P], KD).then_inc(kd_stored, 16)
            sp.wait_ge(kd_stored, 16 * NPIECE)
            sp.wait_ge(kz_stored, 64)
            sp.wait_ge(im_ready, 2 * NPIECE)
            for gh in range(2):
                for s in range(SUB):
                    sp.dma_start(T[GC * s:GC * (s + 1), gh],
                                 k_dram[GC * gh:GC * (gh + 1), :, (SUB - s) * GC:(SUB - s) * GC + P]).then_inc(t_loaded, 16)
            sp.wait_ge(u_sb, 4)
            sp.dma_start(u_dram.rearrange("(n p) d -> p n d", p=P), region(35840, NT, DM)).then_inc(u_stored, 16)
            sp.wait_ge(u_stored, 16)
            for gh in range(2):
                sp.dma_start(u_n[32 * gh:32 * gh + 32],
                             u_dram[:, 512 * gh:512 * gh + 512].rearrange("(n s) d -> n s d", s=SUB)).then_inc(un_loaded, 16)
            sp.wait_ge(ys_done, NPIECE * 2)
            w_glu = A["s5_w_glu"][0].rearrange("(k p) f -> p k f", p=P)
            for i, c in enumerate((0, 2, 1, 3)):
                sp.dma_start(glu[i], w_glu[:, :, 512 * c:512 * c + 512]).then_inc(slab[i], 16)
            sp.wait_ge(glu_done, 8)

            def expert_loads(e, k):
                w1e, w3e, w2e = (A[f"moe_w{i}"][0][bass.ds(e, 1)].rearrange("e (k p) f -> p (e k) f", p=P) for i in (1, 3, 2))
                for c in range(EC):
                    cols = slice(EW1 * c, EW1 * c + EW1)
                    sp.wait_ge(m_up, k * 2 * EC + 2 * c + 1)
                    sp.dma_start(m1[c], w1e[:, :, cols]).then_inc(m_loaded[c], 16)
                    sp.wait_ge(m_up, k * 2 * EC + 2 * c + 2)
                    sp.dma_start(m3[c], w3e[:, :, cols]).then_inc(m_loaded[c], 16)
                for c in range(EC):
                    sp.wait_ge(m_y, k * EC + c + 1)
                    sp.dma_start(m2[c], w2e[:, :, EW2 * c:EW2 * c + EW2]).then_inc(m_loaded[EC + c], 16)

            expert_loads(0, 0)
            sp.wait_ge(passes_ready, 1)
            n_pass = sp.value_load(passes[0:1, 0:1], min_val=1, max_val=2)
            with sp.Fori(1, n_pass * EXPERTS) as k:
                expert_loads(k % EXPERTS, k)
            sp.wait_ge(m_y, n_pass * (EXPERTS * EC) + EC)
            w_in2 = A["w_in_2"][0].rearrange("(k p) f -> p k f", p=P)
            for i in range(4):
                sp.dma_start(region(4096 * i, KT, 512), w_in2[:, :, 512 * i:512 * i + 512]).then_inc(slab[i], 16)
            for c in range(2):
                sp.dma_start(region(4096 * (6 + c), 4, DM), rows(A["w_out_2"][0], 4 * c, 4)).then_inc(slab[4 + c], 16)
            sp.wait_ge(p_done, 12)
            w_up = A["w_up_2"][0].rearrange("(k p) f -> p k f", p=P)
            for i in range(4):
                for c in range(2):
                    if i:
                        sp.wait_ge(up2_done, 8 * (i - 1) + 4 * (c + 1))
                    f0 = 512 * (2 * i + c)
                    sp.dma_start(region(4096 * c, KT, 512), w_up[:, :, f0:f0 + 512]).then_inc(slab[6 + c], 16)
                for c in range(2):
                    if i:
                        sp.wait_ge(down2_done, 2 * (i - 1) + c + 1)
                    sp.dma_start(region(4096 * (2 + c), 4, DM), rows(A["w_down_2"][0], 4 * (2 * i + c), 4)).then_inc(slab[2 + c], 16)
            sp.wait_ge(norm_done, 7)
            sp.dma_start(out[0].rearrange("(n p) d -> p n d", p=P), xres[:]).then_inc(out_stored, 16)
            sp.wait_ge(out_stored, 16)

        @block.gpsimd
        def _(pool):
            count = [0]

            def link(ins):
                count[0] += 1
                ins.then_inc(chain_p, 1)
                pool.wait_ge(chain_p, count[0])

            pool.dma_start(const[:], A["shape_const"].rearrange("p (a b) -> p a b", b=P)).then_inc(const_loaded, 16)
            pool.dma_start(vrows[0:96], A["gdn_conv_w"][0].rearrange("j (t p) -> (j t) p", p=P)).then_inc(vecs_loaded, 16)
            pool.dma_start(vrows[96:97], A["gdn_norm_g"]).then_inc(vecs_loaded, 16)
            pool.dma_start(vrows[97:101], A["pool_scale_2"][0].rearrange("(t p) -> t p", p=P)).then_inc(vecs_loaded, 16)
            pool.dma_start(region(38984, KT, 16), A["gdn_w_in"][0].rearrange("(k p) f -> p k f", p=P)[:, :, 4096:4112]).then_inc(ba_w_loaded, 16)
            pool.dma_start(a_log, every(A["gdn_a_log"], 8)).then_inc(small_loaded, 16)
            pool.dma_start(dt_b, every(A["gdn_dt_bias"], 8)).then_inc(small_loaded, 16)
            pool.dma_start(router_b, every(A["moe_b_router"], 8)).then_inc(small_loaded, 16)

            def norm_load(slot, name, off):
                pool.dma_start(norm_w[:, slot, :], every(A[name], DM, off)).then_inc(normw_loaded, 16)

            norm_load(0, "ln_g", 0)
            norm_load(1, "ln_b", 0)
            nc.gpsimd.memset(pre[:, :, 0:CONV - 1], 0.0).then_inc(pad_ready, 1)
            for i in range(8):
                pool.wait_ge(silu_done, i // 2 + 1)
                if i == 0:
                    pool.wait_ge(ba_done, 1)
                if i >= 2:
                    pool.wait_ge(ss_ready, i - 1)
                src = qkvT[:, 2 * i:2 * i + 2, :].rearrange("p a b -> p (a b)")
                nc.gpsimd.tensor_tensor(sq[:, i % 2, :], src, src, ALU.mult).then_inc(sq_ready, 1)
            for j in range(4):
                pool.wait_ge(dec_a, 2 * (j + 1))
                s = slice(4 * j, 4 * j + 4)
                nc.gpsimd.tensor_tensor(decL[:, s, :], decL[:, s, :], over(mat(C_LOW), 4), ALU.mult).then_inc(dec_ready, 1)
                nc.gpsimd.tensor_tensor(decT[:, s, :], decT[:, s, :], over(mat(C_TRI), 4), ALU.mult).then_inc(dec_ready, 1)
            for n in (1, 2, 3):
                pool.wait_ge(norm_done, n)
                norm_load(0, "ln_g", n * DM)
                norm_load(1, "ln_b", n * DM)
                if n == 1:
                    pool.dma_start(w_router, A["moe_w_router"][0].rearrange("(k p) f -> p k f", p=P)).then_inc(small_loaded, 16)
                if n == 2:
                    s5_pool(pool, link)
            pool.wait_ge(norm_done, 4)
            norm_load(0, "norm_mix_g_2", 0)
            norm_load(1, "norm_mlp_g_2", 0)
            for r in range(4):
                for i in range(4):
                    src = bass.AP(A["rpb_2"].tensor, (7 + i - r) * 31 - 48, [[1, GRID], [15 * 31, AH], [1, GRID]])
                    dst = bias[GRID * (r % 2):GRID * (r % 2) + GRID, r // 2, :, GRID * i:GRID * i + GRID]
                    pool.dma_start(dst, src).then_inc(b2_loaded, 16)
            pool.dma_start(amask, A["shape_mask"]).then_inc(b2_loaded, 16)
            pool.dma_start(poolw, A["shape_pool"].rearrange("(n p) a b -> p n a b", p=P)).then_inc(b2_loaded, 16)
            pool.dma_start(wpool, A["w_pool_2"][0].rearrange("a p b -> p a b")).then_inc(b2_loaded, 16)
            pool.wait_ge(b2_loaded, 16 * 19)
            for n in range(NT):
                v = bias[:, n].rearrange("p h (i k) -> p (h i) k", k=GRID)
                ins = nc.gpsimd.tensor_tensor(v, v, over(amask, AH * 4), ALU.add)
                ins.then_inc(bias_ready, 1)
            pool.wait_ge(norm_done, 5)
            norm_load(0, "final_g_2", 0)

        @block.vector
        def _(dve):
            V_ = nc.vector
            count = [0]

            def link(ins):
                count[0] += 1
                ins.then_inc(chain_v, 1)
                dve.wait_ge(chain_v, count[0])

            for c, val in ((eps_ln, LN_EPS), (eps_rms, EPS), (one_c, 1.0), (zero_c, 0.0)):
                last = V_.memset(c, val)
            last.then_inc(ready, 1)

            seen_xt = [0]

            def take_xT():
                for j in (0, 2):
                    dve.wait_ge(xt_tr, 4 * seen_xt[0] + j + 1)
                    V_.tensor_copy(xT[:, 4 * (j % 2) + 0:4 * (j % 2) + 4, P * (j // 2):P * (j // 2) + P], four(banks[4 + j])).then_inc(xt_v, 1)
                seen_xt[0] += 1

            dve.wait_ge(vec_tr, 1)
            V_.tensor_copy(vecT, banks[3][:, 0:101]).then_inc(vec_ok, 1)
            take_xT()
            dve.wait_ge(ba_done, 1)
            for n in range(NT):
                last = V_.tensor_copy(ba[:, n], banks[6 + n][:, 0:16])
            link(last)
            dve.wait_ge(small_loaded, 48)
            V_.tensor_tensor(tmp_a, ba[:, :, 8:16], over(dt_b, NT), ALU.add).then_inc(ba_v, 1)
            dve.wait_ge(ba_a, 2)
            dve.wait_ge(ba_v, 1)
            link(V_.tensor_scalar(tmp_a, tmp_a, 0.0, None, ALU.max))
            link(V_.tensor_tensor(tmp_a, tmp_a, tmp_b, ALU.add))
            link(V_.tensor_scalar(tmp_a, tmp_a, -1.0, None, ALU.mult))
            V_.tensor_tensor(g, tmp_a, over(a_log, NT), ALU.mult).then_inc(g_ready, 1)

            for b in range(6):
                dve.wait_ge(pre_ready, 4 * (b + 1))
                if b == 0:
                    dve.wait_ge(pad_ready, 1)
                    dve.wait_ge(vec_ok, 1)
                for j in range(CONV):
                    for m in range(4 * b, 4 * b + 4):
                        w = vecT[:, j * QKV_T + m:j * QKV_T + m + 1]
                        if j == 0:
                            last = V_.tensor_scalar(qkvT[:, m], pre[:, m, 0:SEQ], w, None, ALU.mult)
                        else:
                            last = V_.scalar_tensor_tensor(qkvT[:, m], pre[:, m, j:j + SEQ], w, qkvT[:, m], ALU.mult, ALU.add)
                    if j < CONV - 1:
                        link(last)
                last.then_inc(conv_done, 1)

            for i in range(8):
                dve.wait_ge(nrm_ready, i + 1)
                link(V_.reciprocal(rs[:, i % 2, :], rs[:, i % 2, :]))
                v = qkvT[:, 2 * i:2 * i + 2, :].rearrange("p a b -> p (a b)")
                V_.scalar_tensor_tensor(v, rs[:, i % 2, :], DK ** -0.5 if i < 4 else 1.0, v, ALU.mult, ALU.mult).then_inc(unit_ready, 1)
            dve.wait_ge(grow_done, 1)
            link(V_.tensor_copy(gc.rearrange("p a b -> p (a b)"), banks[3][:, 0:16]))
            for j in range(4):
                dve.wait_ge(grow_done, j + 2)
                for b in range(4 * j, 4 * j + 4):
                    src = four(banks[4 + j])[:, b % 4]
                    col = gc.rearrange("p a b -> p (a b)")[:, b:b + 1]
                    V_.tensor_scalar(decL[:, b], src, col, 0.0, ALU.subtract, ALU.max)
                    last = V_.tensor_scalar(decT[:, b], src, col, 0.0, ALU.subtract, ALU.min)
                if j < 2:
                    link(last)
                    last = V_.tensor_copy(glast[:, 4 * j:4 * j + 4], four(banks[4 + j])[:, :, P - 1])
                last.then_inc(dec_v, 1)
            dve.wait_ge(dec_v, 4)
            V_.tensor_tensor(tmp_a[:, 0], glast, gc[:, 0], ALU.subtract).then_inc(gc_ready, 1)
            dve.wait_ge(dec_a, 12)
            link(V_.tensor_scalar(neg_eg, neg_eg, -1.0, None, ALU.mult))
            dve.wait_ge(unit_ready, 4)
            link(V_.tensor_tensor(e_row, e_row, qkvT[:, 0:8, P:2 * P], ALU.mult))
            for j in range(4):
                dve.wait_ge(kq_done, j + 1)
                dve.wait_ge(dec_ready, 2 * (j + 1))
                for b in range(4 * j, 4 * j + 4):
                    bcol = beta.rearrange("p a b -> p (a b)")[:, b:b + 1]
                    V_.scalar_tensor_tensor(decL[:, b], four(banks[j % 2])[:, b % 4], bcol, decL[:, b], ALU.mult, ALU.mult)
                s = slice(4 * j, 4 * j + 4)
                last = V_.tensor_tensor(decT[:, s], four(banks[2 + j % 2]), decT[:, s], ALU.mult)
                link(last)
                link(V_.scalar_tensor_tensor(D[:, s], decL[:, s], -1.0, over(mat(C_M0), 4), ALU.mult, ALU.mult))
                V_.tensor_tensor(D[:, s], D[:, s], over(ident, 4), ALU.add).then_inc(kq_read, 1)
            for j in range(4):
                dve.wait_ge(d_tr, j + 1)
                V_.tensor_copy(DT[:, 4 * j:4 * j + 4], four(banks[4 + j])).then_inc(d_evac, 1)
            for lv in range(1, LEVELS):
                for j in range(4):
                    s = slice(4 * j, 4 * j + 4)
                    i = 4 * (lv - 1) + j
                    dve.wait_ge(lv_q, i + 1)
                    V_.tensor_tensor(QT[:, s], four(banks[j % 2]), over(mat(C_LV + lv), 4), ALU.mult).then_inc(lv_qe, 1)
                    if j:
                        inverse_update(dve, V_, lv, j - 1)
                inverse_update(dve, V_, lv, 3)
            dve.wait_ge(vk_tr, 4)
            for b in range(16):
                src = four(banks[b // 4])[:, b % 4]
                if b < 8:
                    V_.tensor_scalar(vtok[:, b], src, beta[:, 0, b:b + 1], None, ALU.mult).then_inc(vk_ready, 1)
                else:
                    V_.tensor_copy(vtok[:, b], src).then_inc(vk_ready, 1)
            for h in range(8):
                dve.wait_ge(vk_tr, 5 + h // 4)
                V_.tensor_scalar(kd[:, h], four(banks[4 + h // 4])[:, h % 4], kdf[:, h:h + 1], None, ALU.mult).then_inc(vk_ready, 1)
            for j in range(2):
                dve.wait_ge(rec, j + 1)
                V_.tensor_copy(vn[:, 0, 4 * j:4 * j + 4], four(banks[6 + j])).then_inc(rec_ev, 1)
            for j in range(2):
                dve.wait_ge(rec, 3 + 2 * j)
                V_.tensor_copy(s1[:, 4 * j:4 * j + 4], four(banks[j])).then_inc(rec_ev, 1)
                dve.wait_ge(rec, 4 + 2 * j)
                V_.tensor_copy(o[:, 4 * j:4 * j + 4], four(banks[2 + j])).then_inc(rec_ev, 1)
            for j in range(2):
                dve.wait_ge(rec, 7 + j)
                dve.wait_ge(vk_ready, 24)
                for h in range(4 * j, 4 * j + 4):
                    last = V_.scalar_tensor_tensor(r1[:, h], four(banks[4 + j])[:, h % 4], neg_eg[:, h:h + 1], vtok[:, 8 + h], ALU.mult, ALU.add)
                link(last)
                for h in range(4 * j, 4 * j + 4):
                    last = V_.tensor_scalar(r1[:, h], r1[:, h], beta[:, 1, h:h + 1], None, ALU.mult)
                last.then_inc(rec_ev, 1)
            for j in range(2):
                dve.wait_ge(rec, 9 + j)
                V_.tensor_copy(vn[:, 1, 4 * j:4 * j + 4], four(banks[6 + j])).then_inc(rec_ev, 1)
            for j in range(2):
                dve.wait_ge(rec, 11 + j)
                V_.tensor_copy(o[:, 8 + 4 * j:12 + 4 * j], four(banks[j])).then_inc(rec_ev, 1)
            dve.wait_ge(o_std, 1)
            link(V_.reciprocal(o_ss, o_ss))
            V_.tensor_tensor(o, o, o_ss[:, :, None].broadcast_to((P, 16, P)), ALU.mult).then_inc(o_norm, 1)
            for j in range(4):
                dve.wait_ge(o_tr, j + 1)
                hs, ts = slice(4 * (j % 2), 4 * (j % 2) + 4), slice(P * (j // 2), P * (j // 2) + P)
                V_.scalar_tensor_tensor(oT[:, hs, ts], four(banks[4 + j]), vecT[:, 96:97], zT[:, hs, ts], ALU.mult, ALU.mult).then_inc(o_ready, 1)

            done = [0]

            def norm_tail(rms):
                done[0] += 1
                dve.wait_ge(std_ready, done[0])
                link(V_.reciprocal(rstd, rstd))

            def layer_norm(src, scale, signal):
                for n in range(NT):
                    for hf in range(2):
                        r = xres[:, n, 512 * hf:512 * hf + 512]
                        link(V_.scalar_tensor_tensor(r, r, scale, src(n, hf), ALU.mult, ALU.add))
                        link(V_.bn_stats(stats[:, n, hf, :], r))
                    last = V_.bn_aggr(mv[:, n], stats[:, n].rearrange("p a b -> p (a b)"))
                    if n == 0:
                        link(last)
                last.then_inc(var_ready, 1)
                norm_tail(False)
                dve.wait_ge(normw_loaded, 32 * (signal + 1))
                for n in range(NT):
                    r = xres[:, n]
                    link(V_.tensor_scalar(r, r, mv[:, n, 0:1], rstd[:, n:n + 1], ALU.subtract, ALU.mult))
                    link(V_.tensor_tensor(r, r, norm_w[:, 0], ALU.mult))
                    last = V_.tensor_tensor(r, r, norm_w[:, 1], ALU.add)
                    if n == 0:
                        link(last)
                last.then_inc(norm_done, 1)
                dve.wait_ge(norm_done, signal + 1)

            def from_banks(n, hf):
                dve.wait_ge(y_done, 2 * n + hf + 1)
                return banks[2 * n + hf][:, :]

            layer_norm(from_banks, ALPHA, 0)
            take_xT()

            def swiglu_halves():
                for k in range(2):
                    for m in range(FE_T):
                        dve.wait_ge(sil_done, k * FE_T + m + 1)
                        dve.wait_ge(up_done, k * 2 * FE_T + 2 * m + 2)
                        V_.tensor_tensor(hT[:, m], hsil[:, m % 2], banks[6 + m % 2][:, 0:SEQ], ALU.mult).then_inc(h_done, 1)
                    dve.wait_ge(down_done, k * 3 + 3)
                    for n in range(NT):
                        for hf in range(2):
                            a = acc[:, n, 512 * hf:512 * hf + 512]
                            V_.tensor_tensor(a, banks[2 * n + hf][:, :], a, ALU.add).then_inc(acc_done, 1)

            link(V_.memset(acc, 0.0))
            swiglu_halves()
            dve.wait_ge(acc_done, 8)
            layer_norm(lambda n, hf: acc[:, n, 512 * hf:512 * hf + 512], ALPHA, 1)
            take_xT()

            dve.wait_ge(s5_in, 1)
            dve.wait_ge(s5_tr, 1)
            link(V_.tensor_copy(lam.rearrange("p a b -> p (a b)"), banks[0][:, 0:64]))
            for i in range(2):
                for jb in range(8):
                    half = slice(64 * (jb // 4), 64 * (jb // 4) + 64)
                    last = V_.tensor_copy(Ct[half, i, 8 * (jb % 4):8 * (jb % 4) + 8].rearrange("p a b -> p (a b)"),
                                          banks[2 + 2 * i][half, P * (jb % 4):P * (jb % 4) + P])
            link(last)
            link(V_.tensor_tensor(z, lam, dts[:, None, :].broadcast_to((P, 2, PAIRS)), ALU.mult))
            for k in range(9):
                V_.tensor_scalar(pw_mag[:, k], z[:, 0], float(k), None, ALU.mult)
                V_.tensor_scalar(pw_ang[:, 1, k], z[:, 1], float(k), None, ALU.mult)
                last = V_.tensor_scalar(pw_ang[:, 0, k], z[:, 1], float(k), float(np.pi / 2), ALU.mult, ALU.add)
            link(last)
            ROUND = 12582912.0
            C1 = 6.28125
            C2 = 0.0019353071795864769
            flat = [t.rearrange("p a b c -> p (a b c)") for t in (pw_ang, pw_n)]
            link(V_.tensor_scalar(flat[1], flat[0], float(1 / (2 * np.pi)), ROUND, ALU.mult, ALU.add))
            link(V_.tensor_scalar(flat[1], flat[1], ROUND, None, ALU.subtract))
            link(V_.scalar_tensor_tensor(flat[0], flat[1], -C1, flat[0], ALU.mult, ALU.add))
            link(V_.scalar_tensor_tensor(flat[0], flat[1], -C2, flat[0], ALU.mult, ALU.add))
            link(V_.tensor_scalar(flat[0], flat[0], 3.1415925, -3.1415925, ALU.min, ALU.max))
            V_.tensor_scalar(sin_b, pw_ang[:, 1, 1], 0.5, None, ALU.mult).then_inc(s5_v, 1)
            dve.wait_ge(s5_a, 1)
            for c in range(2):
                last = V_.tensor_tensor(pw[:, c], pw_mag, pw_ang[:, c], ALU.mult)
            link(last)
            for k in range(SUB):
                V_.tensor_copy(pw_back[:, :, SUB - 1 - k, :], pw[:, :, k, :])
            link(V_.tensor_copy(a8, pw[:, :, 8, :]))
            th, ex1, s2, re, im, den, t1, t2 = sc[:8]
            link(V_.tensor_scalar(t1, th, -1.0, 1.0, ALU.mult, ALU.add))
            link(V_.reciprocal(t1, t1))
            link(V_.scalar_tensor_tensor(ex1, th, 2.0, t1, ALU.mult, ALU.mult))
            link(V_.tensor_tensor(s2, sin_b, sin_b, ALU.mult))
            link(V_.tensor_tensor(s2, s2, pw_mag[:, 1], ALU.mult))
            link(V_.scalar_tensor_tensor(re, s2, -2.0, ex1, ALU.mult, ALU.add))
            link(V_.tensor_copy(im, pw[:, 1, 1]))
            link(V_.tensor_tensor(t1, lam[:, 0], lam[:, 0], ALU.mult))
            link(V_.tensor_tensor(t2, lam[:, 1], lam[:, 1], ALU.mult))
            link(V_.tensor_tensor(den, t1, t2, ALU.add))
            link(V_.reciprocal(den, den))
            fr, fi, t3, t4 = sc[8:12]
            link(V_.tensor_tensor(t1, re, lam[:, 0], ALU.mult))
            link(V_.tensor_tensor(t2, im, lam[:, 1], ALU.mult))
            link(V_.tensor_tensor(t1, t1, t2, ALU.add))
            link(V_.tensor_tensor(fr, t1, den, ALU.mult))
            link(V_.tensor_tensor(t3, im, lam[:, 0], ALU.mult))
            link(V_.tensor_tensor(t4, re, lam[:, 1], ALU.mult))
            link(V_.tensor_tensor(t3, t3, t4, ALU.subtract))
            link(V_.tensor_tensor(fi, t3, den, ALU.mult))

            def wide(v):
                return v[:, :, None].broadcast_to((P, PAIRS, GC))
            tb = t_v[:, 0:PAIRS * GC].rearrange("p (a b) -> p a b", a=PAIRS)
            link(table_product(V_, link, Bb[:, 0], wide(fr), wide(fi), B_raw[:, 0], B_raw[:, 1], tb, True))
            table_product(V_, link, Bb[:, 1], wide(fr), wide(fi), B_raw[:, 1], B_raw[:, 0], tb, False).then_inc(bb_ready, 1)
            dve.wait_ge(bb_ready, 1)
            for j in range(NPIECE):
                if j:
                    dve.wait_ge(w_tr, 4 * j)
                s5_w_table(V_, link, j, 0, t_v).then_inc(w_ready, 1)
                s5_v_table(V_, link, j, 0, t_v).then_inc(v_ready, 1)
                dve.wait_ge(v_ready, j + 1)
                for i in range(4):
                    dve.wait_ge(w_tr, 4 * j + i + 1)
                    ri, h4 = i // 2, i % 2
                    V_.tensor_copy(W1T[:, ri, PIECE * j + 4 * h4:PIECE * j + 4 * h4 + 4], four(banks[4 + i])).then_inc(w_in, 1)
                for i in range(2):
                    dve.wait_ge(kd_done, 2 * j + i + 1)
                    if i == 0 and j:
                        dve.wait_ge(kd_stored, 16 * j)
                    kd_piece = KD[:, 4 * i:4 * i + 4]
                    link(V_.tensor_copy(kd_piece, four(banks[2 + i])[0:2 * GC]))
                    dd = t_v[0:2 * GC, 0:64].rearrange("p (a b) -> p a b", a=4)
                    p0 = PIECE * j + 4 * i
                    link(V_.tensor_tensor(dd, mat(C_EYE)[0:2 * GC, None, 0:GC].broadcast_to((2 * GC, 4, GC)),
                                          d_col[:, p0:p0 + 4, None].broadcast_to((2 * GC, 4, GC)), ALU.mult))
                    V_.tensor_tensor(kd_piece[:, :, 0:GC], kd_piece[:, :, 0:GC], dd, ALU.add).then_inc(kd_ready, 1)
            dve.wait_ge(kd_ready, 8)
            dve.wait_ge(kd_done, 8)
            for i in range(4):
                dve.wait_ge(y_done, 4 + i + 1)
                V_.tensor_copy(region(35840, NT, DM)[:, i // 2, 512 * (i % 2):512 * (i % 2) + 512], banks[i][:, :]).then_inc(u_sb, 1)
            dve.wait_ge(un_loaded, 32)
            V_.tensor_copy(u_r.rearrange("p a (s c) -> p a s c", c=GC), u_n.rearrange("p s (a c) -> p a s c", c=GC)).then_inc(ur_ready, 1)
            for j in range(4):
                dve.wait_ge(u_tr, j + 1)
                V_.tensor_copy(U[:, 8 * j:8 * j + 8].rearrange("p a b c -> p (a b c)"), banks[4 + j][:, :]).then_inc(u_ready, 1)
            for j in range(NPIECE):
                for ri in range(2):
                    dve.wait_ge(e_done, 2 * j + ri + 1)
                    src = banks[(2 * j + ri) % 4][:, :].rearrange("p (a b c) -> p a b c", a=8, b=2)
                    for gh in range(2):
                        half = slice(64 * gh, 64 * gh + 64)
                        last = V_.tensor_copy(E[half, ri, 8 * j:8 * j + 8], src[half, :, gh])
                    last.then_inc(e_read, 1)
            dve.wait_ge(e_read, 8)
            link(V_.memset(H[:, 0], 0.0))
            wide_re = a8[:, 0:1, :].broadcast_to((P, 2, PAIRS))
            wide_im = a8[:, 1:2, :].broadcast_to((P, 2, PAIRS))
            for n in range(NSUB - 1):
                V_.tensor_tensor(ht[0], H[:, n], wide_re, ALU.mult)
                link(V_.tensor_tensor(ht[1], H[:, n], wide_im, ALU.mult))
                link(V_.tensor_tensor(ht[0], ht[0], E[:, :, :, n], ALU.add))
                V_.tensor_tensor(H[:, n + 1, 0], ht[0][:, 0], ht[1][:, 1], ALU.subtract)
                link(V_.tensor_tensor(H[:, n + 1, 1], ht[0][:, 1], ht[1][:, 0], ALU.add))
            dve.wait_ge(hbd_zero, 1)
            for ri in range(2):
                for gh in range(2):
                    half = slice(64 * gh, 64 * gh + 64)
                    V_.tensor_copy(Hbd[half, ri, :, gh], H[half, :, ri].rearrange("p n a -> p a n")).then_inc(h_bd, 1)
            for j in range(NPIECE):
                if j >= 2:
                    dve.wait_ge(yt_done, 2 * (j - 1))
                for i in range(2):
                    dve.wait_ge(ys_done, 2 * j + i + 1)
                    src = banks[i][0:64, :].rearrange("p (a s c) -> p s a c", a=4, s=SUB)
                    dst = y_sb[:, j % 2].rearrange("p s (a c) -> p s a c", c=GC)[:, :, 4 * i:4 * i + 4, :]
                    V_.tensor_copy(dst, src).then_inc(ys_read, 1)
            for hf in range(2):
                for n in range(NT):
                    i = 2 * hf + n
                    dve.wait_ge(sig_done, i + 1)
                    s = gsig[:, n, 512 * hf:512 * hf + 512]
                    V_.tensor_tensor(s, banks[i][:, :], s, ALU.mult).then_inc(glu_read, 1)
            dve.wait_ge(glu_read, 4)
            layer_norm(lambda n, hf: gsig[:, n, 512 * hf:512 * hf + 512], ALPHA, 2)
            take_xT()

            for n in range(NT):
                dve.wait_ge(route_done, n + 1)
                link(V_.tensor_tensor(logits[:, n], banks[n][:, 0:8], router_b, ALU.add))
                link(V_.max(top[:, n], logits[:, n]))
                link(V_.tensor_scalar(gate[:, n], logits[:, n], top[:, n, 0:1], None, ALU.subtract))
                V_.tensor_tensor(etop[:, n, 0:1], top[:, n, 1:2], top[:, n, 0:1], ALU.subtract).then_inc(route_read, 1)
            dve.wait_ge(route_a, 1)
            for n in range(NT):
                lg = logits[:, n]
                mine = lg[:, :, None].broadcast_to((P, 8, 8))
                other = lg[:, None, :].broadcast_to((P, 8, 8))
                ca, cb = (t.rearrange("p (a b) -> p a b", a=8) for t in (cmp_a, cmp_b))
                link(V_.tensor_tensor(ca, other, mine, ALU.is_equal))
                link(V_.tensor_tensor(ca, ca, mat(C_EYE)[:, 32:96].rearrange("p (a b) -> p a b", a=8), ALU.mult))
                link(V_.tensor_tensor(cb, other, mine, ALU.is_gt))
                link(V_.tensor_tensor(ca, ca, cb, ALU.add))
                link(V_.tensor_reduce(rank, ca, AX, ALU.add))
                link(V_.tensor_scalar(rank, rank, 2.0, None, ALU.is_lt))
                link(V_.tensor_scalar(etop[:, n, 1:2], etop[:, n, 1:2], 1.0, None, ALU.add))
                link(V_.reciprocal(etop[:, n, 1:2], etop[:, n, 1:2]))
                link(V_.tensor_copy(chosen[:, n], rank))
                link(V_.tensor_tensor(gate[:, n], gate[:, n], rank, ALU.mult))
                link(V_.tensor_scalar(gate[:, n], gate[:, n], etop[:, n, 1:2], None, ALU.mult))
            link(V_.memset(place, -1.0))
            link(V_.memset(gates, 0.0))
            for t in range(2):
                last = V_.tensor_copy(gates[:, :, EXPERTS * t:EXPERTS * t + EXPERTS], gate)
            last.then_inc(chosen_ready, 1)
            dve.wait_ge(place_done, 1)
            for n in range(NT):
                link(V_.tensor_tensor(place[:, n, 0:EXPERTS], banks[n][:, 0:EXPERTS], chosen[:, n], ALU.mult))
            link(V_.tensor_scalar(place[:, :, EXPERTS:2 * EXPERTS], place[:, :, 0:EXPERTS], -1.0 - P, None, ALU.add))
            link(V_.tensor_scalar(place[:, :, 0:EXPERTS], place[:, :, 0:EXPERTS], -1.0, None, ALU.add))
            link(V_.tensor_reduce(passes_f, banks[2][:, 0:EXPERTS], AX, ALU.max))
            link(V_.tensor_scalar(passes_f, passes_f, float(P), 1.0, ALU.is_gt, ALU.add))
            V_.tensor_copy(passes[:, :], passes_f).then_inc(passes_ready, 1)

            def picks(dst, k, scaled, signal):
                for n in range(NT):
                    at = place[:, n, bass.ds(k, 1)]
                    if scaled:
                        last = V_.tensor_scalar(dst[:, n], mat(C_IOTA), at, gates[:, n, bass.ds(k, 1)], ALU.is_equal, ALU.mult)
                    else:
                        last = V_.tensor_scalar(dst[:, n], mat(C_IOTA), at, None, ALU.is_equal)
                last.then_inc(signal, 1)

            def take_tokens(k):
                for i in range(2):
                    dve.wait_ge(gath_done, k * 2 + i + 1)
                    V_.tensor_copy(xg[:, 4 * i:4 * i + 4], four(banks[6 + i])).then_inc(xg_ready, 1)

            dve.wait_ge(passes_ready, 1)
            link(V_.memset(macc, 0.0))
            picks(pick, 0, False, pick_ready)
            picks(pick_g, 0, True, pickg_ready)
            take_tokens(0)
            n_pass = dve.value_load(passes[0:1, 0:1], min_val=1, max_val=2)
            with dve.Fori(0, n_pass * EXPERTS) as k:
                dve.wait_ge(gath_done, k * 2 + 2)
                picks(pick, k + 1, False, pick_ready)
                for c in range(EC):
                    dve.wait_ge(m_sil, k * EC + c + 1)
                    dve.wait_ge(m_up, k * 2 * EC + 2 * EC + 2 * c + 2)
                    if c == 0:
                        dve.wait_ge(m_tr, k * 4 + 4)
                    V_.tensor_tensor(mh[:, EW1 * c:EW1 * c + EW1], msil[:, c % 2], banks[2 + c % 2][:, 0:EW1], ALU.mult).then_inc(m_h, 1)
                dve.wait_ge(m_tr, k * 4 + 5)
                picks(pick_g, k + 1, True, pickg_ready)
                take_tokens(k + 1)
                for n in range(NT):
                    for hf in range(2):
                        dve.wait_ge(m_sc, k * 4 + 2 * n + hf + 1)
                        a = macc[:, n, 512 * hf:512 * hf + 512]
                        V_.tensor_tensor(a, banks[(2 if n == 0 else 6) + hf][:, :], a, ALU.add).then_inc(m_acc, 1)
            link(V_.memset(scratch1, 0.0))
            layer_norm(lambda n, hf: macc[:, n, 512 * hf:512 * hf + 512], ALPHA, 3)

            def rms_norm(dst, slot, n_loads, final=False):
                done[0] += 1
                dve.wait_ge(std_ready, done[0])
                link(V_.reciprocal(rstd, rstd))
                dve.wait_ge(normw_loaded, 16 * n_loads)
                for n in range(NT):
                    last = V_.scalar_tensor_tensor(dst[:, n], xres[:, n], rstd[:, n:n + 1], norm_w[:, slot], ALU.mult, ALU.mult)
                last.then_inc(norm_done, 1)

            rms_norm(h2n, 0, 10)
            take_xT()
            for n in range(NT):
                dve.wait_ge(p_done, n + 1)
                V_.tensor_copy(u2[:, n], banks[n][:, :]).then_inc(p_read_v, 1)
            for m in range(4):
                dve.wait_ge(p_done, 6 + m + 1)
                V_.tensor_copy(k2[:, m], banks[m][:, 0:SEQ]).then_inc(p_read_v, 1)
            for n in range(NT):
                dve.wait_ge(p_done, 10 + n + 1)
                V_.tensor_copy(v2[:, n], banks[4 + n][:, :]).then_inc(p_read_v, 1)
            for gi in range(4):
                dve.wait_ge(pool_done, gi + 1)
                V_.tensor_copy(poolT[:, gi], banks[6 + gi % 2][:, 0:SEQ]).then_inc(pool_read, 1)
            for gi in range(4):
                dve.wait_ge(mix_done, gi + 1)
                V_.tensor_scalar(catT[:, gi], banks[6 + gi % 2][:, 0:SEQ], vecT[:, 97 + gi:98 + gi], None, ALU.mult).then_inc(mix_read, 1)
            for hp in range(4):
                for n in range(NT):
                    i = 2 * hp + n
                    dve.wait_ge(sc_done, i + 1)
                    if i:
                        dve.wait_ge(exp_done, 2 * i)
                        dve.wait_ge(pn_ready, i)
                    for e in range(2):
                        last = V_.tensor_reduce(nmax[:, e:e + 1], banks[2 * n + e][:, 0:SEQ], AX, ALU.max)
                    link(last)
                    V_.tensor_scalar(nmax, nmax, -1.0, None, ALU.mult).then_inc(max_ready, 1)
                    dve.wait_ge(exp_done, 2 * i + 2)
                    link(V_.reciprocal(psum_p, psum_p))
                    V_.tensor_tensor(prob[:, n], prob[:, n], psum_p[:, :, None].broadcast_to((P, 2, SEQ)), ALU.mult).then_inc(pn_ready, 1)
                for kt in range(2):
                    dve.wait_ge(pt_done, 2 * hp + kt + 1)
                    if hp and kt == 0:
                        dve.wait_ge(pv_done, hp)
                    V_.tensor_copy(probT[:, kt].rearrange("p a b -> p (a b)"), banks[4 + kt][:, :]).then_inc(pt_read, 1)
                dve.wait_ge(pv_done, hp + 1)
                V_.tensor_copy(catT[:, 4 + hp], banks[6][:, 0:SEQ]).then_inc(pv_read, 1)
            for n in range(NT):
                for hf in range(2):
                    dve.wait_ge(y2_done, 2 * n + hf + 1)
                    r = xres[:, n, 512 * hf:512 * hf + 512]
                    last = V_.tensor_tensor(r, banks[2 * n + hf][:, :], r, ALU.add)
            last.then_inc(var_ready, 1)
            rms_norm(h2n, 1, 10)
            take_xT()
            for i in range(32):
                dve.wait_ge(relu_done, i + 1)
                if i >= 8:
                    dve.wait_ge(down2_done, i // 4 - 1)
                t = mT[:, (i // 4) % 2, i % 4]
                V_.tensor_tensor(t, t, t, ALU.mult).then_inc(sqr_done, 1)
            dve.wait_ge(down2_done, 8)
            for n in range(NT):
                for hf in range(2):
                    r = xres[:, n, 512 * hf:512 * hf + 512]
                    last = V_.tensor_tensor(r, banks[2 * n + hf][:, :], r, ALU.add)
            last.then_inc(var_ready, 1)
            rms_norm(xres, 0, 11)

        @block.scalar
        def _(act):
            A_ = nc.scalar.activation
            count = [0]

            def link(ins):
                count[0] += 1
                ins.then_inc(chain_a, 1)
                act.wait_ge(chain_a, count[0])

            seen_xt = [0]

            def take_xT():
                for j in (1, 3):
                    act.wait_ge(xt_tr, 4 * seen_xt[0] + j + 1)
                    nc.scalar.copy(xT[:, 4:8, P * (j // 2):P * (j // 2) + P], four(banks[4 + j])).then_inc(xt_a, 1)
                seen_xt[0] += 1

            act.wait_ge(ready, 1)
            take_xT()
            act.wait_ge(ba_v, 1)
            link(A_(tmp_b, tmp_a, ACT.Abs, bias=zero_c))
            link(A_(tmp_b, tmp_b, ACT.Exp, bias=zero_c, scale=-1.0))
            A_(a_log, a_log, ACT.Exp, bias=zero_c).then_inc(ba_a, 1)
            A_(tmp_b, tmp_b, ACT.Ln, bias=one_c).then_inc(ba_a, 1)
            link(A_(beta, ba[:, :, 0:8], ACT.Sigmoid, bias=zero_c))
            for b in range(8):
                for m in range(4 * b, 4 * b + 4):
                    act.wait_ge(in_tile, m + 1)
                    if b < 6:
                        nc.scalar.copy(pre[:, m, CONV - 1:], banks[m % 8][:, 0:SEQ]).then_inc(pre_ready, 1)
                    else:
                        A_(zT[:, m - QKV_T], banks[m % 8][:, 0:SEQ], ACT.Silu, bias=zero_c).then_inc(pre_ready, 1)
                if 1 <= b <= 6:
                    act.wait_ge(conv_done, b)
                    t = qkvT[:, 4 * (b - 1):4 * b].rearrange("p a b -> p (a b)")
                    A_(t, t, ACT.Silu, bias=zero_c).then_inc(silu_done, 1)
            for i in range(8):
                act.wait_ge(ss_ready, i + 1)
                if i >= 2:
                    act.wait_ge(unit_ready, i - 1)
                A_(rs[:, i % 2, :], banks[i % 3][:, :], ACT.Sqrt, bias=eps_rms).then_inc(nrm_ready, 1)
            for j in range(4):
                act.wait_ge(dec_v, j + 1)
                for t, s in ((decL, -1.0), (decT, 1.0)):
                    v = t[:, 4 * j:4 * j + 4].rearrange("p a b -> p (a b)")
                    A_(v, v, ACT.Exp, bias=zero_c, scale=s).then_inc(dec_a, 1)
            for j in range(2):
                A_(e_row[:, 4 * j:4 * j + 4].rearrange("p a b -> p (a b)"), banks[6 + j][:, :], ACT.Exp, bias=zero_c).then_inc(dec_a, 1)
            A_(neg_eg, gc[:, 1], ACT.Exp, bias=zero_c).then_inc(dec_a, 1)
            act.wait_ge(gc_ready, 1)
            A_(kdf, tmp_a[:, 0], ACT.Exp, bias=zero_c).then_inc(dec_a, 1)
            act.wait_ge(rec_ev, 12)
            for b in range(16):
                act.wait_ge(rec_ev, 12)
                last = A_(vn[:, b // 8, b % 8], o[:, b], ACT.Square, bias=zero_c, accum_out=o_ss[:, b:b + 1])
            link(last)
            A_(o_ss, o_ss, ACT.Sqrt, bias=eps_rms, scale=1.0 / DK).then_inc(o_std, 1)

            norms = [0]

            def std(eps):
                norms[0] += 1
                act.wait_ge(var_ready, norms[0])
                A_(rstd, mv[:, :, 1], ACT.Sqrt, bias=eps).then_inc(std_ready, 1)

            std(eps_ln)
            take_xT()

            def swiglu_halves():
                for k in range(2):
                    for m in range(FE_T):
                        act.wait_ge(up_done, k * 2 * FE_T + 2 * m + 1)
                        after(act, h_done, k * FE_T + max(m - 1, 0))
                        A_(hsil[:, m % 2], banks[4 + m % 2][:, 0:SEQ], ACT.Silu, bias=zero_c).then_inc(sil_done, 1)

            swiglu_halves()
            std(eps_ln)
            take_xT()
            act.wait_ge(s5_loaded, 16 * 14)
            A_(dts, dts, ACT.Exp, bias=zero_c).then_inc(s5_in, 1)
            act.wait_ge(s5_v, 1)
            A_(pw_mag, pw_mag, ACT.Exp, bias=zero_c)
            link(A_(sc[0], z[:, 0], ACT.Tanh, bias=zero_c, scale=0.5))
            A_(pw_ang, pw_ang, ACT.Sin, bias=zero_c)
            A_(sin_b, sin_b, ACT.Sin, bias=zero_c).then_inc(s5_a, 1)
            for j in range(NPIECE):
                for q in range(2):
                    act.wait_ge(yt_done, 2 * j + q + 1)
                    src = banks[4 + (2 * j + q) % 4][:, 0:256].rearrange("p (s g n) -> p g n s", s=4, g=2)
                    for gh in range(2):
                        dst = hidT[:, j + 4 * gh].rearrange("p (n s) -> p n s", s=SUB)[:, :, 4 * q:4 * q + 4]
                        A_(dst, src[:, gh], ACT.Gelu, bias=zero_c).then_inc(hid_ready, 1)
            for hf in range(2):
                for n in range(NT):
                    i = 2 * hf + n
                    act.wait_ge(glu_done, 4 * hf + 2 * n + 2)
                    A_(gsig[:, n, 512 * hf:512 * hf + 512], banks[4 + i][:, :], ACT.Sigmoid, bias=zero_c).then_inc(sig_done, 1)
            std(eps_ln)
            take_xT()
            act.wait_ge(route_read, 2)
            A_(gate, gate, ACT.Exp, bias=zero_c)
            A_(etop[:, :, 1], etop[:, :, 0], ACT.Exp, bias=zero_c).then_inc(route_a, 1)
            act.wait_ge(passes_ready, 1)
            n_pass = act.value_load(passes[0:1, 0:1], min_val=1, max_val=2)
            with act.Fori(0, n_pass * EXPERTS) as k:
                def silu_of(c):
                    act.wait_ge(m_up, k * 2 * EC + 2 * EC + 2 * c + 1)
                    if c >= 2:
                        act.wait_ge(m_h, k * EC + c - 1)
                    elif c == 0:
                        act.wait_ge(pickg_ready, k + 1)
                    A_(msil[:, c % 2], banks[c % 2][:, 0:EW1], ACT.Silu, bias=zero_c).then_inc(m_sil, 1)

                def take_hT(t):
                    act.wait_ge(m_tr, k * 4 + t + 5)
                    if t == 0:
                        nc.scalar.copy(spread.rearrange("p a b -> p (a b)"), banks[4][:, 2 * P:4 * P])
                        nc.scalar.copy(mhT[:, 0:2].rearrange("p a b -> p (a b)"), banks[4][:, 0:2 * P]).then_inc(m_hT, 1)
                    else:
                        m = 3 * t - 1
                        nc.scalar.copy(mhT[:, m:m + 3].rearrange("p a b -> p (a b)"), banks[4 + t % 2][:, 0:3 * P]).then_inc(m_hT, 1)

                silu_of(0)
                silu_of(1)
                take_hT(0)
                silu_of(2)
                take_hT(1)
                silu_of(3)
                take_hT(2)
                take_hT(3)
                for hf in range(2):
                    act.wait_ge(m_y, k * EC + EC + 2 * hf + 2)
                    nc.scalar.copy(ysb[:, 512 * hf:512 * hf + 512], banks[hf][:, :]).then_inc(m_yread, 1)
            std(eps_ln)

            def mean_square():
                for n in range(NT):
                    link(A_(region(39936, 1024), xres[:, n], ACT.Square, bias=zero_c, accum_out=mv[:, n, 1:2]))
                A_(rstd, mv[:, :, 1], ACT.Sqrt, bias=eps_rms, scale=1.0 / DM).then_inc(std_ready, 1)

            act.wait_ge(norm_done, 4)
            mean_square()
            take_xT()
            for m in range(4):
                act.wait_ge(p_done, 2 + m + 1)
                A_(q2[:, m], banks[4 + m][:, 0:SEQ], ACT.Copy, scale=AD ** -0.5).then_inc(p_read_a, 1)
            for hp in range(4):
                for n in range(NT):
                    i = 2 * hp + n
                    act.wait_ge(max_ready, i + 1)
                    if hp:
                        act.wait_ge(pt_done, 2 * hp)
                    for e in range(2):
                        A_(prob[:, n, e], banks[2 * n + e][:, 0:SEQ], ACT.Exp, bias=nmax[:, e:e + 1],
                           accum_out=psum_p[:, e:e + 1]).then_inc(exp_done, 1)
            act.wait_ge(var_ready, 5)
            mean_square()
            take_xT()
            for i in range(32):
                act.wait_ge(up2_done, i + 1)
                if i >= 8:
                    act.wait_ge(down2_done, i // 4 - 1)
                A_(mT[:, (i // 4) % 2, i % 4], banks[4 + i % 4][:, 0:SEQ], ACT.Relu, bias=zero_c).then_inc(relu_done, 1)
            act.wait_ge(var_ready, 6)
            mean_square()

        @block.tensor
        def _(pe):
            mm = nc.tensor.matmul

            def transpose(dst, src):
                k = src.shape[0]
                if dst.shape[0] < P:
                    return mm(dst, src, const[0:k, C_ID, 0:k], start=True, stop=True)
                return nc.tensor.transpose(dst, src, const[0:k, C_ID, 0:k])

            made_xt = [0]

            def make_xT(src):
                for j in range(4):
                    for i in range(4):
                        c = 4 * (j % 2) + i
                        last = transpose(four(banks[4 + j])[:, i], src[:, j // 2, P * c:P * c + P])
                    last.then_inc(xt_tr, 1)
                made_xt[0] += 1

            def need_xT():
                pe.wait_ge(xt_v, 2 * made_xt[0])
                pe.wait_ge(xt_a, 2 * made_xt[0])

            def t_form(bank, w, m, x=xT):
                for k in range(KT):
                    last = mm(bank[:, 0:SEQ], w[:, k, P * m:P * m + P], x[:, k, :], start=(k == 0), stop=(k == KT - 1))
                return last

            def token_major(bank, x, w, n, k0=0, total=KT):
                nk = w.shape[1]
                for k in range(nk):
                    last = mm(bank, x[:, k0 + k, P * n:P * n + P], w[:, k], start=(k0 + k == 0), stop=(k0 + k == total - 1))
                return last

            pe.wait_ge(const_loaded, 16)
            pe.wait_ge(vecs_loaded, 48)
            transpose(banks[3][:, 0:101], vrows).then_inc(vec_tr, 1)
            pe.wait_ge(x_loaded, 16)
            make_xT(xres)
            need_xT()
            w_ba = region(38984, KT, 16)
            pe.wait_ge(ba_w_loaded, 16)
            for n in range(NT):
                last = token_major(banks[6 + n][:, 0:16], xT, w_ba, n)
            last.then_inc(ba_done, 1)
            for m in range(32):
                b = m // 4
                if m % 4 == 0:
                    pe.wait_ge(slab[b % 4], 16 * (b // 4 + 1))
                if m in (6, 7):
                    pe.wait_ge(ba_v, 1)
                if m == 3:
                    pe.wait_ge(vec_ok, 1)
                if m >= 8:
                    pe.wait_ge(pre_ready, m - 7)
                t_form(banks[m % 8], region(4096 * (b % 4), KT, 512), m % 4).then_inc(in_tile, 1)
            pe.wait_ge(pre_ready, 32)
            for i in range(8):
                pe.wait_ge(sq_ready, i + 1)
                if i >= 3:
                    pe.wait_ge(nrm_ready, i - 2)
                mm(banks[i % 3][:, :], mat(C_ONE), sq[:, i % 2, :], start=True, stop=True).then_inc(ss_ready, 1)
            pe.wait_ge(g_ready, 1)
            mm(banks[3][:, 0:16], mat(C_TRI), g.rearrange("p a b -> p (a b)"), start=True, stop=True).then_inc(grow_done, 1)
            for j in range(4):
                for b in range(4 * j, 4 * j + 4):
                    gcol = g.rearrange("p a b -> p (a b)")[:, b:b + 1]
                    last = mm(four(banks[4 + j])[:, b % 4], gcol.broadcast_to((P, P)), mat(C_TRI), start=True, stop=True)
                last.then_inc(grow_done, 1)
            pe.wait_ge(unit_ready, 8)
            for j in range(4):
                if j == 0:
                    pe.wait_ge(nrm_ready, 8)
                    pe.wait_ge(dec_v, 1)
                if j >= 2:
                    pe.wait_ge(kq_read, j - 1)
                for b in range(4 * j, 4 * j + 4):
                    n, h = b // 8, b % 8
                    kt, qt = (qkvT[:, t + h, P * n:P * n + P] for t in (8, 0))
                    mm(four(banks[j % 2])[:, b % 4], kt, kt, start=True, stop=True)
                    last = mm(four(banks[2 + j % 2])[:, b % 4], kt, qt, start=True, stop=True)
                last.then_inc(kq_done, 1)
            pe.wait_ge(dec_a, 12)
            for j in range(4):
                pe.wait_ge(kq_read, j + 1)
                for b in range(4 * j, 4 * j + 4):
                    last = transpose(four(banks[4 + j])[:, b % 4], D[:, b])
                last.then_inc(d_tr, 1)

            def level_q(lv, j):
                i = 4 * (lv - 1) + j
                if lv == 1:
                    pe.wait_ge(d_evac, 4)
                else:
                    pe.wait_ge(lv_pe, 8 * (lv - 2) + 2 * (j + 1))
                if i >= 2:
                    pe.wait_ge(lv_qe, i - 1)
                for b in range(4 * j, 4 * j + 4):
                    last = mm(four(banks[j % 2])[:, b % 4], decL[:, b], DT[:, b], start=True, stop=True)
                last.then_inc(lv_q, 1)

            def level_p(lv, j):
                i = 4 * (lv - 1) + j
                pe.wait_ge(lv_qe, i + 1)
                if i >= 2:
                    prev = i - 2
                    pe.wait_ge(lv_pe, 2 * (prev + 1) if prev < 20 else 40 + prev - 19)
                for b in range(4 * j, 4 * j + 4):
                    last = mm(four(banks[2 + j % 2])[:, b % 4], D[:, b], QT[:, b], start=True, stop=True)
                    if lv < LEVELS - 1:
                        last = mm(four(banks[4 + j % 2])[:, b % 4], QT[:, b], D[:, b], start=True, stop=True)
                last.then_inc(lv_p, 1)

            for lv in range(1, LEVELS):
                level_q(lv, 0)
                for j in range(4):
                    if j < 3:
                        level_q(lv, j + 1)
                    level_p(lv, j)
            pe.wait_ge(lv_pe, 44)
            for j in range(4):
                for b in range(4 * j, 4 * j + 4):
                    last = transpose(four(banks[j])[:, b % 4], qkvT[:, 16 + b % 8, P * (b // 8):P * (b // 8) + P])
                last.then_inc(vk_tr, 1)
            for j in range(2):
                for h in range(4 * j, 4 * j + 4):
                    last = transpose(four(banks[4 + j])[:, h % 4], qkvT[:, 8 + h, 0:P])
                last.then_inc(vk_tr, 1)
            def each(j, bank, pairs, sem_=rec):
                for h in range(4 * j, 4 * j + 4):
                    terms = pairs(h)
                    for t, (lhsT, rhs) in enumerate(terms):
                        last = mm(four(bank)[:, h % 4], lhsT, rhs, start=(t == 0), stop=(t == len(terms) - 1))
                last.then_inc(sem_, 1)

            for j in range(2):
                pe.wait_ge(vk_ready, 4 * (j + 1))
                each(j, banks[6 + j], lambda h: [(DT[:, h], vtok[:, h])])
            pe.wait_ge(vk_ready, 24)
            for j in range(2):
                pe.wait_ge(rec_ev, j + 1)
                each(j, banks[j], lambda h: [(kd[:, h], vn[:, 0, h])])
                each(j, banks[2 + j], lambda h: [(decT[:, h], vn[:, 0, h])])
            for j in range(2):
                pe.wait_ge(rec_ev, 3 + 2 * j)
                each(j, banks[4 + j], lambda h: [(qkvT[:, 8 + h, P:2 * P], s1[:, h])])
            for j in range(2):
                pe.wait_ge(rec_ev, 7 + j)
                each(j, banks[6 + j], lambda h: [(DT[:, 8 + h], r1[:, h])])
            for j in range(2):
                pe.wait_ge(rec_ev, 9 + j)
                each(j, banks[j], lambda h: [(e_row[:, h], s1[:, h]), (decT[:, 8 + h], vn[:, 1, h])])
            pe.wait_ge(o_norm, 1)
            for j in range(4):
                for i in range(4):
                    last = transpose(four(banks[4 + j])[:, i], o[:, 4 * j + i])
                last.then_inc(o_tr, 1)
            pe.wait_ge(o_ready, 4)
            pe.wait_ge(rec_ev, 12)
            for n in range(NT):
                for hf in range(2):
                    for c in range(2):
                        pe.wait_ge(slab[c], 48)
                        last = token_major(banks[2 * n + hf][:, :], oT, region(4096 * c, 4, DM)[:, :, 512 * hf:512 * hf + 512], n, 4 * c)
                    last.then_inc(y_done, 1)
            pe.wait_ge(norm_done, 1)
            make_xT(xres)

            def swiglu_halves(slabs):
                need_xT()
                for k in range(2):
                    i = k
                    for gr, (t0, n) in enumerate(GR):
                        pe.wait_ge(slab[gr], (i + slabs[gr] + 1) * 16)
                        pe.wait_ge(slab[3 + gr], (i + slabs[3 + gr] + 1) * 16)
                        for m in range(t0, t0 + n):
                            after(pe, sil_done, k * FE_T + max(m - 1, 0))
                            t_form(banks[4 + m % 2], w1s[gr], m - t0).then_inc(up_done, 1)
                            after(pe, h_done, k * FE_T + max(m - 1, 0))
                            t_form(banks[6 + m % 2], w3s[gr], m - t0).then_inc(up_done, 1)
                    after(pe, acc_done, k * 4)
                    for gr, (t0, n) in enumerate(GR):
                        pe.wait_ge(slab[6 + gr], (i + slabs[6 + gr] + 1) * 16)
                        pe.wait_ge(h_done, k * FE_T + t0 + n)
                        for nt in range(NT):
                            for hf in range(2):
                                last = token_major(banks[2 * nt + hf][:, :], hT, w2s[gr][:, :, 512 * hf:512 * hf + 512], nt, t0, FE_T)
                        last.then_inc(down_done, 1)

            swiglu_halves([3, 3, 2, 2, 0, 0, 0, 0, 0])
            pe.wait_ge(norm_done, 2)
            make_xT(xres)
            pe.wait_ge(s5_loaded, 16 * 14)
            need_xT()
            for gh, raw in enumerate((lam_raw, lam_raw2)):
                for i in range(2):
                    transpose(banks[0][64 * gh:64 * gh + 64, PAIRS * i:PAIRS * i + PAIRS], raw[:, i])
            for i in range(2):
                for jb in range(8):
                    half = slice(64 * (jb // 4), 64 * (jb // 4) + 64)
                    last = transpose(banks[2 + 2 * i][half, P * (jb % 4):P * (jb % 4) + P], C_raw[:, i, jb])
            last.then_inc(s5_tr, 1)
            for j in range(NPIECE):
                if j == 0:
                    pe.wait_ge(bb_ready, 1)
                else:
                    pe.wait_ge(w_in, 4 * j)
                pe.wait_ge(w_ready, j + 1)
                pe.wait_ge(im_ready, 2 * j + 1)
                for i in range(4):
                    ri, h4 = i // 2, i % 2
                    for a in range(4):
                        last = transpose(four(banks[4 + i])[:, a], Wp[:, ri, 4 * h4 + a].rearrange("p s c -> p (s c)"))
                    last.then_inc(w_tr, 1)
                pe.wait_ge(v_ready, j + 1)
                pe.wait_ge(im_ready, 2 * j + 2)
                for i in range(2):
                    if j:
                        pe.wait_ge(kd_ready, 2 * (j - 1) + i + 1)
                    for a in range(4):
                        pr = PIECE * j + 4 * i + a
                        for ri in range(2):
                            last = mm(four(banks[2 + i])[0:2 * GC, a], Bbd[:, ri, pr], V[:, ri, pr, 0:SUB].rearrange("p k c -> p (k c)"),
                                      start=(ri == 0), stop=(ri == 1))
                    last.then_inc(kd_done, 1)
            pe.wait_ge(kd_ready, 8)
            for n in range(NT):
                for hf in range(2):
                    for c in range(2):
                        pe.wait_ge(slab[c], 16 * 6)
                        last = token_major(banks[2 * n + hf][:, :], xT, region(4096 * c, 4, DM)[:, :, 512 * hf:512 * hf + 512], n, 4 * c)
                    last.then_inc(y_done, 1)
            pe.wait_ge(ur_ready, 1)
            pe.wait_ge(w_in, 16)
            for j in range(4):
                for a in range(8):
                    last = transpose(banks[4 + j][:, 64 * a:64 * a + 64], u_r[:, 8 * j + a])
                last.then_inc(u_tr, 1)
            pe.wait_ge(u_sb, 4)
            for j in range(NPIECE):
                pe.wait_ge(u_ready, j + 1)
                for ri in range(2):
                    i = 2 * j + ri
                    if i >= 4:
                        pe.wait_ge(e_read, i - 3)
                    for a in range(8):
                        pr = 8 * j + a
                        last = mm(banks[i % 4][:, 64 * a:64 * a + 64], W1T[:, ri, pr], U[:, pr].rearrange("p a b -> p (a b)"), start=True, stop=True)
                    last.then_inc(e_done, 1)
            pe.wait_ge(e_read, 8)
            pe.wait_ge(h_bd, 4)
            pe.wait_ge(t_loaded, 16 * 16)
            pe.wait_ge(u_ready, 4)

            def y_transposes(j):
                for q in range(2):
                    pe.wait_ge(ys_read, 2 * j + 2)
                    if j >= 2:
                        pe.wait_ge(hid_ready, 4 * (j - 2) + 2 * q + 2)
                    for s in range(4):
                        last = transpose(banks[4 + (2 * j + q) % 4][:, 64 * s:64 * s + 64], y_sb[:, j % 2, 4 * q + s])
                    last.then_inc(yt_done, 1)

            for j in range(NPIECE):
                for i in range(2):
                    if j:
                        pe.wait_ge(ys_read, 2 * (j - 1) + i + 1)
                    for a in range(4):
                        pr = PIECE * j + 4 * i + a
                        dst = four(banks[i])
                        for ri in range(2):
                            mm(dst[0:64, a], Hbd[:, ri, pr].rearrange("p a b -> p (a b)"), V[:, ri, pr, 1:SUB + 1].rearrange("p k c -> p (k c)"),
                               start=(ri == 0), stop=False, skip_group_check=True)
                        for gh in range(2):
                            last = mm(dst[32 * gh:32 * gh + 32, a], U[:, pr, gh], T[:, gh, pr], start=False, stop=(gh == 1), skip_group_check=True)
                    last.then_inc(ys_done, 1)
                if j:
                    y_transposes(j - 1)
            y_transposes(NPIECE - 1)
            pe.wait_ge(hid_ready, 16)
            pe.wait_ge(ys_read, 8)
            for hf in range(2):
                for n in range(NT):
                    for c in range(2):
                        pe.wait_ge(slab[2 * hf + c], 16 * {0: 7, 1: 7, 2: 5, 3: 5}[2 * hf + c])
                        token_major(banks[4 * c + 2 * hf + n][:, :], hidT, glu[2 * hf + c], n).then_inc(glu_done, 1)
            for counter, n in ((m_up, 2 * EC), (m_y, EC), (m_tr, 4), (m_yread, 2), (m_acc, 4)):
                pe.sem_inc(counter, n)
            pe.wait_ge(norm_done, 3)
            make_xT(xres)
            need_xT()
            pe.wait_ge(small_loaded, 64)
            for n in range(NT):
                token_major(banks[n][:, 0:8], xT, w_router, n).then_inc(route_done, 1)
            pe.wait_ge(route_read, 2)
            pe.wait_ge(chosen_ready, 1)
            mm(banks[0][:, 0:EXPERTS], mat(C_TRI), chosen[:, 0], start=True, stop=True)
            mm(banks[1][:, 0:EXPERTS], mat(C_TRI), chosen[:, 1], start=True, stop=False)
            mm(banks[1][:, 0:EXPERTS], mat(C_ONE), chosen[:, 0], start=False, stop=True)
            mm(banks[2][:, 0:EXPERTS], mat(C_ONE), chosen[:, 0], start=True, stop=False)
            mm(banks[2][:, 0:EXPERTS], mat(C_ONE), chosen[:, 1], start=False, stop=True).then_inc(place_done, 1)
            pe.wait_ge(passes_ready, 1)

            def gather(k):
                pe.wait_ge(pick_ready, k + 1)
                for i in range(2):
                    for c in range(4):
                        for n in range(NT):
                            last = mm(four(banks[6 + i])[:, c], xres[:, n, P * (4 * i + c):P * (4 * i + c) + P], pick[:, n],
                                      start=(n == 0), stop=(n == 1))
                    last.then_inc(gath_done, 1)

            gather(0)
            n_pass = pe.value_load(passes[0:1, 0:1], min_val=1, max_val=2)
            with pe.Fori(0, n_pass * EXPERTS) as k:
                def up(c):
                    pe.wait_ge(m_loaded[c], (k + 1) * 32)
                    if c >= 2:
                        pe.wait_ge(m_sil, k * EC + c - 1)
                    for kt in range(KT):
                        last = mm(banks[c % 2][:, 0:EW1], xg[:, kt], m1[c][:, kt], start=(kt == 0), stop=(kt == KT - 1))
                    last.then_inc(m_up, 1)
                    if c >= 2:
                        pe.wait_ge(m_h, k * EC + c - 1)
                    for kt in range(KT):
                        last = mm(banks[2 + c % 2][:, 0:EW1], xg[:, kt], m3[c][:, kt], start=(kt == 0), stop=(kt == KT - 1))
                    last.then_inc(m_up, 1)

                def hidden(t):
                    pe.wait_ge(m_h, k * EC + t + 1)
                    if t >= 2:
                        pe.wait_ge(m_hT, k * 4 + t - 1)
                    bank = four(banks[4 + t % 2])
                    if t == 0:
                        pe.wait_ge(pickg_ready, k + 1)
                        for n in range(NT):
                            transpose(bank[:, 2 + n], pick_g[:, n])
                        tiles = (0, 1)
                    else:
                        tiles = range(3 * t - 1, 3 * t + 2)
                    for i, m in enumerate(tiles):
                        last = transpose(bank[:, i], mh[:, P * m:P * m + P])
                    last.then_inc(m_tr, 1)

                pe.wait_ge(xg_ready, k * 2 + 2)
                pe.wait_ge(m_yread, k * 2 + 2)
                pe.wait_ge(m_acc, k * 4 + 4)
                up(0)
                up(1)
                hidden(0)
                up(2)
                hidden(1)
                up(3)
                hidden(2)
                gather(k + 1)
                hidden(3)
                pe.wait_ge(m_hT, k * 4 + 4)
                pe.wait_ge(m_sil, k * EC + 4)
                for c in range(EC):
                    pe.wait_ge(m_loaded[EC + c], (k + 1) * 16)
                    dst = banks[c // 2][:, EW2 * (c % 2):EW2 * (c % 2) + EW2]
                    for kt in range(FE_T):
                        last = mm(dst, mhT[:, kt], m2[c][:, kt], start=(kt == 0), stop=(kt == FE_T - 1))
                    last.then_inc(m_y, 1)
                pe.wait_ge(xg_ready, k * 2 + 4)
                for n in range(NT):
                    for hf in range(2):
                        pe.wait_ge(m_yread, k * 2 + hf + 3)
                        last = mm(banks[(2 if n == 0 else 6) + hf][:, :], spread[:, n], ysb[:, 512 * hf:512 * hf + 512], start=True, stop=True)
                        last.then_inc(m_sc, 1)
            pe.wait_ge(norm_done, 5)
            make_xT(h2n)
            need_xT()
            pe.wait_ge(slab[0], 16 * 8)
            for n in range(NT):
                token_major(banks[n][:, :], xT, region(0, KT, 512), n).then_inc(p_done, 1)
            pe.wait_ge(slab[1], 16 * 8)
            for m in range(4):
                t_form(banks[4 + m], region(4096, KT, 512), m).then_inc(p_done, 1)
            pe.wait_ge(slab[2], 16 * 6)
            for m in range(4):
                if m < 2:
                    pe.wait_ge(p_read_v, m + 1)
                t_form(banks[m], region(8192, KT, 512), m).then_inc(p_done, 1)
            pe.wait_ge(slab[3], 16 * 6)
            for n in range(NT):
                pe.wait_ge(p_read_a, n + 1)
                token_major(banks[4 + n][:, :], xT, region(12288, KT, 512), n).then_inc(p_done, 1)
            pe.wait_ge(b2_loaded, 16 * 19)
            pe.wait_ge(p_read_a, 4)
            for gi in range(4):
                if gi >= 2:
                    pe.wait_ge(pool_read, gi - 1)
                for n in range(NT):
                    last = mm(banks[6 + gi % 2][:, 0:SEQ], u2[:, n, P * gi:P * gi + P], poolw[:, n, gi], start=(n == 0), stop=(n == 1))
                last.then_inc(pool_done, 1)
            for gi in range(4):
                pe.wait_ge(pool_read, 3 + gi % 2 if gi < 2 else 4)
                if gi >= 2:
                    pe.wait_ge(mix_read, gi - 1)
                mm(banks[6 + gi % 2][:, 0:SEQ], wpool[:, gi], poolT[:, gi], start=True, stop=True).then_inc(mix_done, 1)
            pe.wait_ge(bias_ready, 2)
            pe.wait_ge(p_read_v, 8)
            pe.wait_ge(mix_read, 4)

            def scores(hp):
                for n in range(NT):
                    i = 2 * hp + n
                    if i >= 2:
                        pe.wait_ge(exp_done, 2 * (i - 1))
                    for e in range(2):
                        pp = slice(64 * e, 64 * e + 64)
                        mm(banks[2 * n + e][:, 0:SEQ], q2[pp, hp, P * n:P * n + P], k2[pp, hp, :], start=True, stop=False)
                    for e in range(2):
                        last = mm(banks[2 * n + e][:, 0:SEQ], mat(C_REV), bias[:, n, 2 * hp + e], start=False, stop=True)
                    last.then_inc(sc_done, 1)

            scores(0)
            for hp in range(4):
                if hp < 3:
                    scores(hp + 1)
                pe.wait_ge(pn_ready, 2 * hp + 2)
                for kt in range(2):
                    if hp:
                        pe.wait_ge(pt_read, 2 * (hp - 1) + kt + 1)
                    for n in range(NT):
                        for e in range(2):
                            last = transpose(banks[4 + kt][:, SEQ * e + P * n:SEQ * e + P * n + P], prob[:, n, e, P * kt:P * kt + P])
                    last.then_inc(pt_done, 1)
                pe.wait_ge(pt_read, 2 * hp + 2)
                if hp:
                    pe.wait_ge(pv_read, hp)
                for e in range(2):
                    for kt in range(2):
                        h = 2 * hp + e
                        last = mm(banks[6][64 * e:64 * e + 64, 0:SEQ], v2[:, kt, AD * h:AD * h + AD], probT[:, kt, e], start=(kt == 0), stop=(kt == 1))
                last.then_inc(pv_done, 1)
            pe.wait_ge(pv_read, 4)
            pe.wait_ge(exp_done, 16)
            for n in range(NT):
                for hf in range(2):
                    for c in range(2):
                        pe.wait_ge(slab[4 + c], 16 * 3)
                        last = token_major(banks[2 * n + hf][:, :], catT, region(4096 * (6 + c), 4, DM)[:, :, 512 * hf:512 * hf + 512], n, 4 * c)
                    last.then_inc(y2_done, 1)
            pe.wait_ge(norm_done, 6)
            make_xT(h2n)
            need_xT()
            arrived = {6: 2, 7: 2, 2: 6, 3: 6}

            def mlp_up(s):
                c = s % 2
                pe.wait_ge(slab[6 + c], 16 * (arrived[6 + c] + s // 2 + 1))
                for m in range(4):
                    i = 4 * s + m
                    if i >= 4:
                        pe.wait_ge(relu_done, i - 3)
                    t_form(banks[4 + m], region(4096 * c, KT, 512), m).then_inc(up2_done, 1)

            def mlp_down(s):
                c = s % 2
                pe.wait_ge(slab[2 + c], 16 * (arrived[2 + c] + s // 2 + 1))
                pe.wait_ge(sqr_done, 4 * s + 4)
                for n in range(NT):
                    for hf in range(2):
                        for k in range(4):
                            last = mm(banks[2 * n + hf][:, :], mT[:, s % 2, k, P * n:P * n + P],
                                      region(4096 * (2 + c), 4, DM)[:, k, 512 * hf:512 * hf + 512],
                                      start=(s == 0 and k == 0), stop=(s == 7 and k == 3))
                last.then_inc(down2_done, 1)

            mlp_up(0)
            for s in range(8):
                if s < 7:
                    mlp_up(s + 1)
                mlp_down(s)


_INS = ["x", "gdn_w_in", "gdn_conv_w", "gdn_a_log", "gdn_dt_bias", "gdn_norm_g", "gdn_w_out",
        "ffn_w1", "ffn_w3", "ffn_w2", "s5_w_in", "s5_lam_re", "s5_lam_im", "s5_log_dt", "s5_b_re",
        "s5_b_im", "s5_c_re", "s5_c_im", "s5_d", "s5_w_glu", "moe_w_router", "moe_b_router",
        "moe_w1", "moe_w3", "moe_w2", "ln_g", "ln_b", "norm_mix_g_2", "w_in_2", "w_pool_2",
        "pool_scale_2", "rpb_2", "w_out_2", "norm_mlp_g_2", "w_up_2", "w_down_2", "final_g_2"]


def kernel(**inputs):
    import concourse.bacc as bacc
    from concourse.bass_utils import run_bass_kernel_spmd

    nc = bacc.Bacc("TRN2", target_bir_lowering=False, num_devices=1)
    arrays = {name: np.ascontiguousarray(inputs[name]) for name in _INS}
    arrays["shape_const"], arrays["shape_pool"], arrays["shape_mask"] = shape_constants()
    aps = {name: nc.dram_tensor(name, a.shape, F32, kind="ExternalInput").ap() for name, a in arrays.items()}
    out = nc.dram_tensor("out", (1, SEQ, DM), F32, kind="ExternalOutput").ap()
    build(nc, aps, out)
    r = run_bass_kernel_spmd(nc, [arrays], core_ids=[0])
    return r.results[0]["out"]
```

```python
from contextlib import ExitStack

import numpy as np

import concourse.bass as bass
from concourse import mybir

P = 128
F32 = mybir.dt.float32
ALU = mybir.AluOpType
ACT = mybir.ActivationFunctionType
AX = mybir.AxisListType.X

SEQ, DM = 256, 1024
NT = SEQ // P
KT = DM // P
HEADS, DK = 8, 128
CONV = 4
QKV_T = 3 * HEADS
FE = 1408
FE_T = FE // P
FF1 = 2 * FE
FC = 2
FF_CHUNKS = FF1 // P // FC
FF_SETS = 3
S5_PARAMS_AT = 3
S5_PIECE_AT = (6, 7, 8, 9)
EC = 4
EW1, EW2 = FE // EC, DM // EC
ESLAB = KT * EW1
EXPERTS = 8
GROUPS, STATE, GC = 64, 64, 16
PAIRS = GROUPS // 2
SUB = 8
NSUB = SEQ // SUB
PIECE = 8
NPIECE = PAIRS // PIECE
POOLS = (2, 4, 8, 16)
AH, AD = 8, 64
GRID, WCOL = 64, 16
FF2 = 4096
ALPHA = 4.0 ** 0.25
LN_EPS, EPS = 1e-5, 1e-6
MASKED = -1e30

C_ID, C_TRI, C_LOW, C_ONE, C_REV, C_LV = 0, 1, 2, 3, 4, 5
LEVELS = 7
C_M0 = C_LV
C_EYE = C_LV + LEVELS
C_IOTA = C_EYE + 1
N_CONST = C_IOTA + 1


def shape_constants():
    i = np.arange(P)
    row, col = i[:, None], i[None, :]
    mats = [row == col, row <= col, row > col, np.ones((P, P)),
            (row // GRID == col // GRID) & (row % GRID == GRID - 1 - col % GRID)]
    for lv in range(LEVELS):
        low = (row >> (lv + 1) == col >> (lv + 1)) & (row >> lv & 1 == 1) & (col >> lv & 1 == 0)
        mats.append(low.T if lv else low)
    eye = np.zeros((P, P))
    eye[:2 * GC, :GC] = row[:2 * GC] % GC == col[:, :GC]
    eye[:, 16] = row[:, 0] % 8
    eye[:, 32:96] = (np.arange(8)[None, :] < np.arange(8)[:, None]).reshape(1, 64)
    mats.append(eye)
    mats.append(np.broadcast_to(col, (P, P)))
    const = np.concatenate([np.asarray(m, np.float32) for m in mats], axis=1)
    t = np.arange(SEQ)
    pool = np.zeros((SEQ, len(POOLS), SEQ), np.float32)
    for g, w in enumerate(POOLS):
        lo, hi = np.clip(t - w // 2, 0, SEQ), np.clip(t - w // 2 + w, 0, SEQ)
        inside = (t[:, None] >= lo[None]) & (t[:, None] < hi[None])
        pool[:, g] = inside / (hi - lo).astype(np.float32)[None] - (t[:, None] == t[None])
    c = GRID - 1 - np.arange(P) % GRID
    c0 = np.clip(c - WCOL // 2, 0, GRID - WCOL)[:, None]
    kc = np.arange(GRID)[None]
    mask = np.where((kc >= c0) & (kc < c0 + WCOL), 0.0, MASKED).astype(np.float32)
    return const, pool, mask


def build(nc, A, out):
    with ExitStack() as ctx:
        def sb(name, shape):
            return ctx.enter_context(nc.sbuf_tensor(name, shape, F32))

        def sem(name):
            return ctx.enter_context(nc.semaphore(name))

        xres = sb("xres", [P, NT, DM])
        xT = sb("xT", [P, KT, SEQ])
        const = sb("const", [P, N_CONST, P])
        norm_w = sb("norm_w", [P, 2, DM])
        small = sb("small", [P, 900])
        arena = sb("arena", [P, 44288])
        banks = [ctx.enter_context(nc.psum_tensor(f"bank{i}", [P, 512], F32)) for i in range(8)]

        def region(off, *dims, parts=P):
            n = int(np.prod(dims))
            ap = arena[0:parts, off:off + n]
            if len(dims) == 1:
                return ap
            names = "abcde"[:len(dims)]
            return ap.rearrange(f"p ({' '.join(names)}) -> p {' '.join(names)}",
                                **{n: d for n, d in zip(names[1:], dims[1:])})

        used = [0]

        def vec(*dims):
            n = int(np.prod(dims))
            ap = small[:, used[0]:used[0] + n]
            used[0] += n
            assert used[0] <= 900
            if len(dims) == 1:
                return ap
            names = "abcd"[:len(dims)]
            return ap.rearrange(f"p ({' '.join(names)}) -> p {' '.join(names)}",
                                **{n: d for n, d in zip(names[1:], dims[1:])})

        def mat(i):
            return const[:, i, :]

        def over(ap, n):
            return ap[:, None, :].broadcast_to((ap.shape[0], n, ap.shape[1]))

        def four(bank):
            return bank[:, :].rearrange("p (a b) -> p a b", a=4)

        ident = mat(C_ID)
        stats, mv, rstd = vec(NT, 2, 6), vec(NT, 2), vec(NT)
        eps_ln, eps_rms, one_c, zero_c = vec(1), vec(1), vec(1), vec(1)
        vecT = vec(101)
        ba, a_log, dt_b = vec(NT, 16), vec(8), vec(8)
        beta, g, gc, tmp_a, tmp_b = vec(NT, 8), vec(NT, 8), vec(NT, 8), vec(NT, 8), vec(NT, 8)
        glast, kdf, neg_eg = vec(8), vec(8), vec(8)
        o_ss = vec(NT * HEADS)
        router_b, logits, top, gate = vec(8), vec(NT, 8), vec(NT, 8), vec(NT, 8)
        cmp_a, cmp_b, rank, etop = vec(64), vec(64), vec(8), vec(NT, 2)
        a8 = vec(2, PAIRS)
        w_router = vec(KT, 8)
        chosen = vec(NT, 8)
        place = vec(NT, 2 * EXPERTS + 1)
        gates = vec(NT, 2 * EXPERTS + 1)
        passes_f, scratch1 = vec(1), vec(1)
        passes = ctx.enter_context(nc.sbuf_tensor("passes", [P, 1], mybir.dt.int32))
        nmax, psum_p = vec(2), vec(2)
        d_small = vec(PAIRS)
        vrows = xT[0:101, 0, 0:128]

        pre = region(16384, QKV_T, SEQ + CONV - 1)
        qkvT = region(22600, QKV_T, SEQ)
        zT = region(28744, HEADS, SEQ)
        decT = region(30792, 16, P)
        decL = region(32840, 16, P)
        e_row = region(34888, HEADS, P)
        vn = region(35912, NT, HEADS, P)
        s1 = region(37960, HEADS, P)
        o = region(38984, NT * HEADS, P)
        sq = region(38984, 2, 512)
        rs = region(40008, 2, 512)
        r1 = region(41032, HEADS, P)
        kd = region(42056, HEADS, P)
        D, DT, QT = region(16384, 16, P), region(18432, 16, P), region(20480, 16, P)
        vtok = region(22600 + 16 * SEQ, 16, P)
        oT = region(32840, HEADS, SEQ)
        f1 = [region(6144 * i, KT, FC * P) for i in range(FF_SETS)]
        f3 = [region(6144 * i + 2048, KT, FC * P) for i in range(FF_SETS)]
        f2 = [region(6144 * i + 4096, FC, DM) for i in range(FF_SETS)]
        hT = region(18432, 2, FC, SEQ)
        hsil = region(19456, 2, SEQ)
        m1 = [region(ESLAB * c, KT, EW1) for c in range(EC)]
        m3 = [region(ESLAB * (EC + c), KT, EW1) for c in range(EC)]
        m2 = [region(ESLAB * (2 * EC + c), FE_T, EW2) for c in range(EC)]
        xg = region(33792, KT, P)
        msil = region(34816, 2, EW1)
        mh = region(35520, FE)
        macc = region(36928, NT, DM)
        mhT = region(38976, FE_T, P)
        ysb = region(40384, DM)
        pick = region(41408, NT, P)
        pick_g = region(41664, NT, P)
        spread = region(41920, NT, P)
        V = region(19968, 2, PAIRS, 9, GC)
        W1T = region(29184, 2, PAIRS, P)
        Wp = region(37376, 2, PIECE, SUB, GC)
        KD = region(39424, PIECE, P, parts=2 * GC)
        skip = region(40448, 4, GC, parts=2 * GC)
        Bb = region(40576, 2, PAIRS, GC)
        Ct = region(41600, 2, PAIRS, GC)
        pw = region(42624, 2, 9, PAIRS)
        pw_back = region(43200, 2, SUB, PAIRS)
        Bbd = region(43712, 2, PIECE, 2 * GC)
        B_raw = region(29184, 2, PAIRS, GC)
        C_raw = region(30208, 2, 8, STATE)
        lam_raw = region(31232, 2, STATE, parts=32)
        lam_raw2 = region(31360, 2, STATE, parts=32)
        lam = region(31488, 2, PAIRS)
        dts = region(31552, PAIRS)
        z = region(31584, 2, PAIRS)
        pw_mag = region(31648, 9, PAIRS)
        pw_ang = region(32192, 2, 9, PAIRS)
        pw_n = region(33280, 2, 9, PAIRS)
        sc = [region(34368 + 32 * i, PAIRS) for i in range(12)]
        sin_b = region(34752, PAIRS)
        tb = region(34784, PAIRS, GC)
        kzero = region(35296, 1024, parts=2 * GC)
        flat_w = norm_w[:].rearrange("p a b -> p (a b)")
        t_p, t_v = flat_w[:, 0:PIECE * 9 * GC], flat_w[:, PIECE * 9 * GC:PIECE * 9 * GC * 3 // 2]
        d_col = d_small[0:2 * GC]
        u_n = region(0, SUB, PAIRS * GC, parts=64)
        u_r = region(4096, PAIRS, P, parts=64)
        y_sb = region(0, 2, SUB, P, parts=64)
        hidT = region(2048, KT, SEQ)
        T = region(8192, 2, PAIRS, P)
        U = region(16384, PAIRS, 2, NSUB)
        u_tok = region(16384, NT, DM)
        E = region(37376, 2, PAIRS, NSUB)
        H = region(29184, NSUB, 2, PAIRS)
        Hbd = region(31232, 2, PAIRS, 2, NSUB)
        ht = [region(35328 + 672 * i, 4, 2, PAIRS) for i in range(2)]
        hc = [region(35328 + 672 * i, 3, 7, PAIRS) for i in range(2)]
        p8 = region(43712, 2, 8, PAIRS)
        carry = region(18432, 4, 2, PAIRS)
        ebuf = region(18688, 4, 2, PAIRS)
        glu = [region(o_, KT, 512) for o_ in (4096, 39424, 8192, 12288)]
        gsig = region(33792, NT, DM)
        slot8 = [4096 * i for i in range(8)]
        q2 = region(32768 + 0, 4, SEQ)
        k2 = region(33792, 4, SEQ)
        v2 = region(34816, NT, 512)
        u2 = region(35840, NT, 512)
        poolT = region(36864, 4, SEQ)
        catT = region(37888, 8, SEQ)
        prob = region(39936, 2, 2, SEQ)
        probT = region(40960, 2, 2, SEQ)
        bias = region(16384, NT, AH, SEQ)
        poolw = region(20480, NT, 4, SEQ)
        wpool = region(22528, 4, P)
        amask = region(23040, GRID)
        h2n = region(41984, NT, DM)
        mT = region(32768, 2, 4, SEQ)
        u_dram = nc.dram_tensor("u_scratch", (SEQ, DM), F32, kind="Internal").ap()
        k_dram = nc.dram_tensor("k_scratch", (2 * GC, PAIRS, 2 * P), F32, kind="Internal").ap()

        x_loaded, const_loaded, vecs_loaded = sem("x_loaded"), sem("const_loaded"), sem("vecs_loaded")
        normw_loaded, small_loaded = sem("normw_loaded"), sem("small_loaded")
        ba_w_loaded = sem("ba_w_loaded")
        ready = sem("consts_ready")
        vec_tr, vec_ok = sem("vec_transposed"), sem("vec_ok")
        slab = [sem(f"slab{i}_loaded") for i in range(9)]
        xt_tr, xt_v, xt_a = sem("x_transposed"), sem("xT_by_vector"), sem("xT_by_scalar")
        norm_done = sem("norm_done")
        var_ready, std_ready = sem("var_ready"), sem("std_ready")
        ba_done = sem("ba_done")
        ba_v, ba_a, g_ready = sem("ba_by_vector"), sem("ba_by_scalar"), sem("g_ready")
        in_tile, pre_ready, conv_done, silu_done = sem("in_tile"), sem("pre_ready"), sem("conv_done"), sem("silu_done")
        pad_ready = sem("pad_ready")
        sq_ready, ss_ready, nrm_ready, unit_ready = sem("sq_ready"), sem("ss_ready"), sem("nrm_ready"), sem("unit_ready")
        grow_done, gc_ready, dec_v, dec_a, dec_ready = sem("grow_done"), sem("gc_ready"), sem("dec_v"), sem("dec_a"), sem("dec_ready")
        kq_done, kq_read = sem("kq_done"), sem("kq_read")
        d_tr, d_evac = sem("d_transposed"), sem("dT_ready")
        lv_q, lv_qe, lv_p, lv_pe = sem("level_q"), sem("level_q_read"), sem("level_p"), sem("level_p_read")
        vk_tr, vk_ready = sem("vk_transposed"), sem("vk_ready")
        rec, rec_ev = sem("recurrence_step"), sem("recurrence_read")
        o_std, o_norm, o_tr, o_ready = sem("o_std"), sem("o_norm"), sem("o_tr"), sem("o_ready")
        y_done = sem("y_done")
        up_done, sil_done, h_done = sem("up_done"), sem("sil_done"), sem("h_done")
        down_done = sem("down_done")
        s5_loaded, s5_tr, s5_in, s5_read = sem("s5_loaded"), sem("s5_param_tr"), sem("s5_dt_ready"), sem("s5_param_read")
        s5_v, s5_a = sem("s5_by_vector"), sem("s5_by_scalar")
        bb_ready, w_ready, w_tr, w_in, v_ready = sem("bb_ready"), sem("w_ready"), sem("w_tr"), sem("w1t_ready"), sem("v_ready")
        im_ready = sem("im_ready")
        kd_done, kd_ready, kd_stored, t_loaded = sem("kd_done"), sem("kd_ready"), sem("kd_stored"), sem("t_loaded")
        kz_stored = sem("kz_stored")
        u_sb, u_stored, un_loaded, ur_ready, u_tr, u_ready = sem("u_sb"), sem("u_stored"), sem("un_loaded"), sem("ur_ready"), sem("u_tr"), sem("u_ready")
        e_done, e_read, h_bd, hbd_zero = sem("e_done"), sem("e_read"), sem("h_bd"), sem("hbd_zero")
        ys_done, ys_read, yt_done, hid_ready = sem("ys_done"), sem("ys_read"), sem("yt_done"), sem("hid_ready")
        glu_done, sig_done, glu_read = sem("glu_done"), sem("sig_done"), sem("glu_read")
        route_done, route_read, route_a = sem("route_done"), sem("route_read"), sem("route_a")
        chosen_ready, place_done, passes_ready = sem("chosen_ready"), sem("place_done"), sem("passes_ready")
        m_loaded = [sem(f"expert_slabs{i}_loaded") for i in range(2 * EC)]
        pick_ready, pickg_ready, gath_done, xg_ready = sem("pick_ready"), sem("pick_gate_ready"), sem("gather_done"), sem("xg_ready")
        m_up, m_sil, m_h, m_tr, m_hT = sem("expert_up"), sem("expert_silu"), sem("expert_h"), sem("expert_hT_transposed"), sem("expert_hT_ready")
        m_y, m_yread, m_sc, m_acc = sem("expert_y"), sem("expert_y_read"), sem("expert_scattered"), sem("expert_added")
        b2_loaded, bias_ready = sem("b2_loaded"), sem("bias_ready")
        p_done, p_read_a, p_read_v = sem("proj2_done"), sem("proj2_by_scalar"), sem("proj2_by_vector")
        pool_done, pool_read, mix_done, mix_read = sem("pool_done"), sem("pool_read"), sem("mix_done"), sem("mix_read")
        sc_done, max_ready, exp_done, pn_ready = sem("score_done"), sem("max_ready"), sem("exp_done"), sem("prob_ready")
        pt_done, pt_read, pv_done, pv_read = sem("pt_done"), sem("pt_read"), sem("pv_done"), sem("pv_read")
        y2_done, up2_done, relu_done, sqr_done = sem("y2_done"), sem("up2_done"), sem("relu_done"), sem("sqr_done")
        down2_done, out_stored = sem("down2_done"), sem("out_stored")
        chain_v, chain_a, chain_p = sem("vector_chain"), sem("scalar_chain"), sem("pool_chain")

        block = ctx.enter_context(nc.Block())

        def rows(w, k0, n):
            return w[k0 * P:(k0 + n) * P, :].rearrange("(k p) f -> p k f", p=P)

        sent, arrival = {}, {}

        def load(eng, key, i, dst, src):
            sent[i] = sent.get(i, 0) + 16
            arrival[key] = (slab[i], sent[i])
            eng.dma_start(dst, src).then_inc(slab[i], 16)

        def arrived(eng, key):
            eng.wait_ge(*arrival[key])

        def after(eng, sem_, value):
            if not isinstance(value, int) or value > 0:
                eng.wait_ge(sem_, value)

        def every(ap, n, off=0):
            return bass.AP(ap.tensor, ap.offset + off, [[0, P], [1, n]])

        def table_product(eng_ns, link, dst, pa, pb, qa, qb, t, sub):
            link(eng_ns.tensor_tensor(dst, pa, qa, ALU.mult))
            link(eng_ns.tensor_tensor(t, pb, qb, ALU.mult))
            return eng_ns.tensor_tensor(dst, dst, t, ALU.subtract if sub else ALU.add)

        def s5_factors(pr, powers, n, tab):
            shape = (P, pr.stop - pr.start, n, GC)

            def power(c):
                return powers[:, c, :, pr].rearrange("p k a -> p a k")[:, :, :, None].broadcast_to(shape)

            def table(c):
                return tab[:, c, pr, None, :].broadcast_to(shape)
            return power, table

        def s5_v_table(eng_ns, link, pr, part, t):
            power, table = s5_factors(pr, pw, 9, Ct)
            n = pr.stop - pr.start
            dst = V[:, part, pr]
            tt = t[:, 0:n * 9 * GC].rearrange("p (a b c) -> p a b c", a=n, b=9)
            if part == 0:
                return table_product(eng_ns, link, dst, power(0), power(1), table(0), table(1), tt, True)
            link(table_product(eng_ns, link, dst, power(0), power(1), table(1), table(0), tt, False))
            return eng_ns.tensor_scalar(dst, dst, -1.0, None, ALU.mult)

        def s5_w_table(eng_ns, link, j, part, t):
            power, table = s5_factors(slice(PIECE * j, PIECE * (j + 1)), pw_back, SUB, Bb)
            tt = t[:, 0:PIECE * SUB * GC].rearrange("p (a b c) -> p a b c", a=PIECE, b=SUB)
            if part == 0:
                return table_product(eng_ns, link, Wp[:, 0], power(0), power(1), table(0), table(1), tt, True)
            return table_product(eng_ns, link, Wp[:, 1], power(0), power(1), table(1), table(0), tt, False)

        def s5_pool(pool, link):
            for i, name in enumerate(("s5_lam_re", "s5_lam_im")):
                pool.dma_start(lam_raw[:, i], A[name][0, 0:32]).then_inc(s5_loaded, 16)
                pool.dma_start(lam_raw2[:, i], A[name][0, 32:64]).then_inc(s5_loaded, 16)
            for i, name in enumerate(("s5_c_re", "s5_c_im")):
                pool.dma_start(C_raw[:, i], A[name][0].rearrange("(j g) c p -> (g c) j p", j=8)).then_inc(s5_loaded, 16)
            for gh in range(2):
                half = slice(64 * gh, 64 * gh + 64)
                pool.dma_start(dts[half], bass.AP(A["s5_log_dt"].tensor, 32 * gh, [[0, 64], [1, 32]])).then_inc(s5_loaded, 16)
                for i, name in enumerate(("s5_b_re", "s5_b_im")):
                    pool.dma_start(B_raw[half, i], A[name][0, 32 * gh:32 * gh + 32].rearrange("g p c -> p g c")).then_inc(s5_loaded, 16)
            with nc.allow_non_contiguous_dma("1024 values"):
                for gh in range(2):
                    pool.dma_start(d_col[GC * gh:GC * gh + GC], A["s5_d"][0, 512 * gh:512 * gh + 512].rearrange("(a c) -> c a", c=GC)).then_inc(s5_loaded, 16)
            link(nc.gpsimd.memset(kzero, 0.0))
            for q in range(4):
                pool.dma_start(k_dram[:, 8 * q:8 * q + 8, 0:P], kzero.rearrange("p (a b) -> p a b", a=8)).then_inc(kz_stored, 16)
            link(nc.gpsimd.memset(Bbd, 0.0))
            pool.wait_ge(bb_ready, 1)
            for j in range(NPIECE):
                pr = slice(PIECE * j, PIECE * (j + 1))
                if j:
                    pool.wait_ge(w_tr, 4 * j)
                for part in range(2):
                    s5_w_table(nc.gpsimd, link, j, part, t_p).then_inc(w_ready, 1)
                    pool.wait_ge(w_ready, 2 * j + part + 1)
                if j:
                    pool.wait_ge(kd_done, 2 * j)
                for gh in range(2):
                    half = slice(64 * gh, 64 * gh + 64)
                    link(nc.gpsimd.tensor_copy(Bbd[half, :, :, GC * gh:GC * gh + GC], Bb[half, :, pr]))
                s5_v_table(nc.gpsimd, link, pr, 1, t_p).then_inc(im_ready, 1)
                pool.wait_ge(im_ready, j + 1)

        def inverse_update(dve, V_, lv, j):
            s = slice(4 * j, 4 * j + 4)
            i = 4 * (lv - 1) + j
            dve.wait_ge(lv_p, i + 1)
            V_.tensor_tensor(DT[:, s], DT[:, s], four(banks[2 + j % 2]), ALU.subtract).then_inc(lv_pe, 1)
            if lv < LEVELS - 1:
                V_.tensor_tensor(D[:, s], D[:, s], four(banks[4 + j % 2]), ALU.subtract).then_inc(lv_pe, 1)

        @block.sync
        def _(sp):
            sp.dma_start(const[:], A["shape_const"].rearrange("p (a b) -> p a b", b=P)).then_inc(const_loaded, 16)
            sp.dma_start(xres[:], A["x"][0].rearrange("(n p) d -> p n d", p=P)).then_inc(x_loaded, 16)
            w_in = A["gdn_w_in"][0].rearrange("(k p) f -> p k f", p=P)
            sp.wait_ge(vecs_loaded, 48)
            sp.wait_ge(ba_w_loaded, 16)
            for b in range(8):
                if b >= 4:
                    sp.wait_ge(in_tile, 4 * (b - 3))
                load(sp, ("gdn_in", b), b % 4, region(4096 * (b % 4), KT, 512), w_in[:, :, 512 * b:512 * b + 512])

            w1, w3 = (A[f"ffn_w{i}"][0].rearrange("(k p) f -> p k f", p=P) for i in (1, 3))
            w2 = A["ffn_w2"][0]

            def swiglu_loads(c):
                i, cols = c % FF_SETS, slice(FC * P * c, FC * P * (c + 1))
                if c >= FF_SETS:
                    sp.wait_ge(up_done, 2 * FC * (c - FF_SETS + 1))
                load(sp, ("ffn_w1", c), 4 + i, f1[i], w1[:, :, cols])
                load(sp, ("ffn_w3", c), 4 + i, f3[i], w3[:, :, cols])
                if c >= FF_SETS:
                    sp.wait_ge(down_done, c - FF_SETS + 1)
                load(sp, ("ffn_w2", c), i, f2[i], rows(w2, FC * c, FC))

            for c in range(2):
                sp.wait_ge(in_tile, 4 * (c + 7))
                load(sp, ("gdn_out", c), 2 + c, region(4096 * (2 + c), 4, DM), rows(A["gdn_w_out"][0], 4 * c, 4))
            swiglu_loads(0)
            sp.wait_ge(y_done, 4)
            for c in range(1, FF_CHUNKS):
                swiglu_loads(c)
            sp.wait_ge(up_done, 2 * FC * FF_CHUNKS)
            sp.wait_ge(down_done, FF_CHUNKS - 1)
            for c in range(2):
                load(sp, ("s5_in", c), 7 + c, region(4096 * c, 4, DM), rows(A["s5_w_in"][0], 4 * c, 4))
            sp.wait_ge(kd_stored, 16 * NPIECE)
            sp.wait_ge(kz_stored, 64)
            sp.wait_ge(y_done, 8)
            for gh in range(2):
                for s in range(SUB):
                    sp.dma_start(T[GC * s:GC * (s + 1), gh],
                                 k_dram[GC * gh:GC * (gh + 1), :, (SUB - s) * GC:(SUB - s) * GC + P]).then_inc(t_loaded, 16)
            sp.wait_ge(u_sb, 4)
            sp.dma_start(u_dram.rearrange("(n p) d -> p n d", p=P), u_tok).then_inc(u_stored, 16)
            sp.wait_ge(u_stored, 16)
            for gh in range(2):
                sp.dma_start(u_n[32 * gh:32 * gh + 32],
                             u_dram[:, 512 * gh:512 * gh + 512].rearrange("(n s) d -> n s d", s=SUB)).then_inc(un_loaded, 16)
            w_glu = A["s5_w_glu"][0].rearrange("(k p) f -> p k f", p=P)
            sp.wait_ge(u_tr, 4)
            for i, c in enumerate((0, 2, 1, 3)):
                if i == 2:
                    sp.wait_ge(ys_done, NPIECE * 2)
                load(sp, ("glu", i), i, glu[i], w_glu[:, :, 512 * c:512 * c + 512])
            sp.wait_ge(glu_done, 8)

            def expert_loads(e, k):
                w1e, w3e, w2e = (A[f"moe_w{i}"][0][bass.ds(e, 1)].rearrange("e (k p) f -> p (e k) f", p=P) for i in (1, 3, 2))
                for c in range(EC):
                    cols = slice(EW1 * c, EW1 * c + EW1)
                    sp.wait_ge(m_up, k * 2 * EC + 2 * c + 1)
                    sp.dma_start(m1[c], w1e[:, :, cols]).then_inc(m_loaded[c], 16)
                    sp.wait_ge(m_up, k * 2 * EC + 2 * c + 2)
                    sp.dma_start(m3[c], w3e[:, :, cols]).then_inc(m_loaded[c], 16)
                for c in range(EC):
                    sp.wait_ge(m_y, k * EC + c + 1)
                    sp.dma_start(m2[c], w2e[:, :, EW2 * c:EW2 * c + EW2]).then_inc(m_loaded[EC + c], 16)

            expert_loads(0, 0)
            sp.wait_ge(passes_ready, 1)
            n_pass = sp.value_load(passes[0:1, 0:1], min_val=1, max_val=2)
            with sp.Fori(1, n_pass * EXPERTS) as k:
                expert_loads(k % EXPERTS, k)
            sp.wait_ge(m_y, n_pass * (EXPERTS * EC) + EC)
            w_in2 = A["w_in_2"][0].rearrange("(k p) f -> p k f", p=P)
            for i in range(4):
                load(sp, ("in2", i), i, region(4096 * i, KT, 512), w_in2[:, :, 512 * i:512 * i + 512])
            for c in range(2):
                load(sp, ("out2", c), 4 + c, region(4096 * (6 + c), 4, DM), rows(A["w_out_2"][0], 4 * c, 4))
            sp.wait_ge(p_done, 12)
            w_up = A["w_up_2"][0].rearrange("(k p) f -> p k f", p=P)
            for i in range(4):
                for c in range(2):
                    if i:
                        sp.wait_ge(up2_done, 8 * (i - 1) + 4 * (c + 1))
                    f0 = 512 * (2 * i + c)
                    load(sp, ("up2", 2 * i + c), 6 + c, region(4096 * c, KT, 512), w_up[:, :, f0:f0 + 512])
                for c in range(2):
                    if i:
                        sp.wait_ge(down2_done, 2 * (i - 1) + c + 1)
                    load(sp, ("down2", 2 * i + c), 2 + c, region(4096 * (2 + c), 4, DM), rows(A["w_down_2"][0], 4 * (2 * i + c), 4))
            sp.wait_ge(norm_done, 7)
            sp.dma_start(out[0].rearrange("(n p) d -> p n d", p=P), xres[:]).then_inc(out_stored, 16)
            sp.wait_ge(out_stored, 16)

        @block.gpsimd
        def _(pool):
            count = [0]

            def link(ins):
                count[0] += 1
                ins.then_inc(chain_p, 1)
                pool.wait_ge(chain_p, count[0])

            pool.dma_start(vrows[0:96], A["gdn_conv_w"][0].rearrange("j (t p) -> (j t) p", p=P)).then_inc(vecs_loaded, 16)
            pool.dma_start(vrows[96:97], A["gdn_norm_g"]).then_inc(vecs_loaded, 16)
            pool.dma_start(vrows[97:101], A["pool_scale_2"][0].rearrange("(t p) -> t p", p=P)).then_inc(vecs_loaded, 16)
            pool.dma_start(region(38984, KT, 16), A["gdn_w_in"][0].rearrange("(k p) f -> p k f", p=P)[:, :, 4096:4112]).then_inc(ba_w_loaded, 16)
            pool.dma_start(a_log, every(A["gdn_a_log"], 8)).then_inc(small_loaded, 16)
            pool.dma_start(dt_b, every(A["gdn_dt_bias"], 8)).then_inc(small_loaded, 16)
            pool.dma_start(router_b, every(A["moe_b_router"], 8)).then_inc(small_loaded, 16)

            def norm_load(slot, name, off):
                pool.dma_start(norm_w[:, slot, :], every(A[name], DM, off)).then_inc(normw_loaded, 16)

            norm_load(0, "ln_g", 0)
            norm_load(1, "ln_b", 0)
            nc.gpsimd.memset(pre[:, :, 0:CONV - 1], 0.0).then_inc(pad_ready, 1)
            for i in range(8):
                pool.wait_ge(silu_done, i // 2 + 1)
                if i == 0:
                    pool.wait_ge(ba_done, 1)
                if i >= 2:
                    pool.wait_ge(ss_ready, i - 1)
                src = qkvT[:, 2 * i:2 * i + 2, :].rearrange("p a b -> p (a b)")
                nc.gpsimd.tensor_tensor(sq[:, i % 2, :], src, src, ALU.mult).then_inc(sq_ready, 1)
            for j in range(4):
                pool.wait_ge(dec_a, 2 * (j + 1))
                s = slice(4 * j, 4 * j + 4)
                nc.gpsimd.tensor_tensor(decL[:, s, :], decL[:, s, :], over(mat(C_LOW), 4), ALU.mult).then_inc(dec_ready, 1)
                nc.gpsimd.tensor_tensor(decT[:, s, :], decT[:, s, :], over(mat(C_TRI), 4), ALU.mult).then_inc(dec_ready, 1)
            pool.wait_ge(norm_done, 1)
            pool.dma_start(w_router, A["moe_w_router"][0].rearrange("(k p) f -> p k f", p=P)).then_inc(small_loaded, 16)
            s5_pool(pool, link)
            pool.wait_ge(v_ready, 2 * NPIECE)
            norm_load(0, "ln_g", DM)
            norm_load(1, "ln_b", DM)
            for n in (2, 3):
                pool.wait_ge(norm_done, n)
                norm_load(0, "ln_g", n * DM)
                norm_load(1, "ln_b", n * DM)
                if n == 2:
                    pool.wait_ge(e_read, 8)
                    nc.gpsimd.memset(Hbd, 0.0).then_inc(hbd_zero, 1)
            pool.wait_ge(norm_done, 4)
            norm_load(0, "norm_mix_g_2", 0)
            norm_load(1, "norm_mlp_g_2", 0)
            for r in range(4):
                for i in range(4):
                    src = bass.AP(A["rpb_2"].tensor, (7 + i - r) * 31 - 48, [[1, GRID], [15 * 31, AH], [1, GRID]])
                    dst = bias[GRID * (r % 2):GRID * (r % 2) + GRID, r // 2, :, GRID * i:GRID * i + GRID]
                    pool.dma_start(dst, src).then_inc(b2_loaded, 16)
            pool.dma_start(amask, A["shape_mask"]).then_inc(b2_loaded, 16)
            pool.dma_start(poolw, A["shape_pool"].rearrange("(n p) a b -> p n a b", p=P)).then_inc(b2_loaded, 16)
            pool.dma_start(wpool, A["w_pool_2"][0].rearrange("a p b -> p a b")).then_inc(b2_loaded, 16)
            pool.wait_ge(b2_loaded, 16 * 19)
            for n in range(NT):
                v = bias[:, n].rearrange("p h (i k) -> p (h i) k", k=GRID)
                ins = nc.gpsimd.tensor_tensor(v, v, over(amask, AH * 4), ALU.add)
                ins.then_inc(bias_ready, 1)
            pool.wait_ge(norm_done, 5)
            norm_load(0, "final_g_2", 0)

        @block.vector
        def _(dve):
            V_ = nc.vector
            count = [0]

            def link(ins):
                count[0] += 1
                ins.then_inc(chain_v, 1)
                dve.wait_ge(chain_v, count[0])

            for c, val in ((eps_ln, LN_EPS), (eps_rms, EPS), (one_c, 1.0), (zero_c, 0.0)):
                last = V_.memset(c, val)
            last.then_inc(ready, 1)

            seen_xt = [0]

            def take_xT():
                for j in (0, 2):
                    dve.wait_ge(xt_tr, 4 * seen_xt[0] + j + 1)
                    V_.tensor_copy(xT[:, 4 * (j % 2) + 0:4 * (j % 2) + 4, P * (j // 2):P * (j // 2) + P], four(banks[4 + j])).then_inc(xt_v, 1)
                seen_xt[0] += 1

            dve.wait_ge(vec_tr, 1)
            V_.tensor_copy(vecT, banks[3][:, 0:101]).then_inc(vec_ok, 1)
            take_xT()
            dve.wait_ge(ba_done, 1)
            for n in range(NT):
                last = V_.tensor_copy(ba[:, n], banks[6 + n][:, 0:16])
            link(last)
            dve.wait_ge(small_loaded, 48)
            V_.tensor_tensor(tmp_a, ba[:, :, 8:16], over(dt_b, NT), ALU.add).then_inc(ba_v, 1)
            dve.wait_ge(ba_a, 2)
            dve.wait_ge(ba_v, 1)
            link(V_.tensor_scalar(tmp_a, tmp_a, 0.0, None, ALU.max))
            link(V_.tensor_tensor(tmp_a, tmp_a, tmp_b, ALU.add))
            link(V_.tensor_scalar(tmp_a, tmp_a, -1.0, None, ALU.mult))
            V_.tensor_tensor(g, tmp_a, over(a_log, NT), ALU.mult).then_inc(g_ready, 1)

            for b in range(6):
                dve.wait_ge(pre_ready, 4 * (b + 1))
                if b == 0:
                    dve.wait_ge(pad_ready, 1)
                    dve.wait_ge(vec_ok, 1)
                for j in range(CONV):
                    for m in range(4 * b, 4 * b + 4):
                        w = vecT[:, j * QKV_T + m:j * QKV_T + m + 1]
                        if j == 0:
                            last = V_.tensor_scalar(qkvT[:, m], pre[:, m, 0:SEQ], w, None, ALU.mult)
                        else:
                            last = V_.scalar_tensor_tensor(qkvT[:, m], pre[:, m, j:j + SEQ], w, qkvT[:, m], ALU.mult, ALU.add)
                    if j < CONV - 1:
                        link(last)
                last.then_inc(conv_done, 1)

            for i in range(8):
                dve.wait_ge(nrm_ready, i + 1)
                link(V_.reciprocal(rs[:, i % 2, :], rs[:, i % 2, :]))
                v = qkvT[:, 2 * i:2 * i + 2, :].rearrange("p a b -> p (a b)")
                V_.scalar_tensor_tensor(v, rs[:, i % 2, :], DK ** -0.5 if i < 4 else 1.0, v, ALU.mult, ALU.mult).then_inc(unit_ready, 1)
            dve.wait_ge(grow_done, 1)
            link(V_.tensor_copy(gc.rearrange("p a b -> p (a b)"), banks[3][:, 0:16]))
            for j in range(4):
                dve.wait_ge(grow_done, j + 2)
                for b in range(4 * j, 4 * j + 4):
                    src = four(banks[4 + j])[:, b % 4]
                    col = gc.rearrange("p a b -> p (a b)")[:, b:b + 1]
                    V_.tensor_scalar(decL[:, b], src, col, 0.0, ALU.subtract, ALU.max)
                    last = V_.tensor_scalar(decT[:, b], src, col, 0.0, ALU.subtract, ALU.min)
                if j < 2:
                    link(last)
                    last = V_.tensor_copy(glast[:, 4 * j:4 * j + 4], four(banks[4 + j])[:, :, P - 1])
                last.then_inc(dec_v, 1)
            dve.wait_ge(dec_v, 4)
            V_.tensor_tensor(tmp_a[:, 0], glast, gc[:, 0], ALU.subtract).then_inc(gc_ready, 1)
            dve.wait_ge(dec_a, 12)
            link(V_.tensor_scalar(neg_eg, neg_eg, -1.0, None, ALU.mult))
            dve.wait_ge(unit_ready, 4)
            link(V_.tensor_tensor(e_row, e_row, qkvT[:, 0:8, P:2 * P], ALU.mult))
            for j in range(4):
                dve.wait_ge(kq_done, j + 1)
                dve.wait_ge(dec_ready, 2 * (j + 1))
                for b in range(4 * j, 4 * j + 4):
                    bcol = beta.rearrange("p a b -> p (a b)")[:, b:b + 1]
                    V_.scalar_tensor_tensor(decL[:, b], four(banks[j % 2])[:, b % 4], bcol, decL[:, b], ALU.mult, ALU.mult)
                s = slice(4 * j, 4 * j + 4)
                last = V_.tensor_tensor(decT[:, s], four(banks[2 + j % 2]), decT[:, s], ALU.mult)
                link(last)
                link(V_.scalar_tensor_tensor(D[:, s], decL[:, s], -1.0, over(mat(C_M0), 4), ALU.mult, ALU.mult))
                V_.tensor_tensor(D[:, s], D[:, s], over(ident, 4), ALU.add).then_inc(kq_read, 1)
            for j in range(4):
                dve.wait_ge(d_tr, j + 1)
                V_.tensor_copy(DT[:, 4 * j:4 * j + 4], four(banks[4 + j])).then_inc(d_evac, 1)
            for lv in range(1, LEVELS):
                for j in range(4):
                    s = slice(4 * j, 4 * j + 4)
                    i = 4 * (lv - 1) + j
                    dve.wait_ge(lv_q, i + 1)
                    V_.tensor_tensor(QT[:, s], four(banks[j % 2]), over(mat(C_LV + lv), 4), ALU.mult).then_inc(lv_qe, 1)
                    if j:
                        inverse_update(dve, V_, lv, j - 1)
                inverse_update(dve, V_, lv, 3)
            dve.wait_ge(vk_tr, 4)
            for b in range(16):
                src = four(banks[b // 4])[:, b % 4]
                if b < 8:
                    V_.tensor_scalar(vtok[:, b], src, beta[:, 0, b:b + 1], None, ALU.mult).then_inc(vk_ready, 1)
                else:
                    V_.tensor_copy(vtok[:, b], src).then_inc(vk_ready, 1)
            for h in range(8):
                dve.wait_ge(vk_tr, 5 + h // 4)
                V_.tensor_scalar(kd[:, h], four(banks[4 + h // 4])[:, h % 4], kdf[:, h:h + 1], None, ALU.mult).then_inc(vk_ready, 1)
            for j in range(2):
                dve.wait_ge(rec, j + 1)
                V_.tensor_copy(vn[:, 0, 4 * j:4 * j + 4], four(banks[6 + j])).then_inc(rec_ev, 1)
            for j in range(2):
                dve.wait_ge(rec, 3 + 2 * j)
                V_.tensor_copy(s1[:, 4 * j:4 * j + 4], four(banks[j])).then_inc(rec_ev, 1)
                dve.wait_ge(rec, 4 + 2 * j)
                V_.tensor_copy(o[:, 4 * j:4 * j + 4], four(banks[2 + j])).then_inc(rec_ev, 1)
            for j in range(2):
                dve.wait_ge(rec, 7 + j)
                dve.wait_ge(vk_ready, 24)
                for h in range(4 * j, 4 * j + 4):
                    last = V_.scalar_tensor_tensor(r1[:, h], four(banks[4 + j])[:, h % 4], neg_eg[:, h:h + 1], vtok[:, 8 + h], ALU.mult, ALU.add)
                link(last)
                for h in range(4 * j, 4 * j + 4):
                    last = V_.tensor_scalar(r1[:, h], r1[:, h], beta[:, 1, h:h + 1], None, ALU.mult)
                last.then_inc(rec_ev, 1)
            for j in range(2):
                dve.wait_ge(rec, 9 + j)
                V_.tensor_copy(vn[:, 1, 4 * j:4 * j + 4], four(banks[6 + j])).then_inc(rec_ev, 1)
            for j in range(2):
                dve.wait_ge(rec, 11 + j)
                V_.tensor_copy(o[:, 8 + 4 * j:12 + 4 * j], four(banks[j])).then_inc(rec_ev, 1)
            dve.wait_ge(o_std, 1)
            link(V_.reciprocal(o_ss, o_ss))
            V_.tensor_tensor(o, o, o_ss[:, :, None].broadcast_to((P, 16, P)), ALU.mult).then_inc(o_norm, 1)
            for j in range(4):
                dve.wait_ge(o_tr, j + 1)
                hs, ts = slice(4 * (j % 2), 4 * (j % 2) + 4), slice(P * (j // 2), P * (j // 2) + P)
                V_.scalar_tensor_tensor(oT[:, hs, ts], four(banks[4 + j]), vecT[:, 96:97], zT[:, hs, ts], ALU.mult, ALU.mult).then_inc(o_ready, 1)

            done = [0]

            def norm_tail(rms):
                done[0] += 1
                dve.wait_ge(std_ready, done[0])
                link(V_.reciprocal(rstd, rstd))

            def layer_norm(src, scale, signal):
                for n in range(NT):
                    for hf in range(2):
                        r = xres[:, n, 512 * hf:512 * hf + 512]
                        link(V_.scalar_tensor_tensor(r, r, scale, src(n, hf), ALU.mult, ALU.add))
                        link(V_.bn_stats(stats[:, n, hf, :], r))
                    last = V_.bn_aggr(mv[:, n], stats[:, n].rearrange("p a b -> p (a b)"))
                    if n == 0:
                        link(last)
                last.then_inc(var_ready, 1)
                norm_tail(False)
                dve.wait_ge(normw_loaded, 32 * (signal + 1))
                for n in range(NT):
                    r = xres[:, n]
                    link(V_.tensor_scalar(r, r, mv[:, n, 0:1], rstd[:, n:n + 1], ALU.subtract, ALU.mult))
                    link(V_.tensor_tensor(r, r, norm_w[:, 0], ALU.mult))
                    last = V_.tensor_tensor(r, r, norm_w[:, 1], ALU.add)
                    if n == 0:
                        link(last)
                last.then_inc(norm_done, 1)
                dve.wait_ge(norm_done, signal + 1)

            def from_banks(base):
                def src(n, hf):
                    dve.wait_ge(y_done, base + 2 * n + hf + 1)
                    return banks[2 * n + hf][:, :]
                return src

            layer_norm(from_banks(0), ALPHA, 0)
            take_xT()

            def s5_parameters():
                dve.wait_ge(s5_tr, 1)
                V_.tensor_copy(lam.rearrange("p a b -> p (a b)"), banks[4][:, 0:64])
                for i in range(2):
                    for jb in range(8):
                        half = slice(64 * (jb // 4), 64 * (jb // 4) + 64)
                        last = V_.tensor_copy(Ct[half, i, 8 * (jb % 4):8 * (jb % 4) + 8].rearrange("p a b -> p (a b)"),
                                              banks[5 + i][half, P * (jb % 4):P * (jb % 4) + P])
                last.then_inc(s5_read, 1)
                dve.wait_ge(s5_read, 1)
                dve.wait_ge(s5_in, 1)
                link(V_.tensor_tensor(z, lam, dts[:, None, :].broadcast_to((P, 2, PAIRS)), ALU.mult))
                for k in range(9):
                    V_.tensor_scalar(pw_mag[:, k], z[:, 0], float(k), None, ALU.mult)
                    V_.tensor_scalar(pw_ang[:, 1, k], z[:, 1], float(k), None, ALU.mult)
                    last = V_.tensor_scalar(pw_ang[:, 0, k], z[:, 1], float(k), float(np.pi / 2), ALU.mult, ALU.add)
                link(last)
                ROUND = 12582912.0
                C1 = 6.28125
                C2 = 0.0019353071795864769
                flat = [t.rearrange("p a b c -> p (a b c)") for t in (pw_ang, pw_n)]
                link(V_.tensor_scalar(flat[1], flat[0], float(1 / (2 * np.pi)), ROUND, ALU.mult, ALU.add))
                link(V_.tensor_scalar(flat[1], flat[1], ROUND, None, ALU.subtract))
                link(V_.scalar_tensor_tensor(flat[0], flat[1], -C1, flat[0], ALU.mult, ALU.add))
                link(V_.scalar_tensor_tensor(flat[0], flat[1], -C2, flat[0], ALU.mult, ALU.add))
                link(V_.tensor_scalar(flat[0], flat[0], 3.1415925, -3.1415925, ALU.min, ALU.max))
                V_.tensor_scalar(sin_b, pw_ang[:, 1, 1], 0.5, None, ALU.mult).then_inc(s5_v, 1)
                dve.wait_ge(s5_a, 1)
                for c in range(2):
                    last = V_.tensor_tensor(pw[:, c], pw_mag, pw_ang[:, c], ALU.mult)
                link(last)
                for k in range(SUB):
                    V_.tensor_copy(pw_back[:, :, SUB - 1 - k, :], pw[:, :, k, :])
                link(V_.tensor_copy(a8, pw[:, :, 8, :]))
                th, ex1, s2, re, im, den, t1, t2 = sc[:8]
                link(V_.tensor_scalar(t1, th, -1.0, 1.0, ALU.mult, ALU.add))
                link(V_.reciprocal(t1, t1))
                link(V_.scalar_tensor_tensor(ex1, th, 2.0, t1, ALU.mult, ALU.mult))
                link(V_.tensor_tensor(s2, sin_b, sin_b, ALU.mult))
                link(V_.tensor_tensor(s2, s2, pw_mag[:, 1], ALU.mult))
                link(V_.scalar_tensor_tensor(re, s2, -2.0, ex1, ALU.mult, ALU.add))
                link(V_.tensor_copy(im, pw[:, 1, 1]))
                link(V_.tensor_tensor(t1, lam[:, 0], lam[:, 0], ALU.mult))
                link(V_.tensor_tensor(t2, lam[:, 1], lam[:, 1], ALU.mult))
                link(V_.tensor_tensor(den, t1, t2, ALU.add))
                link(V_.reciprocal(den, den))
                fr, fi, t3, t4 = sc[8:12]
                link(V_.tensor_tensor(t1, re, lam[:, 0], ALU.mult))
                link(V_.tensor_tensor(t2, im, lam[:, 1], ALU.mult))
                link(V_.tensor_tensor(t1, t1, t2, ALU.add))
                link(V_.tensor_tensor(fr, t1, den, ALU.mult))
                link(V_.tensor_tensor(t3, im, lam[:, 0], ALU.mult))
                link(V_.tensor_tensor(t4, re, lam[:, 1], ALU.mult))
                link(V_.tensor_tensor(t3, t3, t4, ALU.subtract))
                link(V_.tensor_tensor(fi, t3, den, ALU.mult))


                def wide(v):
                    return v[:, :, None].broadcast_to((P, PAIRS, GC))
                link(table_product(V_, link, Bb[:, 0], wide(fr), wide(fi), B_raw[:, 0], B_raw[:, 1], tb, True))
                table_product(V_, link, Bb[:, 1], wide(fr), wide(fi), B_raw[:, 1], B_raw[:, 0], tb, False).then_inc(bb_ready, 1)
                dve.wait_ge(bb_ready, 1)

            def s5_kernel_blocks(j):
                for i in range(2):
                    dve.wait_ge(kd_done, 2 * j + i + 1)
                    if i == 0 and j:
                        dve.wait_ge(kd_stored, 16 * j)
                    kd_piece = KD[:, 4 * i:4 * i + 4]
                    link(V_.tensor_copy(kd_piece, four(banks[4 + i])[0:2 * GC]))
                    p0 = PIECE * j + 4 * i
                    link(V_.tensor_tensor(skip, mat(C_EYE)[0:2 * GC, None, 0:GC].broadcast_to((2 * GC, 4, GC)),
                                          d_col[:, p0:p0 + 4, None].broadcast_to((2 * GC, 4, GC)), ALU.mult))
                    V_.tensor_tensor(kd_piece[:, :, 0:GC], kd_piece[:, :, 0:GC], skip, ALU.add).then_inc(kd_ready, 1)

            for m in range(FC * FF_CHUNKS):
                c = m // FC
                dve.wait_ge(sil_done, m + 1)
                dve.wait_ge(up_done, 2 * m + 2)
                if c >= 2:
                    dve.wait_ge(down_done, c - 1)
                V_.tensor_tensor(hT[:, c % 2, m % FC], hsil[:, m % 2], banks[6 + m % 2][:, 0:SEQ], ALU.mult).then_inc(h_done, 1)
                if m % FC == FC - 1:
                    if c == S5_PARAMS_AT:
                        s5_parameters()
                    if c + 2 in S5_PIECE_AT:
                        p0 = PIECE * S5_PIECE_AT.index(c + 2)
                        for q in range(2):
                            s5_v_table(V_, link, slice(p0 + 4 * q, p0 + 4 * q + 4), 0, t_v).then_inc(v_ready, 1)
                            dve.wait_ge(v_ready, (p0 // PIECE) * 2 + q + 1)
                    if c in S5_PIECE_AT:
                        s5_kernel_blocks(S5_PIECE_AT.index(c))
            layer_norm(from_banks(4), ALPHA, 1)
            take_xT()
            link(V_.tensor_copy(p8[:, :, 0], a8))
            for n in (1, 2, 4):
                by = slice(n - 1, n)
                re, im, t0, t1 = p8[:, 0, 0:n], p8[:, 1, 0:n], carry[:, 0:n, 0], ebuf[:, 0:n, 0]
                bre, bim = (p8[:, i, by].broadcast_to((P, n, PAIRS)) for i in range(2))
                link(V_.tensor_tensor(t0, im, bim, ALU.mult))
                link(V_.tensor_tensor(t1, re, bre, ALU.mult))
                link(V_.tensor_tensor(p8[:, 0, n:2 * n], t1, t0, ALU.subtract))
                link(V_.tensor_tensor(t0, im, bre, ALU.mult))
                link(V_.tensor_tensor(t1, re, bim, ALU.mult))
                link(V_.tensor_tensor(p8[:, 1, n:2 * n], t1, t0, ALU.add))
            for i in range(4):
                dve.wait_ge(y_done, 8 + i + 1)
                V_.tensor_copy(u_tok[:, i // 2, 512 * (i % 2):512 * (i % 2) + 512], banks[i][:, :]).then_inc(u_sb, 1)
            dve.wait_ge(un_loaded, 32)
            V_.tensor_copy(u_r.rearrange("p a (s c) -> p a s c", c=GC), u_n.rearrange("p s (a c) -> p a s c", c=GC)).then_inc(ur_ready, 1)
            for j in range(4):
                dve.wait_ge(u_tr, j + 1)
                V_.tensor_copy(U[:, 8 * j:8 * j + 8].rearrange("p a b c -> p (a b c)"), banks[4 + j][:, :]).then_inc(u_ready, 1)
            for j in range(NPIECE):
                for ri in range(2):
                    dve.wait_ge(e_done, 2 * j + ri + 1)
                    src = banks[(2 * j + ri) % 4][:, :].rearrange("p (a b c) -> p a b c", a=8, b=2)
                    for gh in range(2):
                        half = slice(64 * gh, 64 * gh + 64)
                        last = V_.tensor_copy(E[half, ri, 8 * j:8 * j + 8], src[half, :, gh])
                    last.then_inc(e_read, 1)
            dve.wait_ge(e_read, 8)
            Hb = H.rearrange("p (b i) r a -> p b i r a", i=8)
            Eb = E.rearrange("p r a (b i) -> p b r a i", i=8)

            def advance(dst, h, power_re, power_im, e, t0, t1):
                V_.tensor_tensor(t0, h, power_re, ALU.mult)
                link(V_.tensor_tensor(t1, h, power_im, ALU.mult))
                link(V_.tensor_tensor(t0, t0, e, ALU.add))
                V_.tensor_tensor(dst[:, :, 0], t0[:, :, 0], t1[:, :, 1], ALU.subtract)
                link(V_.tensor_tensor(dst[:, :, 1], t0[:, :, 1], t1[:, :, 0], ALU.add))

            def power(i, n):
                return (p8[:, c, None, i:i + 1].broadcast_to((P, n, 2, PAIRS)) for c in range(2))

            link(V_.memset(Hb[:, :, 0], 0.0))
            link(V_.memset(carry[:, 0:1], 0.0))
            p_re, p_im = power(0, 4)
            for i in range(7):
                advance(Hb[:, :, i + 1], Hb[:, :, i], p_re, p_im, Eb[:, :, :, :, i], ht[0], ht[1])
            ends = ebuf
            advance(ends, Hb[:, :, 7], p_re, p_im, Eb[:, :, :, :, 7], ht[0], ht[1])
            p_re, p_im = power(7, 1)
            for b in range(3):
                advance(carry[:, b + 1:b + 2], carry[:, b:b + 1], p_re, p_im, ends[:, b:b + 1], ht[0][:, 0:1], ht[1][:, 0:1])
            for ri in range(2):
                def pk(c):
                    return p8[:, c, None, 0:7].broadcast_to((P, 3, 7, PAIRS))

                def cb(c):
                    return carry[:, 1:4, c, None, :].broadcast_to((P, 3, 7, PAIRS))
                dst = Hb[:, 1:4, 1:8, ri]
                V_.tensor_tensor(hc[0], pk(0), cb(ri), ALU.mult)
                link(V_.tensor_tensor(hc[1], pk(1), cb(1 - ri), ALU.mult))
                link(V_.tensor_tensor(hc[0], hc[0], hc[1], ALU.subtract if ri == 0 else ALU.add))
                link(V_.tensor_tensor(dst, dst, hc[0], ALU.add))
            link(V_.tensor_copy(Hb[:, 1:4, 0], carry[:, 1:4]))
            dve.wait_ge(hbd_zero, 1)
            for ri in range(2):
                for gh in range(2):
                    half = slice(64 * gh, 64 * gh + 64)
                    V_.tensor_copy(Hbd[half, ri, :, gh], H[half, :, ri].rearrange("p n a -> p a n")).then_inc(h_bd, 1)
            for j in range(NPIECE):
                if j >= 2:
                    dve.wait_ge(yt_done, 2 * (j - 1))
                for i in range(2):
                    dve.wait_ge(ys_done, 2 * j + i + 1)
                    src = banks[i][0:64, :].rearrange("p (a s c) -> p s a c", a=4, s=SUB)
                    dst = y_sb[:, j % 2].rearrange("p s (a c) -> p s a c", c=GC)[:, :, 4 * i:4 * i + 4, :]
                    V_.tensor_copy(dst, src).then_inc(ys_read, 1)
            for hf in range(2):
                for n in range(NT):
                    i = 2 * hf + n
                    dve.wait_ge(sig_done, i + 1)
                    s = gsig[:, n, 512 * hf:512 * hf + 512]
                    V_.tensor_tensor(s, banks[i][:, :], s, ALU.mult).then_inc(glu_read, 1)
            dve.wait_ge(glu_read, 4)
            layer_norm(lambda n, hf: gsig[:, n, 512 * hf:512 * hf + 512], ALPHA, 2)
            take_xT()

            for n in range(NT):
                dve.wait_ge(route_done, n + 1)
                link(V_.tensor_tensor(logits[:, n], banks[n][:, 0:8], router_b, ALU.add))
                link(V_.max(top[:, n], logits[:, n]))
                link(V_.tensor_scalar(gate[:, n], logits[:, n], top[:, n, 0:1], None, ALU.subtract))
                V_.tensor_tensor(etop[:, n, 0:1], top[:, n, 1:2], top[:, n, 0:1], ALU.subtract).then_inc(route_read, 1)
            dve.wait_ge(route_a, 1)
            for n in range(NT):
                lg = logits[:, n]
                mine = lg[:, :, None].broadcast_to((P, 8, 8))
                other = lg[:, None, :].broadcast_to((P, 8, 8))
                ca, cb = (t.rearrange("p (a b) -> p a b", a=8) for t in (cmp_a, cmp_b))
                link(V_.tensor_tensor(ca, other, mine, ALU.is_equal))
                link(V_.tensor_tensor(ca, ca, mat(C_EYE)[:, 32:96].rearrange("p (a b) -> p a b", a=8), ALU.mult))
                link(V_.tensor_tensor(cb, other, mine, ALU.is_gt))
                link(V_.tensor_tensor(ca, ca, cb, ALU.add))
                link(V_.tensor_reduce(rank, ca, AX, ALU.add))
                link(V_.tensor_scalar(rank, rank, 2.0, None, ALU.is_lt))
                link(V_.tensor_scalar(etop[:, n, 1:2], etop[:, n, 1:2], 1.0, None, ALU.add))
                link(V_.reciprocal(etop[:, n, 1:2], etop[:, n, 1:2]))
                link(V_.tensor_copy(chosen[:, n], rank))
                link(V_.tensor_tensor(gate[:, n], gate[:, n], rank, ALU.mult))
                link(V_.tensor_scalar(gate[:, n], gate[:, n], etop[:, n, 1:2], None, ALU.mult))
            link(V_.memset(place, -1.0))
            link(V_.memset(gates, 0.0))
            for t in range(2):
                last = V_.tensor_copy(gates[:, :, EXPERTS * t:EXPERTS * t + EXPERTS], gate)
            last.then_inc(chosen_ready, 1)
            dve.wait_ge(place_done, 1)
            for n in range(NT):
                link(V_.tensor_tensor(place[:, n, 0:EXPERTS], banks[n][:, 0:EXPERTS], chosen[:, n], ALU.mult))
            link(V_.tensor_scalar(place[:, :, EXPERTS:2 * EXPERTS], place[:, :, 0:EXPERTS], -1.0 - P, None, ALU.add))
            link(V_.tensor_scalar(place[:, :, 0:EXPERTS], place[:, :, 0:EXPERTS], -1.0, None, ALU.add))
            link(V_.tensor_reduce(passes_f, banks[2][:, 0:EXPERTS], AX, ALU.max))
            link(V_.tensor_scalar(passes_f, passes_f, float(P), 1.0, ALU.is_gt, ALU.add))
            V_.tensor_copy(passes[:, :], passes_f).then_inc(passes_ready, 1)

            def picks(dst, k, scaled, signal):
                for n in range(NT):
                    at = place[:, n, bass.ds(k, 1)]
                    if scaled:
                        last = V_.tensor_scalar(dst[:, n], mat(C_IOTA), at, gates[:, n, bass.ds(k, 1)], ALU.is_equal, ALU.mult)
                    else:
                        last = V_.tensor_scalar(dst[:, n], mat(C_IOTA), at, None, ALU.is_equal)
                last.then_inc(signal, 1)

            def take_tokens(k):
                for i in range(2):
                    dve.wait_ge(gath_done, k * 2 + i + 1)
                    V_.tensor_copy(xg[:, 4 * i:4 * i + 4], four(banks[6 + i])).then_inc(xg_ready, 1)

            dve.wait_ge(passes_ready, 1)
            link(V_.memset(macc, 0.0))
            picks(pick, 0, False, pick_ready)
            picks(pick_g, 0, True, pickg_ready)
            take_tokens(0)
            n_pass = dve.value_load(passes[0:1, 0:1], min_val=1, max_val=2)
            with dve.Fori(0, n_pass * EXPERTS) as k:
                dve.wait_ge(gath_done, k * 2 + 2)
                picks(pick, k + 1, False, pick_ready)
                for c in range(EC):
                    dve.wait_ge(m_sil, k * EC + c + 1)
                    dve.wait_ge(m_up, k * 2 * EC + 2 * EC + 2 * c + 2)
                    if c == 0:
                        dve.wait_ge(m_tr, k * 4 + 4)
                    V_.tensor_tensor(mh[:, EW1 * c:EW1 * c + EW1], msil[:, c % 2], banks[2 + c % 2][:, 0:EW1], ALU.mult).then_inc(m_h, 1)
                dve.wait_ge(m_tr, k * 4 + 5)
                picks(pick_g, k + 1, True, pickg_ready)
                take_tokens(k + 1)
                for n in range(NT):
                    for hf in range(2):
                        dve.wait_ge(m_sc, k * 4 + 2 * n + hf + 1)
                        a = macc[:, n, 512 * hf:512 * hf + 512]
                        V_.tensor_tensor(a, banks[(2 if n == 0 else 6) + hf][:, :], a, ALU.add).then_inc(m_acc, 1)
            link(V_.memset(scratch1, 0.0))
            layer_norm(lambda n, hf: macc[:, n, 512 * hf:512 * hf + 512], ALPHA, 3)

            def rms_norm(dst, slot, n_loads, final=False):
                done[0] += 1
                dve.wait_ge(std_ready, done[0])
                link(V_.reciprocal(rstd, rstd))
                dve.wait_ge(normw_loaded, 16 * n_loads)
                for n in range(NT):
                    last = V_.scalar_tensor_tensor(dst[:, n], xres[:, n], rstd[:, n:n + 1], norm_w[:, slot], ALU.mult, ALU.mult)
                last.then_inc(norm_done, 1)

            rms_norm(h2n, 0, 10)
            take_xT()
            for n in range(NT):
                dve.wait_ge(p_done, n + 1)
                V_.tensor_copy(u2[:, n], banks[n][:, :]).then_inc(p_read_v, 1)
            for m in range(4):
                dve.wait_ge(p_done, 6 + m + 1)
                V_.tensor_copy(k2[:, m], banks[m][:, 0:SEQ]).then_inc(p_read_v, 1)
            for n in range(NT):
                dve.wait_ge(p_done, 10 + n + 1)
                V_.tensor_copy(v2[:, n], banks[4 + n][:, :]).then_inc(p_read_v, 1)
            for gi in range(4):
                dve.wait_ge(pool_done, gi + 1)
                V_.tensor_copy(poolT[:, gi], banks[6 + gi % 2][:, 0:SEQ]).then_inc(pool_read, 1)
            for gi in range(4):
                dve.wait_ge(mix_done, gi + 1)
                V_.tensor_scalar(catT[:, gi], banks[6 + gi % 2][:, 0:SEQ], vecT[:, 97 + gi:98 + gi], None, ALU.mult).then_inc(mix_read, 1)
            for hp in range(4):
                for n in range(NT):
                    i = 2 * hp + n
                    dve.wait_ge(sc_done, i + 1)
                    if i:
                        dve.wait_ge(exp_done, 2 * i)
                        dve.wait_ge(pn_ready, i)
                    for e in range(2):
                        last = V_.tensor_reduce(nmax[:, e:e + 1], banks[2 * n + e][:, 0:SEQ], AX, ALU.max)
                    link(last)
                    V_.tensor_scalar(nmax, nmax, -1.0, None, ALU.mult).then_inc(max_ready, 1)
                    dve.wait_ge(exp_done, 2 * i + 2)
                    link(V_.reciprocal(psum_p, psum_p))
                    V_.tensor_tensor(prob[:, n], prob[:, n], psum_p[:, :, None].broadcast_to((P, 2, SEQ)), ALU.mult).then_inc(pn_ready, 1)
                for kt in range(2):
                    dve.wait_ge(pt_done, 2 * hp + kt + 1)
                    if hp and kt == 0:
                        dve.wait_ge(pv_done, hp)
                    V_.tensor_copy(probT[:, kt].rearrange("p a b -> p (a b)"), banks[4 + kt][:, :]).then_inc(pt_read, 1)
                dve.wait_ge(pv_done, hp + 1)
                V_.tensor_copy(catT[:, 4 + hp], banks[6][:, 0:SEQ]).then_inc(pv_read, 1)
            for n in range(NT):
                for hf in range(2):
                    dve.wait_ge(y2_done, 2 * n + hf + 1)
                    r = xres[:, n, 512 * hf:512 * hf + 512]
                    last = V_.tensor_tensor(r, banks[2 * n + hf][:, :], r, ALU.add)
            last.then_inc(var_ready, 1)
            rms_norm(h2n, 1, 10)
            take_xT()
            for i in range(32):
                dve.wait_ge(relu_done, i + 1)
                if i >= 8:
                    dve.wait_ge(down2_done, i // 4 - 1)
                t = mT[:, (i // 4) % 2, i % 4]
                V_.tensor_tensor(t, t, t, ALU.mult).then_inc(sqr_done, 1)
            dve.wait_ge(down2_done, 8)
            for n in range(NT):
                for hf in range(2):
                    r = xres[:, n, 512 * hf:512 * hf + 512]
                    last = V_.tensor_tensor(r, banks[2 * n + hf][:, :], r, ALU.add)
            last.then_inc(var_ready, 1)
            rms_norm(xres, 0, 11)

        @block.scalar
        def _(act):
            A_ = nc.scalar.activation
            count = [0]

            def link(ins):
                count[0] += 1
                ins.then_inc(chain_a, 1)
                act.wait_ge(chain_a, count[0])

            seen_xt = [0]

            def take_xT():
                for j in (1, 3):
                    act.wait_ge(xt_tr, 4 * seen_xt[0] + j + 1)
                    nc.scalar.copy(xT[:, 4:8, P * (j // 2):P * (j // 2) + P], four(banks[4 + j])).then_inc(xt_a, 1)
                seen_xt[0] += 1

            act.wait_ge(ready, 1)
            take_xT()
            act.wait_ge(ba_v, 1)
            link(A_(tmp_b, tmp_a, ACT.Abs, bias=zero_c))
            link(A_(tmp_b, tmp_b, ACT.Exp, bias=zero_c, scale=-1.0))
            A_(a_log, a_log, ACT.Exp, bias=zero_c).then_inc(ba_a, 1)
            A_(tmp_b, tmp_b, ACT.Ln, bias=one_c).then_inc(ba_a, 1)
            link(A_(beta, ba[:, :, 0:8], ACT.Sigmoid, bias=zero_c))
            for b in range(8):
                for m in range(4 * b, 4 * b + 4):
                    act.wait_ge(in_tile, m + 1)
                    if b < 6:
                        nc.scalar.copy(pre[:, m, CONV - 1:], banks[m % 8][:, 0:SEQ]).then_inc(pre_ready, 1)
                    else:
                        A_(zT[:, m - QKV_T], banks[m % 8][:, 0:SEQ], ACT.Silu, bias=zero_c).then_inc(pre_ready, 1)
                if 1 <= b <= 6:
                    act.wait_ge(conv_done, b)
                    t = qkvT[:, 4 * (b - 1):4 * b].rearrange("p a b -> p (a b)")
                    A_(t, t, ACT.Silu, bias=zero_c).then_inc(silu_done, 1)
            for i in range(8):
                act.wait_ge(ss_ready, i + 1)
                if i >= 2:
                    act.wait_ge(unit_ready, i - 1)
                A_(rs[:, i % 2, :], banks[i % 3][:, :], ACT.Sqrt, bias=eps_rms).then_inc(nrm_ready, 1)
            for j in range(4):
                act.wait_ge(dec_v, j + 1)
                for t, s in ((decL, -1.0), (decT, 1.0)):
                    v = t[:, 4 * j:4 * j + 4].rearrange("p a b -> p (a b)")
                    A_(v, v, ACT.Exp, bias=zero_c, scale=s).then_inc(dec_a, 1)
            for j in range(2):
                A_(e_row[:, 4 * j:4 * j + 4].rearrange("p a b -> p (a b)"), banks[6 + j][:, :], ACT.Exp, bias=zero_c).then_inc(dec_a, 1)
            A_(neg_eg, gc[:, 1], ACT.Exp, bias=zero_c).then_inc(dec_a, 1)
            act.wait_ge(gc_ready, 1)
            A_(kdf, tmp_a[:, 0], ACT.Exp, bias=zero_c).then_inc(dec_a, 1)
            act.wait_ge(rec_ev, 12)
            for b in range(16):
                act.wait_ge(rec_ev, 12)
                last = A_(vn[:, b // 8, b % 8], o[:, b], ACT.Square, bias=zero_c, accum_out=o_ss[:, b:b + 1])
            link(last)
            A_(o_ss, o_ss, ACT.Sqrt, bias=eps_rms, scale=1.0 / DK).then_inc(o_std, 1)

            norms = [0]

            def std(eps):
                norms[0] += 1
                act.wait_ge(var_ready, norms[0])
                A_(rstd, mv[:, :, 1], ACT.Sqrt, bias=eps).then_inc(std_ready, 1)

            std(eps_ln)
            take_xT()

            for m in range(FC * FF_CHUNKS):
                c = m // FC
                act.wait_ge(up_done, 2 * m + 1)
                if m >= 2:
                    act.wait_ge(h_done, m - 1)
                A_(hsil[:, m % 2], banks[4 + m % 2][:, 0:SEQ], ACT.Silu, bias=zero_c).then_inc(sil_done, 1)
                if m % FC < FC - 1:
                    continue
                if c == S5_PARAMS_AT:
                    act.wait_ge(s5_loaded, 16 * 14)
                    A_(dts, dts, ACT.Exp, bias=zero_c).then_inc(s5_in, 1)
                    act.wait_ge(s5_v, 1)
                    A_(pw_mag, pw_mag, ACT.Exp, bias=zero_c)
                    A_(sc[0], z[:, 0], ACT.Tanh, bias=zero_c, scale=0.5)
                    A_(pw_ang, pw_ang, ACT.Sin, bias=zero_c)
                    A_(sin_b, sin_b, ACT.Sin, bias=zero_c).then_inc(s5_a, 1)
                if c in S5_PIECE_AT:
                    j = S5_PIECE_AT.index(c)
                    if j == 0:
                        act.wait_ge(kz_stored, 64)
                        act.wait_ge(bb_ready, 1)
                    for i in range(4):
                        act.wait_ge(w_tr, 4 * j + i + 1)
                        ri, h4 = i // 2, i % 2
                        nc.scalar.copy(W1T[:, ri, PIECE * j + 4 * h4:PIECE * j + 4 * h4 + 4], four(banks[4 + i])).then_inc(w_in, 1)
                    act.wait_ge(kd_ready, 2 * (j + 1))
                    act.dma_start(k_dram[:, PIECE * j:PIECE * (j + 1), P:2 * P], KD).then_inc(kd_stored, 16)
            std(eps_ln)
            take_xT()
            for j in range(NPIECE):
                for q in range(2):
                    act.wait_ge(yt_done, 2 * j + q + 1)
                    src = banks[4 + (2 * j + q) % 4][:, 0:256].rearrange("p (s g n) -> p g n s", s=4, g=2)
                    for gh in range(2):
                        dst = hidT[:, j + 4 * gh].rearrange("p (n s) -> p n s", s=SUB)[:, :, 4 * q:4 * q + 4]
                        A_(dst, src[:, gh], ACT.Gelu, bias=zero_c).then_inc(hid_ready, 1)
            for hf in range(2):
                for n in range(NT):
                    i = 2 * hf + n
                    act.wait_ge(glu_done, 4 * hf + 2 * n + 2)
                    A_(gsig[:, n, 512 * hf:512 * hf + 512], banks[4 + i][:, :], ACT.Sigmoid, bias=zero_c).then_inc(sig_done, 1)
            std(eps_ln)
            take_xT()
            act.wait_ge(route_read, 2)
            A_(gate, gate, ACT.Exp, bias=zero_c)
            A_(etop[:, :, 1], etop[:, :, 0], ACT.Exp, bias=zero_c).then_inc(route_a, 1)
            act.wait_ge(passes_ready, 1)
            n_pass = act.value_load(passes[0:1, 0:1], min_val=1, max_val=2)
            with act.Fori(0, n_pass * EXPERTS) as k:
                def silu_of(c):
                    act.wait_ge(m_up, k * 2 * EC + 2 * EC + 2 * c + 1)
                    if c >= 2:
                        act.wait_ge(m_h, k * EC + c - 1)
                    elif c == 0:
                        act.wait_ge(pickg_ready, k + 1)
                    A_(msil[:, c % 2], banks[c % 2][:, 0:EW1], ACT.Silu, bias=zero_c).then_inc(m_sil, 1)

                def take_hT(t):
                    act.wait_ge(m_tr, k * 4 + t + 5)
                    if t == 0:
                        nc.scalar.copy(spread.rearrange("p a b -> p (a b)"), banks[4][:, 2 * P:4 * P])
                        nc.scalar.copy(mhT[:, 0:2].rearrange("p a b -> p (a b)"), banks[4][:, 0:2 * P]).then_inc(m_hT, 1)
                    else:
                        m = 3 * t - 1
                        nc.scalar.copy(mhT[:, m:m + 3].rearrange("p a b -> p (a b)"), banks[4 + t % 2][:, 0:3 * P]).then_inc(m_hT, 1)

                silu_of(0)
                silu_of(1)
                take_hT(0)
                silu_of(2)
                take_hT(1)
                silu_of(3)
                take_hT(2)
                take_hT(3)
                for hf in range(2):
                    act.wait_ge(m_y, k * EC + EC + 2 * hf + 2)
                    nc.scalar.copy(ysb[:, 512 * hf:512 * hf + 512], banks[hf][:, :]).then_inc(m_yread, 1)
            std(eps_ln)

            def mean_square():
                for n in range(NT):
                    link(A_(region(39936, 1024), xres[:, n], ACT.Square, bias=zero_c, accum_out=mv[:, n, 1:2]))
                A_(rstd, mv[:, :, 1], ACT.Sqrt, bias=eps_rms, scale=1.0 / DM).then_inc(std_ready, 1)

            act.wait_ge(norm_done, 4)
            mean_square()
            take_xT()
            for m in range(4):
                act.wait_ge(p_done, 2 + m + 1)
                A_(q2[:, m], banks[4 + m][:, 0:SEQ], ACT.Copy, scale=AD ** -0.5).then_inc(p_read_a, 1)
            for hp in range(4):
                for n in range(NT):
                    i = 2 * hp + n
                    act.wait_ge(max_ready, i + 1)
                    if hp:
                        act.wait_ge(pt_done, 2 * hp)
                    for e in range(2):
                        A_(prob[:, n, e], banks[2 * n + e][:, 0:SEQ], ACT.Exp, bias=nmax[:, e:e + 1],
                           accum_out=psum_p[:, e:e + 1]).then_inc(exp_done, 1)
            act.wait_ge(var_ready, 5)
            mean_square()
            take_xT()
            for i in range(32):
                act.wait_ge(up2_done, i + 1)
                if i >= 8:
                    act.wait_ge(down2_done, i // 4 - 1)
                A_(mT[:, (i // 4) % 2, i % 4], banks[4 + i % 4][:, 0:SEQ], ACT.Relu, bias=zero_c).then_inc(relu_done, 1)
            act.wait_ge(var_ready, 6)
            mean_square()

        @block.tensor
        def _(pe):
            mm = nc.tensor.matmul

            def transpose(dst, src):
                k = src.shape[0]
                if dst.shape[0] < P:
                    return mm(dst, src, const[0:k, C_ID, 0:k], start=True, stop=True)
                return nc.tensor.transpose(dst, src, const[0:k, C_ID, 0:k])

            made_xt = [0]

            def make_xT(src):
                for j in range(4):
                    for i in range(4):
                        c = 4 * (j % 2) + i
                        last = transpose(four(banks[4 + j])[:, i], src[:, j // 2, P * c:P * c + P])
                    last.then_inc(xt_tr, 1)
                made_xt[0] += 1

            def need_xT():
                pe.wait_ge(xt_v, 2 * made_xt[0])
                pe.wait_ge(xt_a, 2 * made_xt[0])

            def t_form(bank, w, m, x=xT):
                for k in range(KT):
                    last = mm(bank[:, 0:SEQ], w[:, k, P * m:P * m + P], x[:, k, :], start=(k == 0), stop=(k == KT - 1))
                return last

            def token_major(bank, x, w, n, k0=0, total=KT):
                nk = w.shape[1]
                for k in range(nk):
                    last = mm(bank, x[:, k0 + k, P * n:P * n + P], w[:, k], start=(k0 + k == 0), stop=(k0 + k == total - 1))
                return last

            pe.wait_ge(const_loaded, 16)
            pe.wait_ge(vecs_loaded, 48)
            transpose(banks[3][:, 0:101], vrows).then_inc(vec_tr, 1)
            pe.wait_ge(x_loaded, 16)
            make_xT(xres)
            need_xT()
            w_ba = region(38984, KT, 16)
            pe.wait_ge(ba_w_loaded, 16)
            for n in range(NT):
                last = token_major(banks[6 + n][:, 0:16], xT, w_ba, n)
            last.then_inc(ba_done, 1)
            for m in range(32):
                b = m // 4
                if m % 4 == 0:
                    arrived(pe, ("gdn_in", b))
                if m in (6, 7):
                    pe.wait_ge(ba_v, 1)
                if m == 3:
                    pe.wait_ge(vec_ok, 1)
                if m >= 8:
                    pe.wait_ge(pre_ready, m - 7)
                t_form(banks[m % 8], region(4096 * (b % 4), KT, 512), m % 4).then_inc(in_tile, 1)
            pe.wait_ge(pre_ready, 32)
            for i in range(8):
                pe.wait_ge(sq_ready, i + 1)
                if i >= 3:
                    pe.wait_ge(nrm_ready, i - 2)
                mm(banks[i % 3][:, :], mat(C_ONE), sq[:, i % 2, :], start=True, stop=True).then_inc(ss_ready, 1)
            pe.wait_ge(g_ready, 1)
            mm(banks[3][:, 0:16], mat(C_TRI), g.rearrange("p a b -> p (a b)"), start=True, stop=True).then_inc(grow_done, 1)
            for j in range(4):
                for b in range(4 * j, 4 * j + 4):
                    gcol = g.rearrange("p a b -> p (a b)")[:, b:b + 1]
                    last = mm(four(banks[4 + j])[:, b % 4], gcol.broadcast_to((P, P)), mat(C_TRI), start=True, stop=True)
                last.then_inc(grow_done, 1)
            pe.wait_ge(unit_ready, 8)
            for j in range(4):
                if j == 0:
                    pe.wait_ge(nrm_ready, 8)
                    pe.wait_ge(dec_v, 1)
                if j >= 2:
                    pe.wait_ge(kq_read, j - 1)
                for b in range(4 * j, 4 * j + 4):
                    n, h = b // 8, b % 8
                    kt, qt = (qkvT[:, t + h, P * n:P * n + P] for t in (8, 0))
                    mm(four(banks[j % 2])[:, b % 4], kt, kt, start=True, stop=True)
                    last = mm(four(banks[2 + j % 2])[:, b % 4], kt, qt, start=True, stop=True)
                last.then_inc(kq_done, 1)
            pe.wait_ge(dec_a, 12)
            for j in range(4):
                pe.wait_ge(kq_read, j + 1)
                for b in range(4 * j, 4 * j + 4):
                    last = transpose(four(banks[4 + j])[:, b % 4], D[:, b])
                last.then_inc(d_tr, 1)

            def level_q(lv, j):
                i = 4 * (lv - 1) + j
                if lv == 1:
                    pe.wait_ge(d_evac, 4)
                else:
                    pe.wait_ge(lv_pe, 8 * (lv - 2) + 2 * (j + 1))
                if i >= 2:
                    pe.wait_ge(lv_qe, i - 1)
                for b in range(4 * j, 4 * j + 4):
                    last = mm(four(banks[j % 2])[:, b % 4], decL[:, b], DT[:, b], start=True, stop=True)
                last.then_inc(lv_q, 1)

            def level_p(lv, j):
                i = 4 * (lv - 1) + j
                pe.wait_ge(lv_qe, i + 1)
                if i >= 2:
                    prev = i - 2
                    pe.wait_ge(lv_pe, 2 * (prev + 1) if prev < 20 else 40 + prev - 19)
                for b in range(4 * j, 4 * j + 4):
                    last = mm(four(banks[2 + j % 2])[:, b % 4], D[:, b], QT[:, b], start=True, stop=True)
                    if lv < LEVELS - 1:
                        last = mm(four(banks[4 + j % 2])[:, b % 4], QT[:, b], D[:, b], start=True, stop=True)
                last.then_inc(lv_p, 1)

            for lv in range(1, LEVELS):
                level_q(lv, 0)
                for j in range(4):
                    if j < 3:
                        level_q(lv, j + 1)
                    level_p(lv, j)
            pe.wait_ge(lv_pe, 44)
            for j in range(4):
                for b in range(4 * j, 4 * j + 4):
                    last = transpose(four(banks[j])[:, b % 4], qkvT[:, 16 + b % 8, P * (b // 8):P * (b // 8) + P])
                last.then_inc(vk_tr, 1)
            for j in range(2):
                for h in range(4 * j, 4 * j + 4):
                    last = transpose(four(banks[4 + j])[:, h % 4], qkvT[:, 8 + h, 0:P])
                last.then_inc(vk_tr, 1)
            def each(j, bank, pairs, sem_=rec):
                for h in range(4 * j, 4 * j + 4):
                    terms = pairs(h)
                    for t, (lhsT, rhs) in enumerate(terms):
                        last = mm(four(bank)[:, h % 4], lhsT, rhs, start=(t == 0), stop=(t == len(terms) - 1))
                last.then_inc(sem_, 1)

            for j in range(2):
                pe.wait_ge(vk_ready, 4 * (j + 1))
                each(j, banks[6 + j], lambda h: [(DT[:, h], vtok[:, h])])
            pe.wait_ge(vk_ready, 24)
            for j in range(2):
                pe.wait_ge(rec_ev, j + 1)
                each(j, banks[j], lambda h: [(kd[:, h], vn[:, 0, h])])
                each(j, banks[2 + j], lambda h: [(decT[:, h], vn[:, 0, h])])
            for j in range(2):
                pe.wait_ge(rec_ev, 3 + 2 * j)
                each(j, banks[4 + j], lambda h: [(qkvT[:, 8 + h, P:2 * P], s1[:, h])])
            for j in range(2):
                pe.wait_ge(rec_ev, 7 + j)
                each(j, banks[6 + j], lambda h: [(DT[:, 8 + h], r1[:, h])])
            for j in range(2):
                pe.wait_ge(rec_ev, 9 + j)
                each(j, banks[j], lambda h: [(e_row[:, h], s1[:, h]), (decT[:, 8 + h], vn[:, 1, h])])
            pe.wait_ge(o_norm, 1)
            for j in range(4):
                for i in range(4):
                    last = transpose(four(banks[4 + j])[:, i], o[:, 4 * j + i])
                last.then_inc(o_tr, 1)
            pe.wait_ge(o_ready, 4)
            pe.wait_ge(rec_ev, 12)
            for n in range(NT):
                for hf in range(2):
                    for c in range(2):
                        arrived(pe, ("gdn_out", c))
                        last = token_major(banks[2 * n + hf][:, :], oT, region(4096 * (2 + c), 4, DM)[:, :, 512 * hf:512 * hf + 512], n, 4 * c)
                    last.then_inc(y_done, 1)
            pe.wait_ge(norm_done, 1)
            make_xT(xres)

            def s5_transposes():
                pe.wait_ge(s5_loaded, 16 * 14)
                pe.wait_ge(h_done, FC * (S5_PARAMS_AT + 1))
                for gh, raw in enumerate((lam_raw, lam_raw2)):
                    for i in range(2):
                        transpose(banks[4][64 * gh:64 * gh + 64, PAIRS * i:PAIRS * i + PAIRS], raw[:, i])
                for i in range(2):
                    for jb in range(8):
                        half = slice(64 * (jb // 4), 64 * (jb // 4) + 64)
                        last = transpose(banks[5 + i][half, P * (jb % 4):P * (jb % 4) + P], C_raw[:, i, jb])
                last.then_inc(s5_tr, 1)
                pe.wait_ge(s5_read, 1)

            def s5_piece(j):
                pe.wait_ge(h_done, FC * (S5_PIECE_AT[j] + 1))
                pe.wait_ge(w_ready, 2 * j + 2)
                for i in range(4):
                    ri, h4 = i // 2, i % 2
                    for a in range(4):
                        last = transpose(four(banks[4 + i])[:, a], Wp[:, ri, 4 * h4 + a].rearrange("p s c -> p (s c)"))
                    last.then_inc(w_tr, 1)
                pe.wait_ge(v_ready, 2 * j + 2)
                pe.wait_ge(im_ready, j + 1)
                for i in range(2):
                    pe.wait_ge(w_in, 4 * j + i + 1)
                    for a in range(4):
                        pr = 4 * i + a
                        for ri in range(2):
                            last = mm(four(banks[4 + i])[0:2 * GC, a], Bbd[:, ri, pr], V[:, ri, PIECE * j + pr, 0:SUB].rearrange("p k c -> p (k c)"),
                                      start=(ri == 0), stop=(ri == 1))
                    last.then_inc(kd_done, 1)
                pe.wait_ge(w_in, 4 * j + 4)
                pe.wait_ge(kd_ready, 2 * j + 2)

            def swiglu_down(c):
                arrived(pe, ("ffn_w2", c))
                pe.wait_ge(h_done, FC * (c + 1))
                for n in range(NT):
                    for hf in range(2):
                        for k in range(FC):
                            last = mm(banks[2 * n + hf][:, :], hT[:, c % 2, k, P * n:P * n + P], f2[c % FF_SETS][:, k, 512 * hf:512 * hf + 512],
                                      start=(c == 0 and k == 0), stop=(c == FF_CHUNKS - 1 and k == FC - 1))
                        if c == FF_CHUNKS - 1:
                            last.then_inc(y_done, 1)
                if c < FF_CHUNKS - 1:
                    last.then_inc(down_done, 1)

            need_xT()
            for c in range(FF_CHUNKS):
                arrived(pe, ("ffn_w3", c))
                for m in range(FC * c, FC * c + FC):
                    if m >= 2:
                        pe.wait_ge(sil_done, m - 1)
                    t_form(banks[4 + m % 2], f1[c % FF_SETS], m % FC).then_inc(up_done, 1)
                    if m >= 2:
                        pe.wait_ge(h_done, m - 1)
                    t_form(banks[6 + m % 2], f3[c % FF_SETS], m % FC).then_inc(up_done, 1)
                if c:
                    swiglu_down(c - 1)
                if c == S5_PARAMS_AT:
                    s5_transposes()
                if c in S5_PIECE_AT:
                    s5_piece(S5_PIECE_AT.index(c))
            swiglu_down(FF_CHUNKS - 1)
            pe.wait_ge(norm_done, 2)
            make_xT(xres)
            need_xT()
            for n in range(NT):
                for hf in range(2):
                    for c in range(2):
                        arrived(pe, ("s5_in", c))
                        last = token_major(banks[2 * n + hf][:, :], xT, region(4096 * c, 4, DM)[:, :, 512 * hf:512 * hf + 512], n, 4 * c)
                    last.then_inc(y_done, 1)
            pe.wait_ge(ur_ready, 1)
            pe.wait_ge(w_in, 16)
            for j in range(4):
                for a in range(8):
                    last = transpose(banks[4 + j][:, 64 * a:64 * a + 64], u_r[:, 8 * j + a])
                last.then_inc(u_tr, 1)
            pe.wait_ge(u_sb, 4)
            for j in range(NPIECE):
                pe.wait_ge(u_ready, j + 1)
                for ri in range(2):
                    i = 2 * j + ri
                    if i >= 4:
                        pe.wait_ge(e_read, i - 3)
                    for a in range(8):
                        pr = 8 * j + a
                        last = mm(banks[i % 4][:, 64 * a:64 * a + 64], W1T[:, ri, pr], U[:, pr].rearrange("p a b -> p (a b)"), start=True, stop=True)
                    last.then_inc(e_done, 1)
            pe.wait_ge(e_read, 8)
            pe.wait_ge(h_bd, 4)
            pe.wait_ge(t_loaded, 16 * 16)
            pe.wait_ge(u_ready, 4)

            def y_transposes(j):
                for q in range(2):
                    pe.wait_ge(ys_read, 2 * j + 2)
                    if j >= 2:
                        pe.wait_ge(hid_ready, 4 * (j - 2) + 2 * q + 2)
                    for s in range(4):
                        last = transpose(banks[4 + (2 * j + q) % 4][:, 64 * s:64 * s + 64], y_sb[:, j % 2, 4 * q + s])
                    last.then_inc(yt_done, 1)

            for j in range(NPIECE):
                for i in range(2):
                    if j:
                        pe.wait_ge(ys_read, 2 * (j - 1) + i + 1)
                    for a in range(4):
                        pr = PIECE * j + 4 * i + a
                        dst = four(banks[i])
                        for ri in range(2):
                            mm(dst[0:64, a], Hbd[:, ri, pr].rearrange("p a b -> p (a b)"), V[:, ri, pr, 1:SUB + 1].rearrange("p k c -> p (k c)"),
                               start=(ri == 0), stop=False, skip_group_check=True)
                        for gh in range(2):
                            last = mm(dst[32 * gh:32 * gh + 32, a], U[:, pr, gh], T[:, gh, pr], start=False, stop=(gh == 1), skip_group_check=True)
                    last.then_inc(ys_done, 1)
                if j:
                    y_transposes(j - 1)
            y_transposes(NPIECE - 1)
            pe.wait_ge(hid_ready, 16)
            pe.wait_ge(ys_read, 8)
            for hf in range(2):
                for n in range(NT):
                    for c in range(2):
                        arrived(pe, ("glu", 2 * hf + c))
                        token_major(banks[4 * c + 2 * hf + n][:, :], hidT, glu[2 * hf + c], n).then_inc(glu_done, 1)
            for counter, n in ((m_up, 2 * EC), (m_y, EC), (m_tr, 4), (m_yread, 2), (m_acc, 4)):
                pe.sem_inc(counter, n)
            pe.wait_ge(norm_done, 3)
            make_xT(xres)
            need_xT()
            pe.wait_ge(small_loaded, 64)
            for n in range(NT):
                token_major(banks[n][:, 0:8], xT, w_router, n).then_inc(route_done, 1)
            pe.wait_ge(route_read, 2)
            pe.wait_ge(chosen_ready, 1)
            mm(banks[0][:, 0:EXPERTS], mat(C_TRI), chosen[:, 0], start=True, stop=True)
            mm(banks[1][:, 0:EXPERTS], mat(C_TRI), chosen[:, 1], start=True, stop=False)
            mm(banks[1][:, 0:EXPERTS], mat(C_ONE), chosen[:, 0], start=False, stop=True)
            mm(banks[2][:, 0:EXPERTS], mat(C_ONE), chosen[:, 0], start=True, stop=False)
            mm(banks[2][:, 0:EXPERTS], mat(C_ONE), chosen[:, 1], start=False, stop=True).then_inc(place_done, 1)
            pe.wait_ge(passes_ready, 1)

            def gather(k):
                pe.wait_ge(pick_ready, k + 1)
                for i in range(2):
                    for c in range(4):
                        for n in range(NT):
                            last = mm(four(banks[6 + i])[:, c], xres[:, n, P * (4 * i + c):P * (4 * i + c) + P], pick[:, n],
                                      start=(n == 0), stop=(n == 1))
                    last.then_inc(gath_done, 1)

            gather(0)
            n_pass = pe.value_load(passes[0:1, 0:1], min_val=1, max_val=2)
            with pe.Fori(0, n_pass * EXPERTS) as k:
                def up(c):
                    pe.wait_ge(m_loaded[c], (k + 1) * 32)
                    if c >= 2:
                        pe.wait_ge(m_sil, k * EC + c - 1)
                    for kt in range(KT):
                        last = mm(banks[c % 2][:, 0:EW1], xg[:, kt], m1[c][:, kt], start=(kt == 0), stop=(kt == KT - 1))
                    last.then_inc(m_up, 1)
                    if c >= 2:
                        pe.wait_ge(m_h, k * EC + c - 1)
                    for kt in range(KT):
                        last = mm(banks[2 + c % 2][:, 0:EW1], xg[:, kt], m3[c][:, kt], start=(kt == 0), stop=(kt == KT - 1))
                    last.then_inc(m_up, 1)

                def hidden(t):
                    pe.wait_ge(m_h, k * EC + t + 1)
                    if t >= 2:
                        pe.wait_ge(m_hT, k * 4 + t - 1)
                    bank = four(banks[4 + t % 2])
                    if t == 0:
                        pe.wait_ge(pickg_ready, k + 1)
                        for n in range(NT):
                            transpose(bank[:, 2 + n], pick_g[:, n])
                        tiles = (0, 1)
                    else:
                        tiles = range(3 * t - 1, 3 * t + 2)
                    for i, m in enumerate(tiles):
                        last = transpose(bank[:, i], mh[:, P * m:P * m + P])
                    last.then_inc(m_tr, 1)

                pe.wait_ge(xg_ready, k * 2 + 2)
                pe.wait_ge(m_yread, k * 2 + 2)
                pe.wait_ge(m_acc, k * 4 + 4)
                up(0)
                up(1)
                hidden(0)
                up(2)
                hidden(1)
                up(3)
                hidden(2)
                gather(k + 1)
                hidden(3)
                pe.wait_ge(m_hT, k * 4 + 4)
                pe.wait_ge(m_sil, k * EC + 4)
                for c in range(EC):
                    pe.wait_ge(m_loaded[EC + c], (k + 1) * 16)
                    dst = banks[c // 2][:, EW2 * (c % 2):EW2 * (c % 2) + EW2]
                    for kt in range(FE_T):
                        last = mm(dst, mhT[:, kt], m2[c][:, kt], start=(kt == 0), stop=(kt == FE_T - 1))
                    last.then_inc(m_y, 1)
                pe.wait_ge(xg_ready, k * 2 + 4)
                for n in range(NT):
                    for hf in range(2):
                        pe.wait_ge(m_yread, k * 2 + hf + 3)
                        last = mm(banks[(2 if n == 0 else 6) + hf][:, :], spread[:, n], ysb[:, 512 * hf:512 * hf + 512], start=True, stop=True)
                        last.then_inc(m_sc, 1)
            pe.wait_ge(norm_done, 5)
            make_xT(h2n)
            need_xT()
            arrived(pe, ("in2", 0))
            for n in range(NT):
                token_major(banks[n][:, :], xT, region(0, KT, 512), n).then_inc(p_done, 1)
            arrived(pe, ("in2", 1))
            for m in range(4):
                t_form(banks[4 + m], region(4096, KT, 512), m).then_inc(p_done, 1)
            arrived(pe, ("in2", 2))
            for m in range(4):
                if m < 2:
                    pe.wait_ge(p_read_v, m + 1)
                t_form(banks[m], region(8192, KT, 512), m).then_inc(p_done, 1)
            arrived(pe, ("in2", 3))
            for n in range(NT):
                pe.wait_ge(p_read_a, n + 1)
                token_major(banks[4 + n][:, :], xT, region(12288, KT, 512), n).then_inc(p_done, 1)
            pe.wait_ge(b2_loaded, 16 * 19)
            pe.wait_ge(p_read_a, 4)
            for gi in range(4):
                if gi >= 2:
                    pe.wait_ge(pool_read, gi - 1)
                for n in range(NT):
                    last = mm(banks[6 + gi % 2][:, 0:SEQ], u2[:, n, P * gi:P * gi + P], poolw[:, n, gi], start=(n == 0), stop=(n == 1))
                last.then_inc(pool_done, 1)
            for gi in range(4):
                pe.wait_ge(pool_read, 3 + gi % 2 if gi < 2 else 4)
                if gi >= 2:
                    pe.wait_ge(mix_read, gi - 1)
                mm(banks[6 + gi % 2][:, 0:SEQ], wpool[:, gi], poolT[:, gi], start=True, stop=True).then_inc(mix_done, 1)
            pe.wait_ge(bias_ready, 2)
            pe.wait_ge(p_read_v, 8)
            pe.wait_ge(mix_read, 4)

            def scores(hp):
                for n in range(NT):
                    i = 2 * hp + n
                    if i >= 2:
                        pe.wait_ge(exp_done, 2 * (i - 1))
                    for e in range(2):
                        pp = slice(64 * e, 64 * e + 64)
                        mm(banks[2 * n + e][:, 0:SEQ], q2[pp, hp, P * n:P * n + P], k2[pp, hp, :], start=True, stop=False)
                    for e in range(2):
                        last = mm(banks[2 * n + e][:, 0:SEQ], mat(C_REV), bias[:, n, 2 * hp + e], start=False, stop=True)
                    last.then_inc(sc_done, 1)

            scores(0)
            for hp in range(4):
                if hp < 3:
                    scores(hp + 1)
                pe.wait_ge(pn_ready, 2 * hp + 2)
                for kt in range(2):
                    if hp:
                        pe.wait_ge(pt_read, 2 * (hp - 1) + kt + 1)
                    for n in range(NT):
                        for e in range(2):
                            last = transpose(banks[4 + kt][:, SEQ * e + P * n:SEQ * e + P * n + P], prob[:, n, e, P * kt:P * kt + P])
                    last.then_inc(pt_done, 1)
                pe.wait_ge(pt_read, 2 * hp + 2)
                if hp:
                    pe.wait_ge(pv_read, hp)
                for e in range(2):
                    for kt in range(2):
                        h = 2 * hp + e
                        last = mm(banks[6][64 * e:64 * e + 64, 0:SEQ], v2[:, kt, AD * h:AD * h + AD], probT[:, kt, e], start=(kt == 0), stop=(kt == 1))
                last.then_inc(pv_done, 1)
            pe.wait_ge(pv_read, 4)
            pe.wait_ge(exp_done, 16)
            for n in range(NT):
                for hf in range(2):
                    for c in range(2):
                        arrived(pe, ("out2", c))
                        last = token_major(banks[2 * n + hf][:, :], catT, region(4096 * (6 + c), 4, DM)[:, :, 512 * hf:512 * hf + 512], n, 4 * c)
                    last.then_inc(y2_done, 1)
            pe.wait_ge(norm_done, 6)
            make_xT(h2n)
            need_xT()
            def mlp_up(s):
                c = s % 2
                arrived(pe, ("up2", s))
                for m in range(4):
                    i = 4 * s + m
                    if i >= 4:
                        pe.wait_ge(relu_done, i - 3)
                    t_form(banks[4 + m], region(4096 * c, KT, 512), m).then_inc(up2_done, 1)

            def mlp_down(s):
                c = s % 2
                arrived(pe, ("down2", s))
                pe.wait_ge(sqr_done, 4 * s + 4)
                for n in range(NT):
                    for hf in range(2):
                        for k in range(4):
                            last = mm(banks[2 * n + hf][:, :], mT[:, s % 2, k, P * n:P * n + P],
                                      region(4096 * (2 + c), 4, DM)[:, k, 512 * hf:512 * hf + 512],
                                      start=(s == 0 and k == 0), stop=(s == 7 and k == 3))
                last.then_inc(down2_done, 1)

            mlp_up(0)
            for s in range(8):
                if s < 7:
                    mlp_up(s + 1)
                mlp_down(s)


_INS = ["x", "gdn_w_in", "gdn_conv_w", "gdn_a_log", "gdn_dt_bias", "gdn_norm_g", "gdn_w_out",
        "ffn_w1", "ffn_w3", "ffn_w2", "s5_w_in", "s5_lam_re", "s5_lam_im", "s5_log_dt", "s5_b_re",
        "s5_b_im", "s5_c_re", "s5_c_im", "s5_d", "s5_w_glu", "moe_w_router", "moe_b_router",
        "moe_w1", "moe_w3", "moe_w2", "ln_g", "ln_b", "norm_mix_g_2", "w_in_2", "w_pool_2",
        "pool_scale_2", "rpb_2", "w_out_2", "norm_mlp_g_2", "w_up_2", "w_down_2", "final_g_2"]


def kernel(**inputs):
    import concourse.bacc as bacc
    from concourse.bass_utils import run_bass_kernel_spmd

    nc = bacc.Bacc("TRN2", target_bir_lowering=False, num_devices=1)
    arrays = {name: np.ascontiguousarray(inputs[name]) for name in _INS}
    arrays["shape_const"], arrays["shape_pool"], arrays["shape_mask"] = shape_constants()
    aps = {name: nc.dram_tensor(name, a.shape, F32, kind="ExternalInput").ap() for name, a in arrays.items()}
    out = nc.dram_tensor("out", (1, SEQ, DM), F32, kind="ExternalOutput").ap()
    build(nc, aps, out)
    r = run_bass_kernel_spmd(nc, [arrays], core_ids=[0])
    return r.results[0]["out"]
```

```python
from contextlib import ExitStack

import numpy as np

import concourse.bass as bass
from concourse import mybir

P = 128
F32 = mybir.dt.float32
ALU = mybir.AluOpType
ACT = mybir.ActivationFunctionType
AX = mybir.AxisListType.X

SEQ, DM = 256, 1024
NT = SEQ // P
KT = DM // P
HEADS, DK = 8, 128
CONV = 4
QKV_T = 3 * HEADS
FE = 1408
FE_T = FE // P
FF1 = 2 * FE
FC = 2
FF_CHUNKS = FF1 // P // FC
FF_SETS = 3
S5_PARAMS_AT = 3
S5_PIECE_AT = (6, 7, 8, 9)
EC = 4
EW1, EW2 = FE // EC, DM // EC
ESLAB = KT * EW1
EXPERTS = 8
GROUPS, STATE, GC = 64, 64, 16
PAIRS = GROUPS // 2
SUB = 8
NSUB = SEQ // SUB
PIECE = 8
NPIECE = PAIRS // PIECE
POOLS = (2, 4, 8, 16)
AH, AD = 8, 64
GRID, WCOL = 64, 16
FF2 = 4096
ALPHA = 4.0 ** 0.25
LN_EPS, EPS = 1e-5, 1e-6
MASKED = -1e30

C_ID, C_TRI, C_LOW, C_ONE, C_REV, C_LV = 0, 1, 2, 3, 4, 5
LEVELS = 7
C_M0 = C_LV
C_EYE = C_LV + LEVELS
C_IOTA = C_EYE + 1
N_CONST = C_IOTA + 1


def shape_constants():
    i = np.arange(P)
    row, col = i[:, None], i[None, :]
    mats = [row == col, row <= col, row > col, np.ones((P, P)),
            (row // GRID == col // GRID) & (row % GRID == GRID - 1 - col % GRID)]
    for lv in range(LEVELS):
        low = (row >> (lv + 1) == col >> (lv + 1)) & (row >> lv & 1 == 1) & (col >> lv & 1 == 0)
        mats.append(low.T if lv else low)
    eye = np.zeros((P, P))
    eye[:2 * GC, :GC] = row[:2 * GC] % GC == col[:, :GC]
    eye[:, 16] = row[:, 0] % 8
    eye[:, 32:96] = (np.arange(8)[None, :] < np.arange(8)[:, None]).reshape(1, 64)
    mats.append(eye)
    mats.append(np.broadcast_to(col, (P, P)))
    const = np.concatenate([np.asarray(m, np.float32) for m in mats], axis=1)
    t = np.arange(SEQ)
    pool = np.zeros((SEQ, len(POOLS), SEQ), np.float32)
    for g, w in enumerate(POOLS):
        lo, hi = np.clip(t - w // 2, 0, SEQ), np.clip(t - w // 2 + w, 0, SEQ)
        inside = (t[:, None] >= lo[None]) & (t[:, None] < hi[None])
        pool[:, g] = inside / (hi - lo).astype(np.float32)[None] - (t[:, None] == t[None])
    c = GRID - 1 - np.arange(P) % GRID
    c0 = np.clip(c - WCOL // 2, 0, GRID - WCOL)[:, None]
    kc = np.arange(GRID)[None]
    mask = np.where((kc >= c0) & (kc < c0 + WCOL), 0.0, MASKED).astype(np.float32)
    return const, pool, mask


def build(nc, A, out):
    with ExitStack() as ctx:
        def sb(name, shape):
            return ctx.enter_context(nc.sbuf_tensor(name, shape, F32))

        def sem(name):
            return ctx.enter_context(nc.semaphore(name))

        xres = sb("xres", [P, NT, DM])
        xT = sb("xT", [P, KT, SEQ])
        const = sb("const", [P, N_CONST, P])
        norm_w = sb("norm_w", [P, 2, DM])
        small = sb("small", [P, 900])
        arena = sb("arena", [P, 44288])
        banks = [ctx.enter_context(nc.psum_tensor(f"bank{i}", [P, 512], F32)) for i in range(8)]

        def region(off, *dims, parts=P):
            n = int(np.prod(dims))
            ap = arena[0:parts, off:off + n]
            if len(dims) == 1:
                return ap
            names = "abcde"[:len(dims)]
            return ap.rearrange(f"p ({' '.join(names)}) -> p {' '.join(names)}",
                                **{n: d for n, d in zip(names[1:], dims[1:])})

        used = [0]

        def vec(*dims):
            n = int(np.prod(dims))
            ap = small[:, used[0]:used[0] + n]
            used[0] += n
            assert used[0] <= 900
            if len(dims) == 1:
                return ap
            names = "abcd"[:len(dims)]
            return ap.rearrange(f"p ({' '.join(names)}) -> p {' '.join(names)}",
                                **{n: d for n, d in zip(names[1:], dims[1:])})

        def mat(i):
            return const[:, i, :]

        def over(ap, n):
            return ap[:, None, :].broadcast_to((ap.shape[0], n, ap.shape[1]))

        def four(bank):
            return bank[:, :].rearrange("p (a b) -> p a b", a=4)

        ident = mat(C_ID)
        stats, mv, rstd, shift = vec(NT, 2, 6), vec(NT, 2), vec(NT), vec(NT)
        eps_ln, eps_rms, one_c, zero_c = vec(1), vec(1), vec(1), vec(1)
        vecT = vec(101)
        ba, a_log, dt_b = vec(NT, 16), vec(8), vec(8)
        beta, g, gc, tmp_a, tmp_b = vec(NT, 8), vec(NT, 8), vec(NT, 8), vec(NT, 8), vec(NT, 8)
        glast, kdf, neg_eg = vec(8), vec(8), vec(8)
        o_ss = vec(NT * HEADS)
        router_b, logits, top, gate = vec(8), vec(NT, 8), vec(NT, 8), vec(NT, 8)
        cmp_a, cmp_b, rank, etop = vec(64), vec(64), vec(8), vec(NT, 2)
        a8 = vec(2, PAIRS)
        w_router = vec(KT, 8)
        chosen = vec(NT, 8)
        place = vec(NT, 2 * EXPERTS + 1)
        gates = vec(NT, 2 * EXPERTS + 1)
        passes_f, scratch1 = vec(1), vec(1)
        passes = ctx.enter_context(nc.sbuf_tensor("passes", [P, 1], mybir.dt.int32))
        nmax, psum_p = vec(2, 2), vec(2, 2)
        d_small = vec(PAIRS)
        vrows = xT[0:101, 0, 0:128]

        pre = region(16384, QKV_T, SEQ + CONV - 1)
        qkvT = region(22600, QKV_T, SEQ)
        zT = region(28744, HEADS, SEQ)
        decT = region(30792, 16, P)
        decL = region(32840, 16, P)
        e_row = region(34888, HEADS, P)
        vn = region(35912, NT, HEADS, P)
        s1 = region(37960, HEADS, P)
        o = region(38984, NT * HEADS, P)
        sq = region(38984, 2, 512)
        rs = region(40008, 2, 512)
        r1 = region(41032, HEADS, P)
        kd = region(42056, HEADS, P)
        D, DT, QT = region(16384, 16, P), region(18432, 16, P), region(20480, 16, P)
        vtok = region(22600 + 16 * SEQ, 16, P)
        oT = region(32840, HEADS, SEQ)
        f1 = [region(6144 * i, KT, FC * P) for i in range(FF_SETS)]
        f3 = [region(6144 * i + 2048, KT, FC * P) for i in range(FF_SETS)]
        f2 = [region(6144 * i + 4096, FC, DM) for i in range(FF_SETS)]
        hT = region(18432, 2, FC, SEQ)
        hsil = region(19456, 2, SEQ)
        early = [ESLAB * (6 + i) for i in range(6)] + [0, ESLAB]
        m1 = [region(early[2 * c], KT, EW1) for c in range(EC)]
        m3 = [region(early[2 * c + 1], KT, EW1) for c in range(EC)]
        m2 = [region(ESLAB * (2 + c), FE_T, EW2) for c in range(EC)]
        xg = region(33792, KT, P)
        msil = region(34816, 2, EW1)
        mh = region(35520, FE)
        macc = region(36928, NT, DM)
        mhT = region(38976, FE_T, P)
        ysb = region(40384, DM)
        pick = region(41408, NT, P)
        pick_g = region(41664, NT, P)
        spread = region(41920, NT, P)
        V = region(19968, 2, PAIRS, 9, GC)
        W1T = region(29184, 2, PAIRS, P)
        Wp = region(37376, 2, PIECE, SUB, GC)
        KD = region(39424, PIECE, P, parts=2 * GC)
        skip = region(40448, 4, GC, parts=2 * GC)
        Bb = region(40576, 2, PAIRS, GC)
        Ct = region(41600, 2, PAIRS, GC)
        pw = region(42624, 2, 9, PAIRS)
        pw_back = region(43200, 2, SUB, PAIRS)
        Bbd = region(43712, 2, PIECE, 2 * GC)
        B_raw = region(29184, 2, PAIRS, GC)
        C_raw = region(30208, 2, 8, STATE)
        lam_raw = region(31232, 2, STATE, parts=32)
        lam_raw2 = region(31360, 2, STATE, parts=32)
        lam = region(31488, 2, PAIRS)
        dts = region(31552, PAIRS)
        z = region(31584, 2, PAIRS)
        pw_mag = region(31648, 9, PAIRS)
        pw_ang = region(32192, 2, 9, PAIRS)
        pw_n = region(33280, 2, 9, PAIRS)
        sc = [region(34368 + 32 * i, PAIRS) for i in range(12)]
        sin_b = region(34752, PAIRS)
        tb = region(34784, PAIRS, GC)
        kzero = region(35296, 1024, parts=2 * GC)
        flat_w = norm_w[:].rearrange("p a b -> p (a b)")
        t_p, t_v = flat_w[:, 0:PIECE * 9 * GC], flat_w[:, PIECE * 9 * GC:PIECE * 9 * GC * 3 // 2]
        d_col = d_small[0:2 * GC]
        u_n = region(0, SUB, PAIRS * GC, parts=64)
        u_r = region(4096, PAIRS, P, parts=64)
        y_sb = region(0, 2, SUB, P, parts=64)
        hidT = region(2048, KT, SEQ)
        T = region(8192, 2, PAIRS, P)
        U = region(16384, PAIRS, 2, NSUB)
        u_tok = region(16384, NT, DM)
        E = region(37376, 2, PAIRS, NSUB)
        H = region(29184, NSUB, 2, PAIRS)
        Hbd = region(31232, 2, PAIRS, 2, NSUB)
        ht = [region(35328 + 672 * i, 4, 2, PAIRS) for i in range(2)]
        hc = [region(35328 + 672 * i, 3, 7, PAIRS) for i in range(2)]
        p8 = region(43712, 2, 8, PAIRS)
        carry = region(18432, 4, 2, PAIRS)
        ebuf = region(18688, 4, 2, PAIRS)
        glu = [region(o_, KT, 512) for o_ in (4096, 39424, 8192, 12288)]
        gsig = region(33792, NT, DM)
        q2 = region(32768 + 0, 4, SEQ)
        k2 = region(33792, 4, SEQ)
        v2 = region(34816, NT, 512)
        u2 = region(35840, NT, 512)
        poolT = region(36864, 4, SEQ)
        catT = region(37888, 8, SEQ)
        prob = [region(o_, 2, 2, SEQ) for o_ in (39936, 12288)]
        probT = region(40960, 2, 2, SEQ)
        in2 = [region(o_, KT, 512) for o_ in (20480, 24576, 28672, 16384)]
        out2 = [region(4096 * c, 4, DM) for c in range(2)]
        bias = region(8192, NT, AH, SEQ)
        poolw = region(12288, NT, 4, SEQ)
        wpool = region(14336, 4, P)
        amask = region(14848, GRID)
        mix_g = region(14848 + GRID, DM)
        up2 = [region(16384 + 4096 * c, KT, 512) for c in range(2)]
        down2 = [region(24576 + 4096 * c, 4, DM) for c in range(2)]
        h2n = region(41984, NT, DM)
        mT = region(0, 2, 4, SEQ)
        u_dram = nc.dram_tensor("u_scratch", (SEQ, DM), F32, kind="Internal").ap()
        k_dram = nc.dram_tensor("k_scratch", (2 * GC, PAIRS, 2 * P), F32, kind="Internal").ap()

        x_loaded, const_loaded, vecs_loaded = sem("x_loaded"), sem("const_loaded"), sem("vecs_loaded")
        normw_loaded, small_loaded = sem("normw_loaded"), sem("small_loaded")
        ba_w_loaded = sem("ba_w_loaded")
        ready = sem("consts_ready")
        vec_tr, vec_ok = sem("vec_transposed"), sem("vec_ok")
        slab = [sem(f"slab{i}_loaded") for i in range(9)]
        xt_tr, xt_v, xt_a = sem("x_transposed"), sem("xT_by_vector"), sem("xT_by_scalar")
        norm_done = sem("norm_done")
        norm_v, norm_a = sem("norm_step_by_vector"), sem("norm_step_by_scalar")
        ba_done = sem("ba_done")
        ba_v, ba_a, g_ready = sem("ba_by_vector"), sem("ba_by_scalar"), sem("g_ready")
        in_tile, pre_ready, conv_done, silu_done = sem("in_tile"), sem("pre_ready"), sem("conv_done"), sem("silu_done")
        pad_ready = sem("pad_ready")
        sq_ready, ss_ready, nrm_ready, unit_ready = sem("sq_ready"), sem("ss_ready"), sem("nrm_ready"), sem("unit_ready")
        grow_done, gc_ready, dec_v, dec_a, dec_ready = sem("grow_done"), sem("gc_ready"), sem("dec_v"), sem("dec_a"), sem("dec_ready")
        kq_done, kq_read = sem("kq_done"), sem("kq_read")
        d_tr, d_evac = sem("d_transposed"), sem("dT_ready")
        lv_q, lv_qe, lv_p, lv_pe = sem("level_q"), sem("level_q_read"), sem("level_p"), sem("level_p_read")
        vk_tr, vk_ready = sem("vk_transposed"), sem("vk_ready")
        rec, rec_ev = sem("recurrence_step"), sem("recurrence_read")
        o_std, o_norm, o_tr, o_ready = sem("o_std"), sem("o_norm"), sem("o_tr"), sem("o_ready")
        y_done = sem("y_done")
        up_done, sil_done, h_done = sem("up_done"), sem("sil_done"), sem("h_done")
        down_done = sem("down_done")
        s5_loaded, s5_tr, s5_in, s5_read = sem("s5_loaded"), sem("s5_param_tr"), sem("s5_dt_ready"), sem("s5_param_read")
        s5_v, s5_a = sem("s5_by_vector"), sem("s5_by_scalar")
        bb_ready, w_ready, w_tr, w_in, v_ready = sem("bb_ready"), sem("w_ready"), sem("w_tr"), sem("w1t_ready"), sem("v_ready")
        im_ready = sem("im_ready")
        kd_done, kd_ready, kd_stored, t_loaded = sem("kd_done"), sem("kd_ready"), sem("kd_stored"), sem("t_loaded")
        kz_stored = sem("kz_stored")
        u_sb, u_stored, un_loaded, ur_ready, u_tr, u_ready = sem("u_sb"), sem("u_stored"), sem("un_loaded"), sem("ur_ready"), sem("u_tr"), sem("u_ready")
        e_done, e_read, h_bd, hbd_zero = sem("e_done"), sem("e_read"), sem("h_bd"), sem("hbd_zero")
        ys_done, ys_read, yt_done, hid_ready = sem("ys_done"), sem("ys_read"), sem("yt_done"), sem("hid_ready")
        glu_done, sig_done, glu_read = sem("glu_done"), sem("sig_done"), sem("glu_read")
        route_done, route_read, route_a = sem("route_done"), sem("route_read"), sem("route_a")
        chosen_ready, place_done, passes_ready = sem("chosen_ready"), sem("place_done"), sem("passes_ready")
        m_loaded = [sem(f"expert_slabs{i}_loaded") for i in range(2 * EC)]
        pick_ready, pickg_ready, gath_done, xg_ready = sem("pick_ready"), sem("pick_gate_ready"), sem("gather_done"), sem("xg_ready")
        m_up, m_sil, m_h, m_tr, m_hT = sem("expert_up"), sem("expert_silu"), sem("expert_h"), sem("expert_hT_transposed"), sem("expert_hT_ready")
        turns_done = sem("turns_done")
        m_y, m_yread, m_sc, m_acc = sem("expert_y"), sem("expert_y_read"), sem("expert_scattered"), sem("expert_added")
        b2_loaded, bias_ready = sem("b2_loaded"), sem("bias_ready")
        p_done, p_read_a, p_read_v = sem("proj2_done"), sem("proj2_by_scalar"), sem("proj2_by_vector")
        pool_done, pool_read, mix_done, mix_read = sem("pool_done"), sem("pool_read"), sem("mix_done"), sem("mix_read")
        sc_done, max_ready, exp_done, pn_ready = sem("score_done"), sem("max_ready"), sem("exp_done"), sem("prob_ready")
        pt_done, pt_read, pv_done, pv_read = sem("pt_done"), sem("pt_read"), sem("pv_done"), sem("pv_read")
        y2_done, up2_done, relu_done, sqr_done = sem("y2_done"), sem("up2_done"), sem("relu_done"), sem("sqr_done")
        down2_done, out_stored = sem("down2_done"), sem("out_stored")
        chain_v, chain_a, chain_p = sem("vector_chain"), sem("scalar_chain"), sem("pool_chain")

        block = ctx.enter_context(nc.Block())

        def rows(w, k0, n):
            return w[k0 * P:(k0 + n) * P, :].rearrange("(k p) f -> p k f", p=P)

        sent, arrival = {}, {}

        def load(eng, key, i, dst, src):
            sent[i] = sent.get(i, 0) + 16
            arrival[key] = (slab[i], sent[i])
            eng.dma_start(dst, src).then_inc(slab[i], 16)

        def arrived(eng, key):
            eng.wait_ge(*arrival[key])

        def after(eng, sem_, value):
            if not isinstance(value, int) or value > 0:
                eng.wait_ge(sem_, value)

        def every(ap, n, off=0):
            return bass.AP(ap.tensor, ap.offset + off, [[0, P], [1, n]])

        def table_product(eng_ns, link, dst, pa, pb, qa, qb, t, sub):
            link(eng_ns.tensor_tensor(dst, pa, qa, ALU.mult))
            link(eng_ns.tensor_tensor(t, pb, qb, ALU.mult))
            return eng_ns.tensor_tensor(dst, dst, t, ALU.subtract if sub else ALU.add)

        def s5_factors(pr, powers, n, tab):
            shape = (P, pr.stop - pr.start, n, GC)

            def power(c):
                return powers[:, c, :, pr].rearrange("p k a -> p a k")[:, :, :, None].broadcast_to(shape)

            def table(c):
                return tab[:, c, pr, None, :].broadcast_to(shape)
            return power, table

        def s5_v_table(eng_ns, link, pr, part, t):
            power, table = s5_factors(pr, pw, 9, Ct)
            n = pr.stop - pr.start
            dst = V[:, part, pr]
            tt = t[:, 0:n * 9 * GC].rearrange("p (a b c) -> p a b c", a=n, b=9)
            if part == 0:
                return table_product(eng_ns, link, dst, power(0), power(1), table(0), table(1), tt, True)
            link(table_product(eng_ns, link, dst, power(0), power(1), table(1), table(0), tt, False))
            return eng_ns.tensor_scalar(dst, dst, -1.0, None, ALU.mult)

        def s5_w_table(eng_ns, link, j, part, t):
            power, table = s5_factors(slice(PIECE * j, PIECE * (j + 1)), pw_back, SUB, Bb)
            tt = t[:, 0:PIECE * SUB * GC].rearrange("p (a b c) -> p a b c", a=PIECE, b=SUB)
            if part == 0:
                return table_product(eng_ns, link, Wp[:, 0], power(0), power(1), table(0), table(1), tt, True)
            return table_product(eng_ns, link, Wp[:, 1], power(0), power(1), table(1), table(0), tt, False)

        def s5_pool(pool, link):
            for i, name in enumerate(("s5_lam_re", "s5_lam_im")):
                pool.dma_start(lam_raw[:, i], A[name][0, 0:32]).then_inc(s5_loaded, 16)
                pool.dma_start(lam_raw2[:, i], A[name][0, 32:64]).then_inc(s5_loaded, 16)
            for i, name in enumerate(("s5_c_re", "s5_c_im")):
                pool.dma_start(C_raw[:, i], A[name][0].rearrange("(j g) c p -> (g c) j p", j=8)).then_inc(s5_loaded, 16)
            for gh in range(2):
                half = slice(64 * gh, 64 * gh + 64)
                pool.dma_start(dts[half], bass.AP(A["s5_log_dt"].tensor, 32 * gh, [[0, 64], [1, 32]])).then_inc(s5_loaded, 16)
                for i, name in enumerate(("s5_b_re", "s5_b_im")):
                    pool.dma_start(B_raw[half, i], A[name][0, 32 * gh:32 * gh + 32].rearrange("g p c -> p g c")).then_inc(s5_loaded, 16)
            with nc.allow_non_contiguous_dma("1024 values"):
                for gh in range(2):
                    pool.dma_start(d_col[GC * gh:GC * gh + GC], A["s5_d"][0, 512 * gh:512 * gh + 512].rearrange("(a c) -> c a", c=GC)).then_inc(s5_loaded, 16)
            link(nc.gpsimd.memset(kzero, 0.0))
            for q in range(4):
                pool.dma_start(k_dram[:, 8 * q:8 * q + 8, 0:P], kzero.rearrange("p (a b) -> p a b", a=8)).then_inc(kz_stored, 16)
            link(nc.gpsimd.memset(Bbd, 0.0))
            pool.wait_ge(bb_ready, 1)
            for j in range(NPIECE):
                pr = slice(PIECE * j, PIECE * (j + 1))
                if j:
                    pool.wait_ge(w_tr, 4 * j)
                for part in range(2):
                    s5_w_table(nc.gpsimd, link, j, part, t_p).then_inc(w_ready, 1)
                    pool.wait_ge(w_ready, 2 * j + part + 1)
                if j:
                    pool.wait_ge(kd_done, 2 * j)
                for gh in range(2):
                    half = slice(64 * gh, 64 * gh + 64)
                    link(nc.gpsimd.tensor_copy(Bbd[half, :, :, GC * gh:GC * gh + GC], Bb[half, :, pr]))
                s5_v_table(nc.gpsimd, link, pr, 1, t_p).then_inc(im_ready, 1)
                pool.wait_ge(im_ready, j + 1)

        def inverse_update(dve, V_, lv, j):
            s = slice(4 * j, 4 * j + 4)
            i = 4 * (lv - 1) + j
            dve.wait_ge(lv_p, i + 1)
            V_.tensor_tensor(DT[:, s], DT[:, s], four(banks[2 + j % 2]), ALU.subtract).then_inc(lv_pe, 1)
            if lv < LEVELS - 1:
                V_.tensor_tensor(D[:, s], D[:, s], four(banks[4 + j % 2]), ALU.subtract).then_inc(lv_pe, 1)

        @block.sync
        def _(sp):
            sp.dma_start(const[:], A["shape_const"].rearrange("p (a b) -> p a b", b=P)).then_inc(const_loaded, 16)
            sp.dma_start(xres[:], A["x"][0].rearrange("(n p) d -> p n d", p=P)).then_inc(x_loaded, 16)
            w_in = A["gdn_w_in"][0].rearrange("(k p) f -> p k f", p=P)
            sp.wait_ge(vecs_loaded, 48)
            sp.wait_ge(ba_w_loaded, 16)
            for b in range(8):
                if b >= 4:
                    sp.wait_ge(in_tile, 4 * (b - 3))
                load(sp, ("gdn_in", b), b % 4, region(4096 * (b % 4), KT, 512), w_in[:, :, 512 * b:512 * b + 512])

            w1, w3 = (A[f"ffn_w{i}"][0].rearrange("(k p) f -> p k f", p=P) for i in (1, 3))
            w2 = A["ffn_w2"][0]

            def swiglu_loads(c):
                i, cols = c % FF_SETS, slice(FC * P * c, FC * P * (c + 1))
                if c >= FF_SETS:
                    sp.wait_ge(up_done, 2 * FC * (c - FF_SETS + 1))
                load(sp, ("ffn_w1", c), 4 + i, f1[i], w1[:, :, cols])
                load(sp, ("ffn_w3", c), 4 + i, f3[i], w3[:, :, cols])
                if c >= FF_SETS:
                    sp.wait_ge(down_done, c - FF_SETS + 1)
                load(sp, ("ffn_w2", c), i, f2[i], rows(w2, FC * c, FC))

            for c in range(2):
                sp.wait_ge(in_tile, 4 * (c + 7))
                load(sp, ("gdn_out", c), 2 + c, region(4096 * (2 + c), 4, DM), rows(A["gdn_w_out"][0], 4 * c, 4))
            swiglu_loads(0)
            sp.wait_ge(y_done, 4)
            for c in range(1, FF_CHUNKS):
                swiglu_loads(c)
            sp.wait_ge(up_done, 2 * FC * FF_CHUNKS)
            sp.wait_ge(down_done, FF_CHUNKS - 1)
            for c in range(2):
                load(sp, ("s5_in", c), 7 + c, region(4096 * c, 4, DM), rows(A["s5_w_in"][0], 4 * c, 4))
            sp.wait_ge(kd_stored, 16 * NPIECE)
            sp.wait_ge(kz_stored, 64)
            sp.wait_ge(y_done, 8)
            for gh in range(2):
                for s in range(SUB):
                    sp.dma_start(T[GC * s:GC * (s + 1), gh],
                                 k_dram[GC * gh:GC * (gh + 1), :, (SUB - s) * GC:(SUB - s) * GC + P]).then_inc(t_loaded, 16)
            sp.wait_ge(u_sb, 4)
            sp.dma_start(u_dram.rearrange("(n p) d -> p n d", p=P), u_tok).then_inc(u_stored, 16)
            sp.wait_ge(u_stored, 16)
            for gh in range(2):
                sp.dma_start(u_n[32 * gh:32 * gh + 32],
                             u_dram[:, 512 * gh:512 * gh + 512].rearrange("(n s) d -> n s d", s=SUB)).then_inc(un_loaded, 16)
            w_glu = A["s5_w_glu"][0].rearrange("(k p) f -> p k f", p=P)
            sp.wait_ge(u_tr, 4)
            for i, c in enumerate((0, 2, 1, 3)):
                if i == 2:
                    sp.wait_ge(ys_done, NPIECE * 2)
                load(sp, ("glu", i), i, glu[i], w_glu[:, :, 512 * c:512 * c + 512])

            def expert_loads(e, k, first=False):
                w1e, w3e, w2e = (A[f"moe_w{i}"][0][bass.ds(e, 1)].rearrange("e (k p) f -> p (e k) f", p=P) for i in (1, 3, 2))
                for c in range(EC):
                    cols = slice(EW1 * c, EW1 * c + EW1)
                    if not first:
                        sp.wait_ge(m_up, k * 2 * EC + 2 * c + 1)
                    elif c == 3:
                        sp.wait_ge(glu_done, 8)
                    sp.dma_start(m1[c], w1e[:, :, cols]).then_inc(m_loaded[c], 16)
                    if not first:
                        sp.wait_ge(m_up, k * 2 * EC + 2 * c + 2)
                    sp.dma_start(m3[c], w3e[:, :, cols]).then_inc(m_loaded[c], 16)
                for c in range(EC):
                    if not first:
                        sp.wait_ge(m_y, k * EC + c + 1)
                    sp.dma_start(m2[c], w2e[:, :, EW2 * c:EW2 * c + EW2]).then_inc(m_loaded[EC + c], 16)

            expert_loads(0, 0, first=True)
            sp.wait_ge(passes_ready, 1)
            n_pass = sp.value_load(passes[0:1, 0:1], min_val=1, max_val=2)
            with sp.Fori(1, n_pass * EXPERTS) as k:
                expert_loads(k % EXPERTS, k)
            sp.wait_ge(m_up, n_pass * (EXPERTS * 2 * EC) + 6)
            w_in2 = A["w_in_2"][0].rearrange("(k p) f -> p k f", p=P)
            for i in range(4):
                if i == 3:
                    sp.wait_ge(m_y, n_pass * (EXPERTS * EC) + EC)
                load(sp, ("in2", i), i, in2[i], w_in2[:, :, 512 * i:512 * i + 512])
            for c in range(2):
                load(sp, ("out2", c), 4 + c, out2[c], rows(A["w_out_2"][0], 4 * c, 4))
            sp.wait_ge(p_done, 12)
            w_up = A["w_up_2"][0].rearrange("(k p) f -> p k f", p=P)
            for i in range(4):
                for c in range(2):
                    if i:
                        sp.wait_ge(up2_done, 8 * (i - 1) + 4 * (c + 1))
                    f0 = 512 * (2 * i + c)
                    load(sp, ("up2", 2 * i + c), 6 + c, up2[c], w_up[:, :, f0:f0 + 512])
                for c in range(2):
                    if i:
                        sp.wait_ge(down2_done, 2 * (i - 1) + c + 1)
                    load(sp, ("down2", 2 * i + c), 2 + c, down2[c], rows(A["w_down_2"][0], 4 * (2 * i + c), 4))
            for n in range(NT):
                sp.wait_ge(norm_done, 13 + n)
                sp.dma_start(out[0, P * n:P * n + P], xres[:, n]).then_inc(out_stored, 16)
            sp.wait_ge(out_stored, 16 * NT)

        @block.gpsimd
        def _(pool):
            count = [0]

            def link(ins):
                count[0] += 1
                ins.then_inc(chain_p, 1)
                pool.wait_ge(chain_p, count[0])

            pool.dma_start(vrows[0:96], A["gdn_conv_w"][0].rearrange("j (t p) -> (j t) p", p=P)).then_inc(vecs_loaded, 16)
            pool.dma_start(vrows[96:97], A["gdn_norm_g"]).then_inc(vecs_loaded, 16)
            pool.dma_start(vrows[97:101], A["pool_scale_2"][0].rearrange("(t p) -> t p", p=P)).then_inc(vecs_loaded, 16)
            pool.dma_start(region(38984, KT, 16), A["gdn_w_in"][0].rearrange("(k p) f -> p k f", p=P)[:, :, 4096:4112]).then_inc(ba_w_loaded, 16)
            pool.dma_start(a_log, every(A["gdn_a_log"], 8)).then_inc(small_loaded, 16)
            pool.dma_start(dt_b, every(A["gdn_dt_bias"], 8)).then_inc(small_loaded, 16)
            pool.dma_start(router_b, every(A["moe_b_router"], 8)).then_inc(small_loaded, 16)

            def norm_load(slot, name, off):
                pool.dma_start(norm_w[:, slot, :], every(A[name], DM, off)).then_inc(normw_loaded, 16)

            norm_load(0, "ln_g", 0)
            norm_load(1, "ln_b", 0)
            nc.gpsimd.memset(pre[:, :, 0:CONV - 1], 0.0).then_inc(pad_ready, 1)
            for j in range(4):
                pool.wait_ge(dec_a, 2 * (j + 1))
                s = slice(4 * j, 4 * j + 4)
                nc.gpsimd.tensor_tensor(decL[:, s, :], decL[:, s, :], over(mat(C_LOW), 4), ALU.mult).then_inc(dec_ready, 1)
                nc.gpsimd.tensor_tensor(decT[:, s, :], decT[:, s, :], over(mat(C_TRI), 4), ALU.mult).then_inc(dec_ready, 1)
            for i in range(8):
                pool.wait_ge(silu_done, i // 2 + 1)
                if i >= 2:
                    pool.wait_ge(ss_ready, i - 1)
                src = qkvT[:, 2 * i:2 * i + 2, :].rearrange("p a b -> p (a b)")
                nc.gpsimd.tensor_tensor(sq[:, i % 2, :], src, src, ALU.mult).then_inc(sq_ready, 1)
            pool.wait_ge(norm_done, 2)
            pool.dma_start(w_router, A["moe_w_router"][0].rearrange("(k p) f -> p k f", p=P)).then_inc(small_loaded, 16)
            s5_pool(pool, link)
            pool.wait_ge(v_ready, 2 * NPIECE)
            norm_load(0, "ln_g", DM)
            norm_load(1, "ln_b", DM)
            for n in (2, 3):
                pool.wait_ge(norm_done, 2 * n)
                norm_load(0, "ln_g", n * DM)
                norm_load(1, "ln_b", n * DM)
                if n == 2:
                    pool.wait_ge(e_read, 8)
                    nc.gpsimd.memset(Hbd, 0.0).then_inc(hbd_zero, 1)
            pool.wait_ge(turns_done, 1)
            pool.dma_start(mix_g, every(A["norm_mix_g_2"], DM)).then_inc(small_loaded, 16)
            for r in range(4):
                for i in range(4):
                    src = bass.AP(A["rpb_2"].tensor, (7 + i - r) * 31 - 48, [[1, GRID], [15 * 31, AH], [1, GRID]])
                    dst = bias[GRID * (r % 2):GRID * (r % 2) + GRID, r // 2, :, GRID * i:GRID * i + GRID]
                    pool.dma_start(dst, src).then_inc(b2_loaded, 16)
            pool.dma_start(amask, A["shape_mask"]).then_inc(b2_loaded, 16)
            pool.dma_start(poolw, A["shape_pool"].rearrange("(n p) a b -> p n a b", p=P)).then_inc(b2_loaded, 16)
            pool.dma_start(wpool, A["w_pool_2"][0].rearrange("a p b -> p a b")).then_inc(b2_loaded, 16)
            pool.wait_ge(norm_done, 8)
            norm_load(0, "final_g_2", 0)
            norm_load(1, "norm_mlp_g_2", 0)
            pool.wait_ge(b2_loaded, 16 * 19)
            for n in range(NT):
                v = bias[:, n].rearrange("p h (i k) -> p (h i) k", k=GRID)
                ins = nc.gpsimd.tensor_tensor(v, v, over(amask, AH * 4), ALU.add)
                ins.then_inc(bias_ready, 1)

        @block.vector
        def _(dve):
            V_ = nc.vector
            count = [0]

            def link(ins):
                count[0] += 1
                ins.then_inc(chain_v, 1)
                dve.wait_ge(chain_v, count[0])

            for c, val in ((eps_ln, LN_EPS), (eps_rms, EPS), (one_c, 1.0), (zero_c, 0.0)):
                last = V_.memset(c, val)
            last.then_inc(ready, 1)

            seen_xt = [0]

            def take_xT():
                for j in (0, 2):
                    dve.wait_ge(xt_tr, 4 * seen_xt[0] + j + 1)
                    V_.tensor_copy(xT[:, 4 * (j % 2) + 0:4 * (j % 2) + 4, P * (j // 2):P * (j // 2) + P], four(banks[4 + j])).then_inc(xt_v, 1)
                seen_xt[0] += 1

            dve.wait_ge(vec_tr, 1)
            V_.tensor_copy(vecT, banks[3][:, 0:101]).then_inc(vec_ok, 1)
            take_xT()
            dve.wait_ge(ba_done, 1)
            for n in range(NT):
                last = V_.tensor_copy(ba[:, n], banks[6 + n][:, 0:16])
            link(last)
            dve.wait_ge(small_loaded, 48)
            V_.tensor_tensor(tmp_a, ba[:, :, 8:16], over(dt_b, NT), ALU.add).then_inc(ba_v, 1)
            dve.wait_ge(ba_a, 2)
            dve.wait_ge(ba_v, 1)
            link(V_.tensor_scalar(tmp_a, tmp_a, 0.0, None, ALU.max))
            link(V_.tensor_tensor(tmp_a, tmp_a, tmp_b, ALU.add))
            link(V_.tensor_scalar(tmp_a, tmp_a, -1.0, None, ALU.mult))
            V_.tensor_tensor(g, tmp_a, over(a_log, NT), ALU.mult).then_inc(g_ready, 1)

            def unit(b):
                for i in (2 * b, 2 * b + 1):
                    dve.wait_ge(nrm_ready, i + 1)
                    link(V_.reciprocal(rs[:, i % 2, :], rs[:, i % 2, :]))
                    v = qkvT[:, 2 * i:2 * i + 2, :].rearrange("p a b -> p (a b)")
                    V_.scalar_tensor_tensor(v, rs[:, i % 2, :], DK ** -0.5 if i < 4 else 1.0, v, ALU.mult, ALU.mult).then_inc(unit_ready, 1)

            def decay_rows():
                dve.wait_ge(grow_done, 1)
                link(V_.tensor_copy(gc.rearrange("p a b -> p (a b)"), banks[3][:, 0:16]))
                for j in range(4):
                    dve.wait_ge(grow_done, j + 2)
                    for b in range(4 * j, 4 * j + 4):
                        src = four(banks[4 + j])[:, b % 4]
                        col = gc.rearrange("p a b -> p (a b)")[:, b:b + 1]
                        V_.tensor_scalar(decL[:, b], src, col, 0.0, ALU.subtract, ALU.max)
                        last = V_.tensor_scalar(decT[:, b], src, col, 0.0, ALU.subtract, ALU.min)
                    if j < 2:
                        link(last)
                        last = V_.tensor_copy(glast[:, 4 * j:4 * j + 4], four(banks[4 + j])[:, :, P - 1])
                    last.then_inc(dec_v, 1)
                dve.wait_ge(dec_v, 4)
                V_.tensor_tensor(tmp_a[:, 0], glast, gc[:, 0], ALU.subtract).then_inc(gc_ready, 1)

            for b in range(6):
                dve.wait_ge(pre_ready, 4 * (b + 1))
                if b == 0:
                    dve.wait_ge(pad_ready, 1)
                    dve.wait_ge(vec_ok, 1)
                for j in range(CONV):
                    for m in range(4 * b, 4 * b + 4):
                        w = vecT[:, j * QKV_T + m:j * QKV_T + m + 1]
                        if j == 0:
                            last = V_.tensor_scalar(qkvT[:, m], pre[:, m, 0:SEQ], w, None, ALU.mult)
                        else:
                            last = V_.scalar_tensor_tensor(qkvT[:, m], pre[:, m, j:j + SEQ], w, qkvT[:, m], ALU.mult, ALU.add)
                    if j < CONV - 1:
                        link(last)
                last.then_inc(conv_done, 1)
                if b == 1:
                    decay_rows()
                if b >= 4:
                    unit(b - 4)
            unit(2)
            unit(3)

            dve.wait_ge(dec_a, 12)
            link(V_.tensor_scalar(neg_eg, neg_eg, -1.0, None, ALU.mult))
            dve.wait_ge(unit_ready, 4)
            link(V_.tensor_tensor(e_row, e_row, qkvT[:, 0:8, P:2 * P], ALU.mult))
            for j in range(4):
                dve.wait_ge(kq_done, j + 1)
                dve.wait_ge(dec_ready, 2 * (j + 1))
                for b in range(4 * j, 4 * j + 4):
                    bcol = beta.rearrange("p a b -> p (a b)")[:, b:b + 1]
                    V_.scalar_tensor_tensor(decL[:, b], four(banks[j % 2])[:, b % 4], bcol, decL[:, b], ALU.mult, ALU.mult)
                s = slice(4 * j, 4 * j + 4)
                last = V_.tensor_tensor(decT[:, s], four(banks[2 + j % 2]), decT[:, s], ALU.mult)
                link(last)
                link(V_.scalar_tensor_tensor(D[:, s], decL[:, s], -1.0, over(mat(C_M0), 4), ALU.mult, ALU.mult))
                V_.tensor_tensor(D[:, s], D[:, s], over(ident, 4), ALU.add).then_inc(kq_read, 1)
            for j in range(4):
                dve.wait_ge(d_tr, j + 1)
                V_.tensor_copy(DT[:, 4 * j:4 * j + 4], four(banks[4 + j])).then_inc(d_evac, 1)
            for lv in range(1, LEVELS):
                for j in range(4):
                    s = slice(4 * j, 4 * j + 4)
                    i = 4 * (lv - 1) + j
                    dve.wait_ge(lv_q, i + 1)
                    V_.tensor_tensor(QT[:, s], four(banks[j % 2]), over(mat(C_LV + lv), 4), ALU.mult).then_inc(lv_qe, 1)
                    if j:
                        inverse_update(dve, V_, lv, j - 1)
                inverse_update(dve, V_, lv, 3)
            dve.wait_ge(vk_tr, 4)
            for b in range(16):
                src = four(banks[b // 4])[:, b % 4]
                if b < 8:
                    V_.tensor_scalar(vtok[:, b], src, beta[:, 0, b:b + 1], None, ALU.mult).then_inc(vk_ready, 1)
                else:
                    V_.tensor_copy(vtok[:, b], src).then_inc(vk_ready, 1)
            for h in range(8):
                dve.wait_ge(vk_tr, 5 + h // 4)
                V_.tensor_scalar(kd[:, h], four(banks[4 + h // 4])[:, h % 4], kdf[:, h:h + 1], None, ALU.mult).then_inc(vk_ready, 1)
            for j in range(2):
                dve.wait_ge(rec, j + 1)
                V_.tensor_copy(vn[:, 0, 4 * j:4 * j + 4], four(banks[6 + j])).then_inc(rec_ev, 1)
            for j in range(2):
                dve.wait_ge(rec, 3 + 2 * j)
                V_.tensor_copy(s1[:, 4 * j:4 * j + 4], four(banks[j])).then_inc(rec_ev, 1)
                dve.wait_ge(rec, 4 + 2 * j)
                V_.tensor_copy(o[:, 4 * j:4 * j + 4], four(banks[2 + j])).then_inc(rec_ev, 1)
            for j in range(2):
                dve.wait_ge(rec, 7 + j)
                dve.wait_ge(vk_ready, 24)
                for h in range(4 * j, 4 * j + 4):
                    last = V_.scalar_tensor_tensor(r1[:, h], four(banks[4 + j])[:, h % 4], neg_eg[:, h:h + 1], vtok[:, 8 + h], ALU.mult, ALU.add)
                link(last)
                for h in range(4 * j, 4 * j + 4):
                    last = V_.tensor_scalar(r1[:, h], r1[:, h], beta[:, 1, h:h + 1], None, ALU.mult)
                last.then_inc(rec_ev, 1)
            for j in range(2):
                dve.wait_ge(rec, 9 + j)
                V_.tensor_copy(vn[:, 1, 4 * j:4 * j + 4], four(banks[6 + j])).then_inc(rec_ev, 1)
            def normalise(n):
                dve.wait_ge(o_std, n + 1)
                ss, on = o_ss[:, HEADS * n:HEADS * n + HEADS], o[:, HEADS * n:HEADS * n + HEADS]
                link(V_.reciprocal(ss, ss))
                V_.tensor_tensor(on, on, ss[:, :, None].broadcast_to((P, HEADS, P)), ALU.mult).then_inc(o_norm, 1)

            normalise(0)
            for j in range(2):
                dve.wait_ge(rec, 11 + j)
                V_.tensor_copy(o[:, 8 + 4 * j:12 + 4 * j], four(banks[j])).then_inc(rec_ev, 1)
            normalise(1)
            for j in range(4):
                dve.wait_ge(o_tr, j + 1)
                hs, ts = slice(4 * (j % 2), 4 * (j % 2) + 4), slice(P * (j // 2), P * (j // 2) + P)
                V_.scalar_tensor_tensor(oT[:, hs, ts], four(banks[4 + j]), vecT[:, 96:97], zT[:, hs, ts], ALU.mult, ALU.mult).then_inc(o_ready, 1)

            steps = [0]

            def scalar_step():
                steps[0] += 1
                dve.wait_ge(norm_a, steps[0])

            def layer_norm(src, scale, signal):
                def statistics(n, hf):
                    r = xres[:, n, 512 * hf:512 * hf + 512]
                    link(V_.scalar_tensor_tensor(r, r, scale, src(n, hf), ALU.mult, ALU.add))
                    link(V_.bn_stats(stats[:, n, hf, :], r))

                def factors(n):
                    V_.bn_aggr(mv[:, n], stats[:, n].rearrange("p a b -> p (a b)")).then_inc(norm_v, 1)
                    scalar_step()
                    link(V_.reciprocal(rstd[:, n:n + 1], rstd[:, n:n + 1]))
                    V_.scalar_tensor_tensor(shift[:, n:n + 1], mv[:, n, 0:1], -1.0, rstd[:, n:n + 1], ALU.mult, ALU.mult).then_inc(norm_v, 1)

                def affine(n):
                    scalar_step()
                    dve.wait_ge(normw_loaded, 32 * (signal + 1))
                    link(V_.tensor_tensor(xres[:, n], xres[:, n], norm_w[:, 0], ALU.mult))
                    V_.tensor_tensor(xres[:, n], xres[:, n], norm_w[:, 1], ALU.add).then_inc(norm_done, 1)

                statistics(0, 0)
                statistics(0, 1)
                factors(0)
                statistics(1, 0)
                affine(0)
                statistics(1, 1)
                factors(1)
                affine(1)
                dve.wait_ge(norm_done, 2 * signal + 2)

            def from_banks(base):
                def src(n, hf):
                    dve.wait_ge(y_done, base + 2 * n + hf + 1)
                    return banks[2 * n + hf][:, :]
                return src

            layer_norm(from_banks(0), ALPHA, 0)
            take_xT()

            def s5_parameters():
                dve.wait_ge(s5_tr, 1)
                V_.tensor_copy(lam.rearrange("p a b -> p (a b)"), banks[4][:, 0:64])
                for i in range(2):
                    for jb in range(8):
                        half = slice(64 * (jb // 4), 64 * (jb // 4) + 64)
                        last = V_.tensor_copy(Ct[half, i, 8 * (jb % 4):8 * (jb % 4) + 8].rearrange("p a b -> p (a b)"),
                                              banks[5 + i][half, P * (jb % 4):P * (jb % 4) + P])
                last.then_inc(s5_read, 1)
                dve.wait_ge(s5_read, 1)
                dve.wait_ge(s5_in, 1)
                link(V_.tensor_tensor(z, lam, dts[:, None, :].broadcast_to((P, 2, PAIRS)), ALU.mult))
                for k in range(9):
                    V_.tensor_scalar(pw_mag[:, k], z[:, 0], float(k), None, ALU.mult)
                    V_.tensor_scalar(pw_ang[:, 1, k], z[:, 1], float(k), None, ALU.mult)
                    last = V_.tensor_scalar(pw_ang[:, 0, k], z[:, 1], float(k), float(np.pi / 2), ALU.mult, ALU.add)
                link(last)
                ROUND = 12582912.0
                C1 = 6.28125
                C2 = 0.0019353071795864769
                flat = [t.rearrange("p a b c -> p (a b c)") for t in (pw_ang, pw_n)]
                link(V_.tensor_scalar(flat[1], flat[0], float(1 / (2 * np.pi)), ROUND, ALU.mult, ALU.add))
                link(V_.tensor_scalar(flat[1], flat[1], ROUND, None, ALU.subtract))
                link(V_.scalar_tensor_tensor(flat[0], flat[1], -C1, flat[0], ALU.mult, ALU.add))
                link(V_.scalar_tensor_tensor(flat[0], flat[1], -C2, flat[0], ALU.mult, ALU.add))
                link(V_.tensor_scalar(flat[0], flat[0], 3.1415925, -3.1415925, ALU.min, ALU.max))
                V_.tensor_scalar(sin_b, pw_ang[:, 1, 1], 0.5, None, ALU.mult).then_inc(s5_v, 1)
                dve.wait_ge(s5_a, 1)
                for c in range(2):
                    last = V_.tensor_tensor(pw[:, c], pw_mag, pw_ang[:, c], ALU.mult)
                link(last)
                for k in range(SUB):
                    V_.tensor_copy(pw_back[:, :, SUB - 1 - k, :], pw[:, :, k, :])
                link(V_.tensor_copy(a8, pw[:, :, 8, :]))
                th, ex1, s2, re, im, den, t1, t2 = sc[:8]
                link(V_.tensor_scalar(t1, th, -1.0, 1.0, ALU.mult, ALU.add))
                link(V_.reciprocal(t1, t1))
                link(V_.scalar_tensor_tensor(ex1, th, 2.0, t1, ALU.mult, ALU.mult))
                link(V_.tensor_tensor(s2, sin_b, sin_b, ALU.mult))
                link(V_.tensor_tensor(s2, s2, pw_mag[:, 1], ALU.mult))
                link(V_.scalar_tensor_tensor(re, s2, -2.0, ex1, ALU.mult, ALU.add))
                link(V_.tensor_copy(im, pw[:, 1, 1]))
                link(V_.tensor_tensor(t1, lam[:, 0], lam[:, 0], ALU.mult))
                link(V_.tensor_tensor(t2, lam[:, 1], lam[:, 1], ALU.mult))
                link(V_.tensor_tensor(den, t1, t2, ALU.add))
                link(V_.reciprocal(den, den))
                fr, fi, t3, t4 = sc[8:12]
                link(V_.tensor_tensor(t1, re, lam[:, 0], ALU.mult))
                link(V_.tensor_tensor(t2, im, lam[:, 1], ALU.mult))
                link(V_.tensor_tensor(t1, t1, t2, ALU.add))
                link(V_.tensor_tensor(fr, t1, den, ALU.mult))
                link(V_.tensor_tensor(t3, im, lam[:, 0], ALU.mult))
                link(V_.tensor_tensor(t4, re, lam[:, 1], ALU.mult))
                link(V_.tensor_tensor(t3, t3, t4, ALU.subtract))
                link(V_.tensor_tensor(fi, t3, den, ALU.mult))


                def wide(v):
                    return v[:, :, None].broadcast_to((P, PAIRS, GC))
                link(table_product(V_, link, Bb[:, 0], wide(fr), wide(fi), B_raw[:, 0], B_raw[:, 1], tb, True))
                table_product(V_, link, Bb[:, 1], wide(fr), wide(fi), B_raw[:, 1], B_raw[:, 0], tb, False).then_inc(bb_ready, 1)
                dve.wait_ge(bb_ready, 1)

            def s5_kernel_blocks(j):
                for i in range(2):
                    dve.wait_ge(kd_done, 2 * j + i + 1)
                    if i == 0 and j:
                        dve.wait_ge(kd_stored, 16 * j)
                    kd_piece = KD[:, 4 * i:4 * i + 4]
                    link(V_.tensor_copy(kd_piece, four(banks[4 + i])[0:2 * GC]))
                    p0 = PIECE * j + 4 * i
                    link(V_.tensor_tensor(skip, mat(C_EYE)[0:2 * GC, None, 0:GC].broadcast_to((2 * GC, 4, GC)),
                                          d_col[:, p0:p0 + 4, None].broadcast_to((2 * GC, 4, GC)), ALU.mult))
                    V_.tensor_tensor(kd_piece[:, :, 0:GC], kd_piece[:, :, 0:GC], skip, ALU.add).then_inc(kd_ready, 1)

            for m in range(FC * FF_CHUNKS):
                c = m // FC
                dve.wait_ge(sil_done, m + 1)
                dve.wait_ge(up_done, 2 * m + 2)
                if c >= 2:
                    dve.wait_ge(down_done, c - 1)
                V_.tensor_tensor(hT[:, c % 2, m % FC], hsil[:, m % 2], banks[6 + m % 2][:, 0:SEQ], ALU.mult).then_inc(h_done, 1)
                if m % FC == FC - 1:
                    if c == S5_PARAMS_AT:
                        s5_parameters()
                    if c + 2 in S5_PIECE_AT:
                        p0 = PIECE * S5_PIECE_AT.index(c + 2)
                        for q in range(2):
                            s5_v_table(V_, link, slice(p0 + 4 * q, p0 + 4 * q + 4), 0, t_v).then_inc(v_ready, 1)
                            dve.wait_ge(v_ready, (p0 // PIECE) * 2 + q + 1)
                    if c in S5_PIECE_AT:
                        s5_kernel_blocks(S5_PIECE_AT.index(c))
            layer_norm(from_banks(4), ALPHA, 1)
            take_xT()
            link(V_.tensor_copy(p8[:, :, 0], a8))
            for n in (1, 2, 4):
                by = slice(n - 1, n)
                re, im, t0, t1 = p8[:, 0, 0:n], p8[:, 1, 0:n], carry[:, 0:n, 0], ebuf[:, 0:n, 0]
                bre, bim = (p8[:, i, by].broadcast_to((P, n, PAIRS)) for i in range(2))
                link(V_.tensor_tensor(t0, im, bim, ALU.mult))
                link(V_.tensor_tensor(t1, re, bre, ALU.mult))
                link(V_.tensor_tensor(p8[:, 0, n:2 * n], t1, t0, ALU.subtract))
                link(V_.tensor_tensor(t0, im, bre, ALU.mult))
                link(V_.tensor_tensor(t1, re, bim, ALU.mult))
                link(V_.tensor_tensor(p8[:, 1, n:2 * n], t1, t0, ALU.add))
            for i in range(4):
                dve.wait_ge(y_done, 8 + i + 1)
                V_.tensor_copy(u_tok[:, i // 2, 512 * (i % 2):512 * (i % 2) + 512], banks[i][:, :]).then_inc(u_sb, 1)
            dve.wait_ge(un_loaded, 32)
            V_.tensor_copy(u_r.rearrange("p a (s c) -> p a s c", c=GC), u_n.rearrange("p s (a c) -> p a s c", c=GC)).then_inc(ur_ready, 1)
            for j in range(4):
                dve.wait_ge(u_tr, j + 1)
                V_.tensor_copy(U[:, 8 * j:8 * j + 8].rearrange("p a b c -> p (a b c)"), banks[4 + j][:, :]).then_inc(u_ready, 1)
            for j in range(NPIECE):
                for ri in range(2):
                    dve.wait_ge(e_done, 2 * j + ri + 1)
                    src = banks[(2 * j + ri) % 4][:, :].rearrange("p (a b c) -> p a b c", a=8, b=2)
                    for gh in range(2):
                        half = slice(64 * gh, 64 * gh + 64)
                        last = V_.tensor_copy(E[half, ri, 8 * j:8 * j + 8], src[half, :, gh])
                    last.then_inc(e_read, 1)
            dve.wait_ge(e_read, 8)
            Hb = H.rearrange("p (b i) r a -> p b i r a", i=8)
            Eb = E.rearrange("p r a (b i) -> p b r a i", i=8)

            def advance(dst, h, power_re, power_im, e, t0, t1):
                V_.tensor_tensor(t0, h, power_re, ALU.mult)
                link(V_.tensor_tensor(t1, h, power_im, ALU.mult))
                link(V_.tensor_tensor(t0, t0, e, ALU.add))
                V_.tensor_tensor(dst[:, :, 0], t0[:, :, 0], t1[:, :, 1], ALU.subtract)
                link(V_.tensor_tensor(dst[:, :, 1], t0[:, :, 1], t1[:, :, 0], ALU.add))

            def power(i, n):
                return (p8[:, c, None, i:i + 1].broadcast_to((P, n, 2, PAIRS)) for c in range(2))

            link(V_.memset(Hb[:, :, 0], 0.0))
            link(V_.memset(carry[:, 0:1], 0.0))
            p_re, p_im = power(0, 4)
            for i in range(7):
                advance(Hb[:, :, i + 1], Hb[:, :, i], p_re, p_im, Eb[:, :, :, :, i], ht[0], ht[1])
            ends = ebuf
            advance(ends, Hb[:, :, 7], p_re, p_im, Eb[:, :, :, :, 7], ht[0], ht[1])
            p_re, p_im = power(7, 1)
            for b in range(3):
                advance(carry[:, b + 1:b + 2], carry[:, b:b + 1], p_re, p_im, ends[:, b:b + 1], ht[0][:, 0:1], ht[1][:, 0:1])
            for ri in range(2):
                def pk(c):
                    return p8[:, c, None, 0:7].broadcast_to((P, 3, 7, PAIRS))

                def cb(c):
                    return carry[:, 1:4, c, None, :].broadcast_to((P, 3, 7, PAIRS))
                dst = Hb[:, 1:4, 1:8, ri]
                V_.tensor_tensor(hc[0], pk(0), cb(ri), ALU.mult)
                link(V_.tensor_tensor(hc[1], pk(1), cb(1 - ri), ALU.mult))
                link(V_.tensor_tensor(hc[0], hc[0], hc[1], ALU.subtract if ri == 0 else ALU.add))
                link(V_.tensor_tensor(dst, dst, hc[0], ALU.add))
            link(V_.tensor_copy(Hb[:, 1:4, 0], carry[:, 1:4]))
            dve.wait_ge(hbd_zero, 1)
            for ri in range(2):
                for gh in range(2):
                    half = slice(64 * gh, 64 * gh + 64)
                    V_.tensor_copy(Hbd[half, ri, :, gh], H[half, :, ri].rearrange("p n a -> p a n")).then_inc(h_bd, 1)
            for j in range(NPIECE):
                if j >= 2:
                    dve.wait_ge(yt_done, 2 * (j - 1))
                for i in range(2):
                    dve.wait_ge(ys_done, 2 * j + i + 1)
                    src = banks[i][0:64, :].rearrange("p (a s c) -> p s a c", a=4, s=SUB)
                    dst = y_sb[:, j % 2].rearrange("p s (a c) -> p s a c", c=GC)[:, :, 4 * i:4 * i + 4, :]
                    V_.tensor_copy(dst, src).then_inc(ys_read, 1)
            gated = [0]

            def gated_products(n, hf):
                dve.wait_ge(sig_done, 2 * hf + n + 1)
                v = gsig[:, n, 512 * hf:512 * hf + 512]
                V_.tensor_tensor(v, banks[2 * hf + n][:, :], v, ALU.mult).then_inc(glu_read, 1)
                gated[0] += 1
                dve.wait_ge(glu_read, gated[0])
                return v

            layer_norm(gated_products, ALPHA, 2)
            take_xT()

            for n in range(NT):
                dve.wait_ge(route_done, n + 1)
                link(V_.tensor_tensor(logits[:, n], banks[n][:, 0:8], router_b, ALU.add))
                link(V_.max(top[:, n], logits[:, n]))
                link(V_.tensor_scalar(gate[:, n], logits[:, n], top[:, n, 0:1], None, ALU.subtract))
                V_.tensor_tensor(etop[:, n, 0:1], top[:, n, 1:2], top[:, n, 0:1], ALU.subtract).then_inc(route_read, 1)
            dve.wait_ge(route_a, 1)
            for n in range(NT):
                lg = logits[:, n]
                mine = lg[:, :, None].broadcast_to((P, 8, 8))
                other = lg[:, None, :].broadcast_to((P, 8, 8))
                ca, cb = (t.rearrange("p (a b) -> p a b", a=8) for t in (cmp_a, cmp_b))
                link(V_.tensor_tensor(ca, other, mine, ALU.is_equal))
                link(V_.tensor_tensor(ca, ca, mat(C_EYE)[:, 32:96].rearrange("p (a b) -> p a b", a=8), ALU.mult))
                link(V_.tensor_tensor(cb, other, mine, ALU.is_gt))
                link(V_.tensor_tensor(ca, ca, cb, ALU.add))
                link(V_.tensor_reduce(rank, ca, AX, ALU.add))
                link(V_.tensor_scalar(rank, rank, 2.0, None, ALU.is_lt))
                link(V_.tensor_scalar(etop[:, n, 1:2], etop[:, n, 1:2], 1.0, None, ALU.add))
                link(V_.reciprocal(etop[:, n, 1:2], etop[:, n, 1:2]))
                link(V_.tensor_copy(chosen[:, n], rank))
                link(V_.tensor_tensor(gate[:, n], gate[:, n], rank, ALU.mult))
                link(V_.tensor_scalar(gate[:, n], gate[:, n], etop[:, n, 1:2], None, ALU.mult))
            link(V_.memset(place, -1.0))
            link(V_.memset(gates, 0.0))
            for t in range(2):
                last = V_.tensor_copy(gates[:, :, EXPERTS * t:EXPERTS * t + EXPERTS], gate)
            last.then_inc(chosen_ready, 1)
            dve.wait_ge(place_done, 1)
            for n in range(NT):
                link(V_.tensor_tensor(place[:, n, 0:EXPERTS], banks[n][:, 0:EXPERTS], chosen[:, n], ALU.mult))
            link(V_.tensor_scalar(place[:, :, EXPERTS:2 * EXPERTS], place[:, :, 0:EXPERTS], -1.0 - P, None, ALU.add))
            link(V_.tensor_scalar(place[:, :, 0:EXPERTS], place[:, :, 0:EXPERTS], -1.0, None, ALU.add))
            link(V_.tensor_reduce(passes_f, banks[2][:, 0:EXPERTS], AX, ALU.max))
            link(V_.tensor_scalar(passes_f, passes_f, float(P), 1.0, ALU.is_gt, ALU.add))
            V_.tensor_copy(passes[:, :], passes_f).then_inc(passes_ready, 1)

            def picks(dst, k, scaled, signal):
                for n in range(NT):
                    at = place[:, n, bass.ds(k, 1)]
                    if scaled:
                        last = V_.tensor_scalar(dst[:, n], mat(C_IOTA), at, gates[:, n, bass.ds(k, 1)], ALU.is_equal, ALU.mult)
                    else:
                        last = V_.tensor_scalar(dst[:, n], mat(C_IOTA), at, None, ALU.is_equal)
                last.then_inc(signal, 1)

            def take_tokens(k):
                for i in range(2):
                    dve.wait_ge(gath_done, k * 2 + i + 1)
                    V_.tensor_copy(xg[:, 4 * i:4 * i + 4], four(banks[6 + i])).then_inc(xg_ready, 1)

            dve.wait_ge(passes_ready, 1)
            link(V_.memset(macc, 0.0))
            picks(pick, 0, False, pick_ready)
            picks(pick_g, 0, True, pickg_ready)
            take_tokens(0)
            n_pass = dve.value_load(passes[0:1, 0:1], min_val=1, max_val=2)
            with dve.Fori(0, n_pass * EXPERTS) as k:
                dve.wait_ge(gath_done, k * 2 + 2)
                picks(pick, k + 1, False, pick_ready)
                for c in range(EC):
                    dve.wait_ge(m_sil, k * EC + c + 1)
                    dve.wait_ge(m_up, k * 2 * EC + 2 * EC + 2 * c + 2)
                    if c == 0:
                        dve.wait_ge(m_tr, k * 4 + 4)
                    V_.tensor_tensor(mh[:, EW1 * c:EW1 * c + EW1], msil[:, c % 2], banks[2 + c % 2][:, 0:EW1], ALU.mult).then_inc(m_h, 1)
                dve.wait_ge(m_tr, k * 4 + 5)
                picks(pick_g, k + 1, True, pickg_ready)
                take_tokens(k + 1)
                for n in range(NT):
                    for hf in range(2):
                        dve.wait_ge(m_sc, k * 4 + 2 * n + hf + 1)
                        a = macc[:, n, 512 * hf:512 * hf + 512]
                        V_.tensor_tensor(a, banks[(2 if n == 0 else 6) + hf][:, :], a, ALU.add).then_inc(m_acc, 1)
            V_.memset(scratch1, 0.0).then_inc(turns_done, 1)
            dve.wait_ge(turns_done, 1)
            layer_norm(lambda n, hf: macc[:, n, 512 * hf:512 * hf + 512], ALPHA, 3)

            def rms_norm(n, dst, weight, loaded, count):
                scalar_step()
                link(V_.reciprocal(rstd[:, n:n + 1], rstd[:, n:n + 1]))
                dve.wait_ge(loaded, count)
                V_.scalar_tensor_tensor(dst[:, n], xres[:, n], rstd[:, n:n + 1], weight, ALU.mult, ALU.mult).then_inc(norm_done, 1)

            def add_products(n, done, count):
                for hf in range(2):
                    dve.wait_ge(done, count(hf))
                    v = xres[:, n, 512 * hf:512 * hf + 512]
                    last = V_.tensor_tensor(v, banks[2 * n + hf][:, :], v, ALU.add)
                last.then_inc(norm_v, 1)

            for n in range(NT):
                rms_norm(n, h2n, mix_g, small_loaded, 80)
            take_xT()
            for n in range(NT):
                dve.wait_ge(p_done, n + 1)
                V_.tensor_copy(u2[:, n], banks[n][:, :]).then_inc(p_read_v, 1)
            for m in range(4):
                dve.wait_ge(p_done, 6 + m + 1)
                V_.tensor_copy(k2[:, m], banks[m][:, 0:SEQ]).then_inc(p_read_v, 1)
            for n in range(NT):
                dve.wait_ge(p_done, 10 + n + 1)
                V_.tensor_copy(v2[:, n], banks[4 + n][:, :]).then_inc(p_read_v, 1)
            for gi in range(4):
                dve.wait_ge(pool_done, gi + 1)
                V_.tensor_copy(poolT[:, gi], banks[6 + gi % 2][:, 0:SEQ]).then_inc(pool_read, 1)
            for gi in range(4):
                dve.wait_ge(mix_done, gi + 1)
                V_.tensor_scalar(catT[:, gi], banks[6 + gi % 2][:, 0:SEQ], vecT[:, 97 + gi:98 + gi], None, ALU.mult).then_inc(mix_read, 1)
            def maxima(i):
                dve.wait_ge(sc_done, i + 1)
                for e in range(2):
                    last = V_.tensor_reduce(nmax[:, i % 2, e:e + 1], banks[2 * (i % 2) + e][:, 0:SEQ], AX, ALU.max)
                link(last)
                V_.tensor_scalar(nmax[:, i % 2], nmax[:, i % 2], -1.0, None, ALU.mult).then_inc(max_ready, 1)

            def head_outputs(hp):
                dve.wait_ge(pv_done, hp + 1)
                V_.tensor_copy(catT[:, 4 + hp], banks[6][:, 0:SEQ]).then_inc(pv_read, 1)

            maxima(0)
            for i in range(8):
                hp, n = i // 2, i % 2
                if i < 7:
                    maxima(i + 1)
                dve.wait_ge(exp_done, 2 * i + 2)
                total, p = psum_p[:, n], prob[hp % 2][:, n]
                link(V_.reciprocal(total, total))
                V_.tensor_tensor(p, p, total[:, :, None].broadcast_to((P, 2, SEQ)), ALU.mult).then_inc(pn_ready, 1)
                if n == 0 and hp:
                    head_outputs(hp - 1)
                if n == 1:
                    for kt in range(2):
                        dve.wait_ge(pt_done, 2 * hp + kt + 1)
                        V_.tensor_copy(probT[:, kt].rearrange("p a b -> p (a b)"), banks[4 + kt][:, :]).then_inc(pt_read, 1)
            head_outputs(3)
            for n in range(NT):
                add_products(n, y2_done, lambda hf: 2 * n + hf + 1)
                rms_norm(n, h2n, norm_w[:, 1], normw_loaded, 160)
            take_xT()
            for i in range(32):
                dve.wait_ge(relu_done, i + 1)
                if i >= 8:
                    dve.wait_ge(down2_done, i // 4 - 1)
                t = mT[:, (i // 4) % 2, i % 4]
                V_.tensor_tensor(t, t, t, ALU.mult).then_inc(sqr_done, 1)
            for n in range(NT):
                add_products(n, y2_done, lambda hf: 5 + n)
                rms_norm(n, xres, norm_w[:, 0], normw_loaded, 160)

        @block.scalar
        def _(act):
            A_ = nc.scalar.activation
            count = [0]

            def link(ins):
                count[0] += 1
                ins.then_inc(chain_a, 1)
                act.wait_ge(chain_a, count[0])

            seen_xt = [0]

            def take_xT():
                for j in (1, 3):
                    act.wait_ge(xt_tr, 4 * seen_xt[0] + j + 1)
                    nc.scalar.copy(xT[:, 4:8, P * (j // 2):P * (j // 2) + P], four(banks[4 + j])).then_inc(xt_a, 1)
                seen_xt[0] += 1

            act.wait_ge(ready, 1)
            take_xT()
            act.wait_ge(ba_v, 1)
            link(A_(tmp_b, tmp_a, ACT.Abs, bias=zero_c))
            link(A_(tmp_b, tmp_b, ACT.Exp, bias=zero_c, scale=-1.0))
            A_(a_log, a_log, ACT.Exp, bias=zero_c).then_inc(ba_a, 1)
            A_(tmp_b, tmp_b, ACT.Ln, bias=one_c).then_inc(ba_a, 1)
            link(A_(beta, ba[:, :, 0:8], ACT.Sigmoid, bias=zero_c))

            def decays():
                for j in range(4):
                    act.wait_ge(dec_v, j + 1)
                    for t, s in ((decL, -1.0), (decT, 1.0)):
                        v = t[:, 4 * j:4 * j + 4].rearrange("p a b -> p (a b)")
                        A_(v, v, ACT.Exp, bias=zero_c, scale=s).then_inc(dec_a, 1)
                for j in range(2):
                    A_(e_row[:, 4 * j:4 * j + 4].rearrange("p a b -> p (a b)"), banks[6 + j][:, :], ACT.Exp, bias=zero_c).then_inc(dec_a, 1)
                A_(neg_eg, gc[:, 1], ACT.Exp, bias=zero_c).then_inc(dec_a, 1)
                act.wait_ge(gc_ready, 1)
                A_(kdf, tmp_a[:, 0], ACT.Exp, bias=zero_c).then_inc(dec_a, 1)

            for b in range(8):
                for m in range(4 * b, 4 * b + 4):
                    act.wait_ge(in_tile, m + 1)
                    if b < 6:
                        nc.scalar.copy(pre[:, m, CONV - 1:], banks[m % 3][:, 0:SEQ]).then_inc(pre_ready, 1)
                    else:
                        A_(zT[:, m - QKV_T], banks[m % 3][:, 0:SEQ], ACT.Silu, bias=zero_c).then_inc(pre_ready, 1)
                if 1 <= b <= 6:
                    act.wait_ge(conv_done, b)
                    t = qkvT[:, 4 * (b - 1):4 * b].rearrange("p a b -> p (a b)")
                    A_(t, t, ACT.Silu, bias=zero_c).then_inc(silu_done, 1)
                if b == 2:
                    decays()
                if b >= 4:
                    for i in (2 * b - 8, 2 * b - 7):
                        act.wait_ge(ss_ready, i + 1)
                        if i >= 2:
                            act.wait_ge(unit_ready, i - 1)
                        A_(rs[:, i % 2, :], banks[4 + i % 4][:, :], ACT.Sqrt, bias=eps_rms).then_inc(nrm_ready, 1)
            for n in range(NT):
                act.wait_ge(rec_ev, 6 * (n + 1))
                for b in range(HEADS * n, HEADS * n + HEADS):
                    last = A_(decL[:, b], o[:, b], ACT.Square, bias=zero_c, accum_out=o_ss[:, b:b + 1])
                link(last)
                ss = o_ss[:, HEADS * n:HEADS * n + HEADS]
                A_(ss, ss, ACT.Sqrt, bias=eps_rms, scale=1.0 / DK).then_inc(o_std, 1)

            steps = [0]

            def vector_step():
                steps[0] += 1
                act.wait_ge(norm_v, steps[0])

            def layer_norm(n):
                vector_step()
                A_(rstd[:, n:n + 1], mv[:, n, 1:2], ACT.Sqrt, bias=eps_ln).then_inc(norm_a, 1)
                vector_step()
                A_(xres[:, n], xres[:, n], ACT.Identity, bias=shift[:, n:n + 1], scale=rstd[:, n:n + 1]).then_inc(norm_a, 1)

            layer_norm(0)
            layer_norm(1)
            take_xT()

            for m in range(FC * FF_CHUNKS):
                c = m // FC
                act.wait_ge(up_done, 2 * m + 1)
                if m >= 2:
                    act.wait_ge(h_done, m - 1)
                A_(hsil[:, m % 2], banks[4 + m % 2][:, 0:SEQ], ACT.Silu, bias=zero_c).then_inc(sil_done, 1)
                if m % FC < FC - 1:
                    continue
                if c == S5_PARAMS_AT:
                    act.wait_ge(s5_loaded, 16 * 14)
                    A_(dts, dts, ACT.Exp, bias=zero_c).then_inc(s5_in, 1)
                    act.wait_ge(s5_v, 1)
                    A_(pw_mag, pw_mag, ACT.Exp, bias=zero_c)
                    A_(sc[0], z[:, 0], ACT.Tanh, bias=zero_c, scale=0.5)
                    A_(pw_ang, pw_ang, ACT.Sin, bias=zero_c)
                    A_(sin_b, sin_b, ACT.Sin, bias=zero_c).then_inc(s5_a, 1)
                if c in S5_PIECE_AT:
                    j = S5_PIECE_AT.index(c)
                    if j == 0:
                        act.wait_ge(kz_stored, 64)
                        act.wait_ge(bb_ready, 1)
                    for i in range(4):
                        act.wait_ge(w_tr, 4 * j + i + 1)
                        ri, h4 = i // 2, i % 2
                        nc.scalar.copy(W1T[:, ri, PIECE * j + 4 * h4:PIECE * j + 4 * h4 + 4], four(banks[4 + i])).then_inc(w_in, 1)
                    act.wait_ge(kd_ready, 2 * (j + 1))
                    act.dma_start(k_dram[:, PIECE * j:PIECE * (j + 1), P:2 * P], KD).then_inc(kd_stored, 16)
            layer_norm(0)
            layer_norm(1)
            take_xT()
            for j in range(NPIECE):
                for q in range(2):
                    act.wait_ge(yt_done, 2 * j + q + 1)
                    src = banks[4 + (2 * j + q) % 4][:, 0:256].rearrange("p (s g n) -> p g n s", s=4, g=2)
                    for gh in range(2):
                        dst = hidT[:, j + 4 * gh].rearrange("p (n s) -> p n s", s=SUB)[:, :, 4 * q:4 * q + 4]
                        A_(dst, src[:, gh], ACT.Gelu, bias=zero_c).then_inc(hid_ready, 1)
            for hf in range(2):
                for n in range(NT):
                    i = 2 * hf + n
                    if i == 3:
                        layer_norm(0)
                    act.wait_ge(glu_done, 4 * hf + 2 * n + 2)
                    A_(gsig[:, n, 512 * hf:512 * hf + 512], banks[4 + i][:, :], ACT.Sigmoid, bias=zero_c).then_inc(sig_done, 1)
            layer_norm(1)
            take_xT()
            act.wait_ge(route_read, 2)
            A_(gate, gate, ACT.Exp, bias=zero_c)
            A_(etop[:, :, 1], etop[:, :, 0], ACT.Exp, bias=zero_c).then_inc(route_a, 1)
            act.wait_ge(passes_ready, 1)
            n_pass = act.value_load(passes[0:1, 0:1], min_val=1, max_val=2)
            with act.Fori(0, n_pass * EXPERTS) as k:
                def silu_of(c):
                    act.wait_ge(m_up, k * 2 * EC + 2 * EC + 2 * c + 1)
                    if c >= 2:
                        act.wait_ge(m_h, k * EC + c - 1)
                    elif c == 0:
                        act.wait_ge(pickg_ready, k + 1)
                    A_(msil[:, c % 2], banks[c % 2][:, 0:EW1], ACT.Silu, bias=zero_c).then_inc(m_sil, 1)

                def take_hT(t):
                    act.wait_ge(m_tr, k * 4 + t + 5)
                    if t == 0:
                        nc.scalar.copy(spread.rearrange("p a b -> p (a b)"), banks[4][:, 2 * P:4 * P])
                        nc.scalar.copy(mhT[:, 0:2].rearrange("p a b -> p (a b)"), banks[4][:, 0:2 * P]).then_inc(m_hT, 1)
                    else:
                        m = 3 * t - 1
                        nc.scalar.copy(mhT[:, m:m + 3].rearrange("p a b -> p (a b)"), banks[4 + t % 2][:, 0:3 * P]).then_inc(m_hT, 1)

                silu_of(0)
                silu_of(1)
                take_hT(0)
                silu_of(2)
                take_hT(1)
                silu_of(3)
                take_hT(2)
                take_hT(3)
                for hf in range(2):
                    act.wait_ge(m_y, k * EC + EC + 2 * hf + 2)
                    nc.scalar.copy(ysb[:, 512 * hf:512 * hf + 512], banks[hf][:, :]).then_inc(m_yread, 1)
            layer_norm(0)
            layer_norm(1)

            def mean_square(n):
                link(A_(region(39936 + 1024 * n, 1024), xres[:, n], ACT.Square, bias=zero_c, accum_out=mv[:, n, 1:2]))
                A_(rstd[:, n:n + 1], mv[:, n, 1:2], ACT.Sqrt, bias=eps_rms, scale=1.0 / DM).then_inc(norm_a, 1)

            for n in range(NT):
                act.wait_ge(norm_done, 7 + n)
                mean_square(n)
            take_xT()
            for m in range(4):
                act.wait_ge(p_done, 2 + m + 1)
                A_(q2[:, m], banks[4 + m][:, 0:SEQ], ACT.Copy, scale=AD ** -0.5).then_inc(p_read_a, 1)
            for hp in range(4):
                for n in range(NT):
                    i = 2 * hp + n
                    act.wait_ge(max_ready, i + 1)
                    if hp >= 2:
                        act.wait_ge(pt_done, 2 * (hp - 1))
                    for e in range(2):
                        A_(prob[hp % 2][:, n, e], banks[2 * n + e][:, 0:SEQ], ACT.Exp, bias=nmax[:, n, e:e + 1],
                           accum_out=psum_p[:, n, e:e + 1]).then_inc(exp_done, 1)
            for n in range(NT):
                vector_step()
                mean_square(n)
            take_xT()
            for i in range(32):
                act.wait_ge(up2_done, i + 1)
                if i >= 8:
                    act.wait_ge(down2_done, i // 4 - 1)
                A_(mT[:, (i // 4) % 2, i % 4], banks[4 + i % 4][:, 0:SEQ], ACT.Relu, bias=zero_c).then_inc(relu_done, 1)
            for n in range(NT):
                vector_step()
                mean_square(n)

        @block.tensor
        def _(pe):
            mm = nc.tensor.matmul

            def transpose(dst, src):
                k = src.shape[0]
                if dst.shape[0] < P:
                    return mm(dst, src, const[0:k, C_ID, 0:k], start=True, stop=True)
                return nc.tensor.transpose(dst, src, const[0:k, C_ID, 0:k])

            made_xt = [0]

            def make_xT(src, normed=None):
                for j in range(4):
                    if normed is not None and j % 2 == 0:
                        pe.wait_ge(norm_done, normed + j // 2 + 1)
                    for i in range(4):
                        c = 4 * (j % 2) + i
                        last = transpose(four(banks[4 + j])[:, i], src[:, j // 2, P * c:P * c + P])
                    last.then_inc(xt_tr, 1)
                made_xt[0] += 1

            def need_xT():
                pe.wait_ge(xt_v, 2 * made_xt[0])
                pe.wait_ge(xt_a, 2 * made_xt[0])

            def t_form(bank, w, m, x=xT):
                for k in range(KT):
                    last = mm(bank[:, 0:SEQ], w[:, k, P * m:P * m + P], x[:, k, :], start=(k == 0), stop=(k == KT - 1))
                return last

            def token_major(bank, x, w, n, k0=0, total=KT):
                nk = w.shape[1]
                for k in range(nk):
                    last = mm(bank, x[:, k0 + k, P * n:P * n + P], w[:, k], start=(k0 + k == 0), stop=(k0 + k == total - 1))
                return last

            pe.wait_ge(const_loaded, 16)
            pe.wait_ge(vecs_loaded, 48)
            transpose(banks[3][:, 0:101], vrows).then_inc(vec_tr, 1)
            pe.wait_ge(x_loaded, 16)
            make_xT(xres)
            need_xT()
            w_ba = region(38984, KT, 16)
            pe.wait_ge(ba_w_loaded, 16)
            for n in range(NT):
                last = token_major(banks[6 + n][:, 0:16], xT, w_ba, n)
            last.then_inc(ba_done, 1)

            def cumulated_g():
                pe.wait_ge(g_ready, 1)
                pe.wait_ge(vec_ok, 1)
                mm(banks[3][:, 0:16], mat(C_TRI), g.rearrange("p a b -> p (a b)"), start=True, stop=True).then_inc(grow_done, 1)
                for j in range(4):
                    for b in range(4 * j, 4 * j + 4):
                        gcol = g.rearrange("p a b -> p (a b)")[:, b:b + 1]
                        last = mm(four(banks[4 + j])[:, b % 4], gcol.broadcast_to((P, P)), mat(C_TRI), start=True, stop=True)
                    last.then_inc(grow_done, 1)

            def square_sums(b):
                if b == 0:
                    pe.wait_ge(dec_v, 4)
                    pe.wait_ge(dec_a, 10)
                for i in (2 * b, 2 * b + 1):
                    pe.wait_ge(sq_ready, i + 1)
                    if i >= 4:
                        pe.wait_ge(nrm_ready, i - 3)
                    mm(banks[4 + i % 4][:, :], mat(C_ONE), sq[:, i % 2, :], start=True, stop=True).then_inc(ss_ready, 1)

            for m in range(32):
                b = m // 4
                if m % 4 == 0:
                    arrived(pe, ("gdn_in", b))
                if m == 8:
                    cumulated_g()
                if m % 4 == 0 and b >= 4:
                    square_sums(b - 4)
                if m >= 3:
                    pe.wait_ge(pre_ready, m - 2)
                t_form(banks[m % 3], region(4096 * (b % 4), KT, 512), m % 4).then_inc(in_tile, 1)
            pe.wait_ge(pre_ready, 32)
            pe.wait_ge(dec_v, 1)
            for j in range(4):
                pe.wait_ge(unit_ready, 6 if j == 0 else 8)
                if j >= 2:
                    pe.wait_ge(kq_read, j - 1)
                for b in range(4 * j, 4 * j + 4):
                    n, h = b // 8, b % 8
                    kt, qt = (qkvT[:, t + h, P * n:P * n + P] for t in (8, 0))
                    mm(four(banks[j % 2])[:, b % 4], kt, kt, start=True, stop=True)
                    last = mm(four(banks[2 + j % 2])[:, b % 4], kt, qt, start=True, stop=True)
                last.then_inc(kq_done, 1)
            pe.wait_ge(dec_a, 12)
            for j in range(4):
                pe.wait_ge(kq_read, j + 1)
                for b in range(4 * j, 4 * j + 4):
                    last = transpose(four(banks[4 + j])[:, b % 4], D[:, b])
                last.then_inc(d_tr, 1)

            def level_q(lv, j):
                i = 4 * (lv - 1) + j
                if lv == 1:
                    pe.wait_ge(d_evac, 4)
                else:
                    pe.wait_ge(lv_pe, 8 * (lv - 2) + 2 * (j + 1))
                if i >= 2:
                    pe.wait_ge(lv_qe, i - 1)
                for b in range(4 * j, 4 * j + 4):
                    last = mm(four(banks[j % 2])[:, b % 4], decL[:, b], DT[:, b], start=True, stop=True)
                last.then_inc(lv_q, 1)

            def level_p(lv, j):
                i = 4 * (lv - 1) + j
                pe.wait_ge(lv_qe, i + 1)
                if i >= 2:
                    prev = i - 2
                    pe.wait_ge(lv_pe, 2 * (prev + 1) if prev < 20 else 40 + prev - 19)
                for b in range(4 * j, 4 * j + 4):
                    last = mm(four(banks[2 + j % 2])[:, b % 4], D[:, b], QT[:, b], start=True, stop=True)
                    if lv < LEVELS - 1:
                        last = mm(four(banks[4 + j % 2])[:, b % 4], QT[:, b], D[:, b], start=True, stop=True)
                last.then_inc(lv_p, 1)

            for lv in range(1, LEVELS):
                level_q(lv, 0)
                for j in range(4):
                    if j < 3:
                        level_q(lv, j + 1)
                    level_p(lv, j)
            pe.wait_ge(lv_pe, 44)
            for j in range(4):
                for b in range(4 * j, 4 * j + 4):
                    last = transpose(four(banks[j])[:, b % 4], qkvT[:, 16 + b % 8, P * (b // 8):P * (b // 8) + P])
                last.then_inc(vk_tr, 1)
            for j in range(2):
                for h in range(4 * j, 4 * j + 4):
                    last = transpose(four(banks[4 + j])[:, h % 4], qkvT[:, 8 + h, 0:P])
                last.then_inc(vk_tr, 1)
            def each(j, bank, pairs, sem_=rec):
                for h in range(4 * j, 4 * j + 4):
                    terms = pairs(h)
                    for t, (lhsT, rhs) in enumerate(terms):
                        last = mm(four(bank)[:, h % 4], lhsT, rhs, start=(t == 0), stop=(t == len(terms) - 1))
                last.then_inc(sem_, 1)

            for j in range(2):
                pe.wait_ge(vk_ready, 4 * (j + 1))
                each(j, banks[6 + j], lambda h: [(DT[:, h], vtok[:, h])])
            pe.wait_ge(vk_ready, 24)
            for j in range(2):
                pe.wait_ge(rec_ev, j + 1)
                each(j, banks[j], lambda h: [(kd[:, h], vn[:, 0, h])])
                each(j, banks[2 + j], lambda h: [(decT[:, h], vn[:, 0, h])])
            for j in range(2):
                pe.wait_ge(rec_ev, 3 + 2 * j)
                each(j, banks[4 + j], lambda h: [(qkvT[:, 8 + h, P:2 * P], s1[:, h])])
            for j in range(2):
                pe.wait_ge(rec_ev, 7 + j)
                each(j, banks[6 + j], lambda h: [(DT[:, 8 + h], r1[:, h])])
            for j in range(2):
                pe.wait_ge(rec_ev, 9 + j)
                each(j, banks[j], lambda h: [(e_row[:, h], s1[:, h]), (decT[:, 8 + h], vn[:, 1, h])])
            for j in range(4):
                pe.wait_ge(o_norm, j // 2 + 1)
                for i in range(4):
                    last = transpose(four(banks[4 + j])[:, i], o[:, 4 * j + i])
                last.then_inc(o_tr, 1)
            pe.wait_ge(o_ready, 4)
            pe.wait_ge(rec_ev, 12)
            for n in range(NT):
                for hf in range(2):
                    for c in range(2):
                        arrived(pe, ("gdn_out", c))
                        last = token_major(banks[2 * n + hf][:, :], oT, region(4096 * (2 + c), 4, DM)[:, :, 512 * hf:512 * hf + 512], n, 4 * c)
                    last.then_inc(y_done, 1)
            make_xT(xres, 0)

            def s5_transposes():
                pe.wait_ge(s5_loaded, 16 * 14)
                pe.wait_ge(h_done, FC * (S5_PARAMS_AT + 1))
                for gh, raw in enumerate((lam_raw, lam_raw2)):
                    for i in range(2):
                        transpose(banks[4][64 * gh:64 * gh + 64, PAIRS * i:PAIRS * i + PAIRS], raw[:, i])
                for i in range(2):
                    for jb in range(8):
                        half = slice(64 * (jb // 4), 64 * (jb // 4) + 64)
                        last = transpose(banks[5 + i][half, P * (jb % 4):P * (jb % 4) + P], C_raw[:, i, jb])
                last.then_inc(s5_tr, 1)
                pe.wait_ge(s5_read, 1)

            def s5_piece(j):
                pe.wait_ge(h_done, FC * (S5_PIECE_AT[j] + 1))
                pe.wait_ge(w_ready, 2 * j + 2)
                for i in range(4):
                    ri, h4 = i // 2, i % 2
                    for a in range(4):
                        last = transpose(four(banks[4 + i])[:, a], Wp[:, ri, 4 * h4 + a].rearrange("p s c -> p (s c)"))
                    last.then_inc(w_tr, 1)
                pe.wait_ge(v_ready, 2 * j + 2)
                pe.wait_ge(im_ready, j + 1)
                for i in range(2):
                    pe.wait_ge(w_in, 4 * j + i + 1)
                    for a in range(4):
                        pr = 4 * i + a
                        for ri in range(2):
                            last = mm(four(banks[4 + i])[0:2 * GC, a], Bbd[:, ri, pr], V[:, ri, PIECE * j + pr, 0:SUB].rearrange("p k c -> p (k c)"),
                                      start=(ri == 0), stop=(ri == 1))
                    last.then_inc(kd_done, 1)
                pe.wait_ge(w_in, 4 * j + 4)
                pe.wait_ge(kd_ready, 2 * j + 2)

            def swiglu_down(c):
                arrived(pe, ("ffn_w2", c))
                pe.wait_ge(h_done, FC * (c + 1))
                for n in range(NT):
                    for hf in range(2):
                        for k in range(FC):
                            last = mm(banks[2 * n + hf][:, :], hT[:, c % 2, k, P * n:P * n + P], f2[c % FF_SETS][:, k, 512 * hf:512 * hf + 512],
                                      start=(c == 0 and k == 0), stop=(c == FF_CHUNKS - 1 and k == FC - 1))
                        if c == FF_CHUNKS - 1:
                            last.then_inc(y_done, 1)
                if c < FF_CHUNKS - 1:
                    last.then_inc(down_done, 1)

            need_xT()
            for c in range(FF_CHUNKS):
                arrived(pe, ("ffn_w3", c))
                for m in range(FC * c, FC * c + FC):
                    if m >= 2:
                        pe.wait_ge(sil_done, m - 1)
                    t_form(banks[4 + m % 2], f1[c % FF_SETS], m % FC).then_inc(up_done, 1)
                    if m >= 2:
                        pe.wait_ge(h_done, m - 1)
                    t_form(banks[6 + m % 2], f3[c % FF_SETS], m % FC).then_inc(up_done, 1)
                if c:
                    swiglu_down(c - 1)
                if c == S5_PARAMS_AT:
                    s5_transposes()
                if c in S5_PIECE_AT:
                    s5_piece(S5_PIECE_AT.index(c))
            swiglu_down(FF_CHUNKS - 1)
            make_xT(xres, 2)
            need_xT()
            for n in range(NT):
                for hf in range(2):
                    for c in range(2):
                        arrived(pe, ("s5_in", c))
                        last = token_major(banks[2 * n + hf][:, :], xT, region(4096 * c, 4, DM)[:, :, 512 * hf:512 * hf + 512], n, 4 * c)
                    last.then_inc(y_done, 1)
            pe.wait_ge(ur_ready, 1)
            pe.wait_ge(w_in, 16)
            for j in range(4):
                for a in range(8):
                    last = transpose(banks[4 + j][:, 64 * a:64 * a + 64], u_r[:, 8 * j + a])
                last.then_inc(u_tr, 1)
            pe.wait_ge(u_sb, 4)
            for j in range(NPIECE):
                pe.wait_ge(u_ready, j + 1)
                for ri in range(2):
                    i = 2 * j + ri
                    if i >= 4:
                        pe.wait_ge(e_read, i - 3)
                    for a in range(8):
                        pr = 8 * j + a
                        last = mm(banks[i % 4][:, 64 * a:64 * a + 64], W1T[:, ri, pr], U[:, pr].rearrange("p a b -> p (a b)"), start=True, stop=True)
                    last.then_inc(e_done, 1)
            pe.wait_ge(e_read, 8)
            pe.wait_ge(h_bd, 4)
            pe.wait_ge(t_loaded, 16 * 16)
            pe.wait_ge(u_ready, 4)

            def y_transposes(j):
                for q in range(2):
                    pe.wait_ge(ys_read, 2 * j + 2)
                    if j >= 2:
                        pe.wait_ge(hid_ready, 4 * (j - 2) + 2 * q + 2)
                    for s in range(4):
                        last = transpose(banks[4 + (2 * j + q) % 4][:, 64 * s:64 * s + 64], y_sb[:, j % 2, 4 * q + s])
                    last.then_inc(yt_done, 1)

            for j in range(NPIECE):
                for i in range(2):
                    if j:
                        pe.wait_ge(ys_read, 2 * (j - 1) + i + 1)
                    for a in range(4):
                        pr = PIECE * j + 4 * i + a
                        dst = four(banks[i])
                        for ri in range(2):
                            mm(dst[0:64, a], Hbd[:, ri, pr].rearrange("p a b -> p (a b)"), V[:, ri, pr, 1:SUB + 1].rearrange("p k c -> p (k c)"),
                               start=(ri == 0), stop=False, skip_group_check=True)
                        for gh in range(2):
                            last = mm(dst[32 * gh:32 * gh + 32, a], U[:, pr, gh], T[:, gh, pr], start=False, stop=(gh == 1), skip_group_check=True)
                    last.then_inc(ys_done, 1)
                if j:
                    y_transposes(j - 1)
            y_transposes(NPIECE - 1)
            pe.wait_ge(hid_ready, 16)
            pe.wait_ge(ys_read, 8)
            for hf in range(2):
                for n in range(NT):
                    for c in range(2):
                        arrived(pe, ("glu", 2 * hf + c))
                        token_major(banks[4 * c + 2 * hf + n][:, :], hidT, glu[2 * hf + c], n).then_inc(glu_done, 1)
            for counter, n in ((m_up, 2 * EC), (m_y, EC), (m_tr, 4), (m_yread, 2), (m_acc, 4)):
                pe.sem_inc(counter, n)
            make_xT(xres, 4)
            need_xT()
            pe.wait_ge(small_loaded, 64)
            for n in range(NT):
                token_major(banks[n][:, 0:8], xT, w_router, n).then_inc(route_done, 1)
            pe.wait_ge(route_read, 2)
            pe.wait_ge(chosen_ready, 1)
            mm(banks[0][:, 0:EXPERTS], mat(C_TRI), chosen[:, 0], start=True, stop=True)
            mm(banks[1][:, 0:EXPERTS], mat(C_TRI), chosen[:, 1], start=True, stop=False)
            mm(banks[1][:, 0:EXPERTS], mat(C_ONE), chosen[:, 0], start=False, stop=True)
            mm(banks[2][:, 0:EXPERTS], mat(C_ONE), chosen[:, 0], start=True, stop=False)
            mm(banks[2][:, 0:EXPERTS], mat(C_ONE), chosen[:, 1], start=False, stop=True).then_inc(place_done, 1)
            pe.wait_ge(passes_ready, 1)

            def gather(k):
                pe.wait_ge(pick_ready, k + 1)
                for i in range(2):
                    for c in range(4):
                        for n in range(NT):
                            last = mm(four(banks[6 + i])[:, c], xres[:, n, P * (4 * i + c):P * (4 * i + c) + P], pick[:, n],
                                      start=(n == 0), stop=(n == 1))
                    last.then_inc(gath_done, 1)

            gather(0)
            n_pass = pe.value_load(passes[0:1, 0:1], min_val=1, max_val=2)
            with pe.Fori(0, n_pass * EXPERTS) as k:
                def up(c):
                    pe.wait_ge(m_loaded[c], (k + 1) * 32)
                    if c >= 2:
                        pe.wait_ge(m_sil, k * EC + c - 1)
                    for kt in range(KT):
                        last = mm(banks[c % 2][:, 0:EW1], xg[:, kt], m1[c][:, kt], start=(kt == 0), stop=(kt == KT - 1))
                    last.then_inc(m_up, 1)
                    if c >= 2:
                        pe.wait_ge(m_h, k * EC + c - 1)
                    for kt in range(KT):
                        last = mm(banks[2 + c % 2][:, 0:EW1], xg[:, kt], m3[c][:, kt], start=(kt == 0), stop=(kt == KT - 1))
                    last.then_inc(m_up, 1)

                def hidden(t):
                    pe.wait_ge(m_h, k * EC + t + 1)
                    if t >= 2:
                        pe.wait_ge(m_hT, k * 4 + t - 1)
                    bank = four(banks[4 + t % 2])
                    if t == 0:
                        pe.wait_ge(pickg_ready, k + 1)
                        for n in range(NT):
                            transpose(bank[:, 2 + n], pick_g[:, n])
                        tiles = (0, 1)
                    else:
                        tiles = range(3 * t - 1, 3 * t + 2)
                    for i, m in enumerate(tiles):
                        last = transpose(bank[:, i], mh[:, P * m:P * m + P])
                    last.then_inc(m_tr, 1)

                pe.wait_ge(xg_ready, k * 2 + 2)
                pe.wait_ge(m_yread, k * 2 + 2)
                pe.wait_ge(m_acc, k * 4 + 4)
                up(0)
                up(1)
                hidden(0)
                up(2)
                hidden(1)
                up(3)
                hidden(2)
                gather(k + 1)
                hidden(3)
                pe.wait_ge(m_hT, k * 4 + 4)
                pe.wait_ge(m_sil, k * EC + 4)
                for c in range(EC):
                    pe.wait_ge(m_loaded[EC + c], (k + 1) * 16)
                    dst = banks[c // 2][:, EW2 * (c % 2):EW2 * (c % 2) + EW2]
                    for kt in range(FE_T):
                        last = mm(dst, mhT[:, kt], m2[c][:, kt], start=(kt == 0), stop=(kt == FE_T - 1))
                    last.then_inc(m_y, 1)
                pe.wait_ge(xg_ready, k * 2 + 4)
                for n in range(NT):
                    for hf in range(2):
                        pe.wait_ge(m_yread, k * 2 + hf + 3)
                        last = mm(banks[(2 if n == 0 else 6) + hf][:, :], spread[:, n], ysb[:, 512 * hf:512 * hf + 512], start=True, stop=True)
                        last.then_inc(m_sc, 1)
            make_xT(h2n, 8)
            need_xT()
            arrived(pe, ("in2", 0))
            for n in range(NT):
                token_major(banks[n][:, :], xT, in2[0], n).then_inc(p_done, 1)
            arrived(pe, ("in2", 1))
            for m in range(4):
                t_form(banks[4 + m], in2[1], m).then_inc(p_done, 1)
            arrived(pe, ("in2", 2))
            for m in range(4):
                if m < 2:
                    pe.wait_ge(p_read_v, m + 1)
                t_form(banks[m], in2[2], m).then_inc(p_done, 1)
            arrived(pe, ("in2", 3))
            for n in range(NT):
                pe.wait_ge(p_read_a, n + 1)
                token_major(banks[4 + n][:, :], xT, in2[3], n).then_inc(p_done, 1)
            pe.wait_ge(b2_loaded, 16 * 19)
            pe.wait_ge(p_read_a, 4)
            for gi in range(4):
                if gi >= 2:
                    pe.wait_ge(pool_read, gi - 1)
                for n in range(NT):
                    last = mm(banks[6 + gi % 2][:, 0:SEQ], u2[:, n, P * gi:P * gi + P], poolw[:, n, gi], start=(n == 0), stop=(n == 1))
                last.then_inc(pool_done, 1)
            for gi in range(4):
                pe.wait_ge(pool_read, 3 + gi % 2 if gi < 2 else 4)
                if gi >= 2:
                    pe.wait_ge(mix_read, gi - 1)
                mm(banks[6 + gi % 2][:, 0:SEQ], wpool[:, gi], poolT[:, gi], start=True, stop=True).then_inc(mix_done, 1)
            pe.wait_ge(bias_ready, 2)
            pe.wait_ge(p_read_v, 8)
            pe.wait_ge(mix_read, 4)

            def scores(hp):
                for n in range(NT):
                    i = 2 * hp + n
                    if i >= 2:
                        pe.wait_ge(exp_done, 2 * (i - 1))
                    for e in range(2):
                        pp = slice(64 * e, 64 * e + 64)
                        mm(banks[2 * n + e][:, 0:SEQ], q2[pp, hp, P * n:P * n + P], k2[pp, hp, :], start=True, stop=False)
                    for e in range(2):
                        last = mm(banks[2 * n + e][:, 0:SEQ], mat(C_REV), bias[:, n, 2 * hp + e], start=False, stop=True)
                    last.then_inc(sc_done, 1)

            scores(0)
            for hp in range(4):
                if hp < 3:
                    scores(hp + 1)
                pe.wait_ge(pn_ready, 2 * hp + 2)
                for kt in range(2):
                    if hp:
                        pe.wait_ge(pt_read, 2 * (hp - 1) + kt + 1)
                    for n in range(NT):
                        for e in range(2):
                            last = transpose(banks[4 + kt][:, SEQ * e + P * n:SEQ * e + P * n + P], prob[hp % 2][:, n, e, P * kt:P * kt + P])
                    last.then_inc(pt_done, 1)
                pe.wait_ge(pt_read, 2 * hp + 2)
                if hp:
                    pe.wait_ge(pv_read, hp)
                for e in range(2):
                    for kt in range(2):
                        h = 2 * hp + e
                        last = mm(banks[6][64 * e:64 * e + 64, 0:SEQ], v2[:, kt, AD * h:AD * h + AD], probT[:, kt, e], start=(kt == 0), stop=(kt == 1))
                last.then_inc(pv_done, 1)
            pe.wait_ge(pv_read, 4)
            pe.wait_ge(exp_done, 16)
            for n in range(NT):
                for hf in range(2):
                    for c in range(2):
                        arrived(pe, ("out2", c))
                        last = token_major(banks[2 * n + hf][:, :], catT, out2[c][:, :, 512 * hf:512 * hf + 512], n, 4 * c)
                    last.then_inc(y2_done, 1)
            make_xT(h2n, 10)
            need_xT()
            def mlp_up(s):
                c = s % 2
                arrived(pe, ("up2", s))
                for m in range(4):
                    i = 4 * s + m
                    if i >= 4:
                        pe.wait_ge(relu_done, i - 3)
                    t_form(banks[4 + m], up2[c], m).then_inc(up2_done, 1)

            def mlp_down(s):
                c = s % 2
                arrived(pe, ("down2", s))
                pe.wait_ge(sqr_done, 4 * s + 4)
                for n in range(NT):
                    for hf in range(2):
                        for k in range(4):
                            last = mm(banks[2 * n + hf][:, :], mT[:, s % 2, k, P * n:P * n + P],
                                      down2[c][:, k, 512 * hf:512 * hf + 512],
                                      start=(s == 0 and k == 0), stop=(s == 7 and k == 3))
                    if s == 7:
                        last.then_inc(y2_done, 1)
                if s < 7:
                    last.then_inc(down2_done, 1)

            mlp_up(0)
            for s in range(8):
                if s < 7:
                    mlp_up(s + 1)
                mlp_down(s)


_INS = ["x", "gdn_w_in", "gdn_conv_w", "gdn_a_log", "gdn_dt_bias", "gdn_norm_g", "gdn_w_out",
        "ffn_w1", "ffn_w3", "ffn_w2", "s5_w_in", "s5_lam_re", "s5_lam_im", "s5_log_dt", "s5_b_re",
        "s5_b_im", "s5_c_re", "s5_c_im", "s5_d", "s5_w_glu", "moe_w_router", "moe_b_router",
        "moe_w1", "moe_w3", "moe_w2", "ln_g", "ln_b", "norm_mix_g_2", "w_in_2", "w_pool_2",
        "pool_scale_2", "rpb_2", "w_out_2", "norm_mlp_g_2", "w_up_2", "w_down_2", "final_g_2"]


def kernel(**inputs):
    import concourse.bacc as bacc
    from concourse.bass_utils import run_bass_kernel_spmd

    nc = bacc.Bacc("TRN2", target_bir_lowering=False, num_devices=1)
    arrays = {name: np.ascontiguousarray(inputs[name]) for name in _INS}
    arrays["shape_const"], arrays["shape_pool"], arrays["shape_mask"] = shape_constants()
    aps = {name: nc.dram_tensor(name, a.shape, F32, kind="ExternalInput").ap() for name, a in arrays.items()}
    out = nc.dram_tensor("out", (1, SEQ, DM), F32, kind="ExternalOutput").ap()
    build(nc, aps, out)
    r = run_bass_kernel_spmd(nc, [arrays], core_ids=[0])
    return r.results[0]["out"]
```
